# Optimizing a Trainium2 kernel written in Bass

```python
import math
import jax, jax.numpy as jnp
from jax import lax
import numpy as np

D_MODEL = 1024
BATCH = 1
SEQ = 512
DEPTH = 2

N_EVEN = (DEPTH + 1) // 2
N_ODD = DEPTH // 2
DN_ALPHA = (2 * DEPTH) ** 0.25
DN_BETA = (8 * DEPTH) ** -0.25
LN_EPS = 1e-5

RWKV_WIDTH = D_MODEL // 2
RWKV_HEAD_DIM = 64
RWKV_HEADS = RWKV_WIDTH // RWKV_HEAD_DIM
W_LORA = 64
A_LORA = 64
G_LORA = 128
RWKV_GN_EPS = 64e-5
RWKV_COLS = 3 * RWKV_WIDTH + W_LORA + A_LORA + G_LORA
RWKV_SPLITS = [RWKV_WIDTH, 2 * RWKV_WIDTH, 3 * RWKV_WIDTH, 3 * RWKV_WIDTH + W_LORA, 3 * RWKV_WIDTH + W_LORA + A_LORA]

LRU_WIDTH = D_MODEL // 2
LRU_BLOCKS = 8
LRU_BLOCK = LRU_WIDTH // LRU_BLOCKS
LRU_C = 8.0
LRU_CONV = 4
EVEN_IN = RWKV_COLS + 2 * LRU_WIDTH
EVEN_MIX = RWKV_WIDTH + LRU_WIDTH

CONF_WIDTH = D_MODEL // 2
CONF_CONV = 31

SSM_INNER = D_MODEL
SSM_HEAD_DIM = 64
SSM_HEADS = SSM_INNER // SSM_HEAD_DIM
SSM_GROUPS = 2
SSM_HEADS_PER_GROUP = SSM_HEADS // SSM_GROUPS
SSM_STATE = 128
SSM_CONV = 4
SSM_CHUNK = 128
SSM_XBC = SSM_INNER + 2 * SSM_GROUPS * SSM_STATE
ODD_IN = 2 * CONF_WIDTH + SSM_INNER + SSM_XBC + SSM_HEADS
ODD_MIX = CONF_WIDTH + SSM_INNER

N_MEM = 256
XA_HEADS = 4
XA_HEAD_DIM = D_MODEL // XA_HEADS
D_FF = 4 * D_MODEL

kernel_name = 'hybrid_rwkv7_rglru_conformer_ssd_deepnorm'

def _layer_norm(x, g, b):
    xf = x.astype(jnp.float32)
    mu = xf.mean(-1, keepdims=True)
    var = jnp.square(xf - mu).mean(-1, keepdims=True)
    return ((xf - mu) * lax.rsqrt(var + LN_EPS) * g + b).astype(x.dtype)

def _causal_dwconv(x, w, b):
    k_w, ch = w.shape
    y = lax.conv_general_dilated(x, w[:, None, :].astype(x.dtype), window_strides=(1,),
                                 padding=[(k_w - 1, 0)], dimension_numbers=('NWC', 'WIO', 'NWC'),
                                 feature_group_count=ch)
    return y + b

def _token_shift(p):
    return jnp.pad(p, ((0, 0), (1, 0), (0, 0)))[:, :-1]

def _linear_combine(e1, e2):
    a1, b1 = e1
    a2, b2 = e2
    return a1 * a2, a2 * b1 + b2

def _rwkv7_time_mix(p, mu, w0, w2, a0, a2, g2, k_k, k_a, r_k, gn_g, gn_b):
    f32 = jnp.float32
    bsz, seqlen, _ = p.shape
    p = p.astype(f32)
    p = p + (_token_shift(p) - p) * mu
    r, k, v, wd, ad, gd = jnp.split(p, RWKV_SPLITS, axis=-1)
    w = -jax.nn.softplus(-(w0 + jnp.tanh(wd) @ w2)) - 0.5
    decay = jnp.exp(-jnp.exp(w))
    a = jax.nn.sigmoid(a0 + ad @ a2)
    g = jax.nn.sigmoid(gd) @ g2
    heads = lambda t: t.reshape(bsz, seqlen, RWKV_HEADS, RWKV_HEAD_DIM)
    kk = heads(k * k_k)
    kk = kk / jnp.maximum(jnp.linalg.norm(kk, axis=-1, keepdims=True), 1e-12)
    k = k * (1.0 + (a - 1.0) * k_a)
    r_h, k_h, v_h, w_h, a_h = heads(r), heads(k), heads(v), heads(decay), heads(a)
    seq_in = tuple(jnp.moveaxis(t, 1, 0) for t in (r_h, w_h, k_h, v_h, kk, a_h))

    def step(state, inp):
        r_t, w_t, k_t, v_t, kk_t, a_t = inp
        sa = jnp.einsum('bhvk,bhk->bhv', state, -kk_t)
        state = (state * w_t[:, :, None, :] + sa[..., None] * (kk_t * a_t)[:, :, None, :]
                 + v_t[..., None] * k_t[:, :, None, :])
        return state, jnp.einsum('bhvk,bhk->bhv', state, r_t)

    s0 = jnp.zeros((bsz, RWKV_HEADS, RWKV_HEAD_DIM, RWKV_HEAD_DIM), f32)
    _, o = lax.scan(step, s0, seq_in)
    o = jnp.moveaxis(o, 0, 1)
    mean = o.mean(-1, keepdims=True)
    var = jnp.square(o - mean).mean(-1, keepdims=True)
    o = ((o - mean) * lax.rsqrt(var + RWKV_GN_EPS)).reshape(bsz, seqlen, RWKV_WIDTH) * gn_g + gn_b
    bonus = jnp.sum(r_h * k_h * r_k, axis=-1, keepdims=True) * v_h
    return (o + bonus.reshape(bsz, seqlen, RWKV_WIDTH)) * g

def _rglru_block(xb, gb, conv_w, conv_b, wa, ba, wx, bx, lam):
    f32 = jnp.float32
    bsz, seqlen, _ = xb.shape
    xb = _causal_dwconv(xb.astype(f32), conv_w, conv_b)
    xh = xb.reshape(bsz, seqlen, LRU_BLOCKS, LRU_BLOCK)
    gate_r = jax.nn.sigmoid(jnp.einsum('btnd,nde->btne', xh, wa).reshape(bsz, seqlen, LRU_WIDTH) + ba)
    gate_i = jax.nn.sigmoid(jnp.einsum('btnd,nde->btne', xh, wx).reshape(bsz, seqlen, LRU_WIDTH) + bx)
    log_a = -LRU_C * jax.nn.softplus(-lam) * gate_r
    a = jnp.exp(log_a)
    u = jnp.sqrt(-jnp.expm1(2.0 * log_a)) * (gate_i * xb)
    _, h = lax.associative_scan(_linear_combine, (a, u), axis=1)
    return h * jax.nn.gelu(gb.astype(f32))

def _conformer_conv(c, conv_w, conv_b, ln_g, ln_b):
    c = c.astype(jnp.float32)
    val, gate = jnp.split(c, 2, axis=-1)
    u = _causal_dwconv(val * jax.nn.sigmoid(gate), conv_w, conv_b)
    return jax.nn.silu(_layer_norm(u, ln_g, ln_b))

def _mamba2_ssd(z, xbc, dt_raw, conv_w, conv_b, dt_bias, a_log, d_skip, norm_g):
    f32 = jnp.float32
    bsz, seqlen, _ = z.shape
    n_c, L = seqlen // SSM_CHUNK, SSM_CHUNK
    G, HG, P, N = SSM_GROUPS, SSM_HEADS_PER_GROUP, SSM_HEAD_DIM, SSM_STATE
    xbc = jax.nn.silu(_causal_dwconv(xbc.astype(f32), conv_w, conv_b))
    xs, bm, cm = jnp.split(xbc, [SSM_INNER, SSM_INNER + G * N], axis=-1)
    dt = jax.nn.softplus(dt_raw.astype(f32) + dt_bias)
    a_head = -jnp.exp(a_log.astype(f32))
    x_c = xs.reshape(bsz, n_c, L, G, HG, P)
    dt_c = dt.reshape(bsz, n_c, L, G, HG)
    b_c = bm.reshape(bsz, n_c, L, G, N)
    c_c = cm.reshape(bsz, n_c, L, G, N)
    a_cum = jnp.cumsum(dt_c * a_head.reshape(G, HG), axis=2)
    xdt = x_c * dt_c[..., None]
    seg = a_cum[:, :, :, None] - a_cum[:, :, None, :]
    causal = jnp.tril(jnp.ones((L, L), dtype=bool))[None, None, :, :, None, None]
    decay_ls = jnp.exp(jnp.where(causal, seg, -jnp.inf))
    cb = jnp.einsum('bclgn,bcsgn->bclsg', c_c, b_c)
    y_diag = jnp.einsum('bclsgh,bcsghp->bclghp', cb[..., None] * decay_ls, xdt)
    decay_to_end = jnp.exp(a_cum[:, :, -1:] - a_cum)
    states = jnp.einsum('bclgn,bclgh,bclghp->bcghpn', b_c, decay_to_end, xdt)
    chunk_decay = jnp.exp(a_cum[:, :, -1])

    def pass_state(s, inp):
        st, dc = inp
        return s * dc[..., None, None] + st, s

    s0 = jnp.zeros((bsz, G, HG, P, N), f32)
    _, prev = lax.scan(pass_state, s0, (jnp.moveaxis(states, 1, 0), jnp.moveaxis(chunk_decay, 1, 0)))
    prev = jnp.moveaxis(prev, 0, 1)
    y_off = jnp.einsum('bclgn,bcghpn,bclgh->bclghp', c_c, prev, jnp.exp(a_cum))
    y = (y_diag + y_off).reshape(bsz, seqlen, SSM_HEADS, P) + d_skip[:, None] * xs.reshape(bsz, seqlen, SSM_HEADS, P)
    y = y.reshape(bsz, seqlen, SSM_INNER) * jax.nn.silu(z.astype(f32))
    yg = y.reshape(bsz, seqlen, G, SSM_INNER // G)
    yg = yg * lax.rsqrt(jnp.mean(jnp.square(yg), axis=-1, keepdims=True) + LN_EPS)
    return yg.reshape(bsz, seqlen, SSM_INNER) * norm_g

def _mem_cross_attn(h, mem, wq, wk, wv, wo):
    bsz, seqlen, _ = h.shape
    q = (h @ wq).reshape(bsz, seqlen, XA_HEADS, XA_HEAD_DIM)
    k = (mem @ wk).reshape(bsz, mem.shape[1], XA_HEADS, XA_HEAD_DIM)
    v = (mem @ wv).reshape(bsz, mem.shape[1], XA_HEADS, XA_HEAD_DIM)
    s = jnp.einsum('bthd,bmhd->bhtm', q, k).astype(jnp.float32) * (XA_HEAD_DIM ** -0.5)
    pr = jax.nn.softmax(s, axis=-1).astype(v.dtype)
    o = jnp.einsum('bhtm,bmhd->bthd', pr, v).reshape(bsz, seqlen, D_MODEL)
    return o @ wo

def setup_inputs(seed: int = 0) -> dict:
    key = jax.random.key(seed)
    keys = jax.random.split(key, 64)
    counter = iter(range(64))
    nk = lambda: keys[next(counter)]
    f32 = jnp.float32
    nrm = lambda shape, scale: scale * jax.random.normal(nk(), shape, f32)
    unif = lambda shape, lo, hi: jax.random.uniform(nk(), shape, f32, lo, hi)
    d_in = D_MODEL ** -0.5
    inp = {}
    inp['x'] = nrm((BATCH, SEQ, D_MODEL), 1.0)
    inp['mem'] = nrm((BATCH, N_MEM, D_MODEL), 1.0)
    inp['ev_w_in'] = nrm((N_EVEN, D_MODEL, EVEN_IN), d_in)
    inp['ev_mu'] = unif((N_EVEN, RWKV_COLS), 0.0, 1.0)
    inp['ev_w0'] = unif((N_EVEN, RWKV_WIDTH), -6.0, -1.0)
    inp['ev_w2'] = nrm((N_EVEN, W_LORA, RWKV_WIDTH), 0.1 * W_LORA ** -0.5)
    inp['ev_a0'] = nrm((N_EVEN, RWKV_WIDTH), 0.1)
    inp['ev_a2'] = nrm((N_EVEN, A_LORA, RWKV_WIDTH), 0.1 * A_LORA ** -0.5)
    inp['ev_g2'] = nrm((N_EVEN, G_LORA, RWKV_WIDTH), G_LORA ** -0.5)
    inp['ev_k_k'] = 0.85 + nrm((N_EVEN, RWKV_WIDTH), 0.05)
    inp['ev_k_a'] = 1.0 + nrm((N_EVEN, RWKV_WIDTH), 0.05)
    inp['ev_r_k'] = nrm((N_EVEN, RWKV_HEADS, RWKV_HEAD_DIM), 0.1)
    inp['ev_gn_g'] = 1.0 + nrm((N_EVEN, RWKV_WIDTH), 0.05)
    inp['ev_gn_b'] = nrm((N_EVEN, RWKV_WIDTH), 0.01)
    inp['ev_lru_conv_w'] = nrm((N_EVEN, LRU_CONV, LRU_WIDTH), LRU_CONV ** -0.5)
    inp['ev_lru_conv_b'] = nrm((N_EVEN, LRU_WIDTH), 0.01)
    inp['ev_lru_wa'] = nrm((N_EVEN, LRU_BLOCKS, LRU_BLOCK, LRU_BLOCK), LRU_BLOCK ** -0.5)
    inp['ev_lru_ba'] = nrm((N_EVEN, LRU_WIDTH), 0.01)
    inp['ev_lru_wx'] = nrm((N_EVEN, LRU_BLOCKS, LRU_BLOCK, LRU_BLOCK), LRU_BLOCK ** -0.5)
    inp['ev_lru_bx'] = nrm((N_EVEN, LRU_WIDTH), 0.01)
    a_c = unif((N_EVEN, LRU_WIDTH), 0.9, 0.999) ** (1.0 / LRU_C)
    inp['ev_lru_lam'] = jnp.log(a_c) - jnp.log1p(-a_c)
    inp['ev_w_out'] = nrm((N_EVEN, EVEN_MIX, D_MODEL), DN_BETA * EVEN_MIX ** -0.5)
    inp['od_w_in'] = nrm((N_ODD, D_MODEL, ODD_IN), d_in)
    inp['od_cf_conv_w'] = nrm((N_ODD, CONF_CONV, CONF_WIDTH), CONF_CONV ** -0.5)
    inp['od_cf_conv_b'] = nrm((N_ODD, CONF_WIDTH), 0.01)
    inp['od_cf_ln_g'] = 1.0 + nrm((N_ODD, CONF_WIDTH), 0.05)
    inp['od_cf_ln_b'] = nrm((N_ODD, CONF_WIDTH), 0.01)
    inp['od_ssm_conv_w'] = nrm((N_ODD, SSM_CONV, SSM_XBC), SSM_CONV ** -0.5)
    inp['od_ssm_conv_b'] = nrm((N_ODD, SSM_XBC), 0.01)
    dt0 = jnp.maximum(jnp.exp(unif((N_ODD, SSM_HEADS), math.log(1e-3), math.log(1e-1))), 1e-4)
    inp['od_dt_bias'] = dt0 + jnp.log(-jnp.expm1(-dt0))
    inp['od_a_log'] = jnp.log(unif((N_ODD, SSM_HEADS), 1.0, 16.0))
    inp['od_d_skip'] = 1.0 + nrm((N_ODD, SSM_HEADS), 0.1)
    inp['od_ssm_norm_g'] = 1.0 + nrm((N_ODD, SSM_INNER), 0.05)
    inp['od_w_out'] = nrm((N_ODD, ODD_MIX, D_MODEL), DN_BETA * ODD_MIX ** -0.5)
    inp['xa_wq'] = nrm((DEPTH, D_MODEL, D_MODEL), d_in)
    inp['xa_wk'] = nrm((DEPTH, D_MODEL, D_MODEL), d_in)
    inp['xa_wv'] = nrm((DEPTH, D_MODEL, D_MODEL), d_in)
    inp['xa_wo'] = nrm((DEPTH, D_MODEL, D_MODEL), DN_BETA * d_in)
    inp['ffn_w1'] = nrm((DEPTH, D_MODEL, D_FF), d_in)
    inp['ffn_w2'] = nrm((DEPTH, D_FF, D_MODEL), DN_BETA * D_FF ** -0.5)
    inp['ln_mix_g'] = 1.0 + nrm((DEPTH, D_MODEL), 0.05)
    inp['ln_mix_b'] = nrm((DEPTH, D_MODEL), 0.01)
    inp['ln_mem_g'] = 1.0 + nrm((DEPTH, D_MODEL), 0.05)
    inp['ln_mem_b'] = nrm((DEPTH, D_MODEL), 0.01)
    inp['ln_ffn_g'] = 1.0 + nrm((DEPTH, D_MODEL), 0.05)
    inp['ln_ffn_b'] = nrm((DEPTH, D_MODEL), 0.01)
    return inp

def reference(x, mem, ev_w_in, ev_mu, ev_w0, ev_w2, ev_a0, ev_a2, ev_g2, ev_k_k, ev_k_a, ev_r_k,
              ev_gn_g, ev_gn_b, ev_lru_conv_w, ev_lru_conv_b, ev_lru_wa, ev_lru_ba, ev_lru_wx, ev_lru_bx,
              ev_lru_lam, ev_w_out, od_w_in, od_cf_conv_w, od_cf_conv_b, od_cf_ln_g, od_cf_ln_b,
              od_ssm_conv_w, od_ssm_conv_b, od_dt_bias, od_a_log, od_d_skip, od_ssm_norm_g, od_w_out,
              xa_wq, xa_wk, xa_wv, xa_wo, ffn_w1, ffn_w2, ln_mix_g, ln_mix_b, ln_mem_g, ln_mem_b,
              ln_ffn_g, ln_ffn_b):
    h = x
    for i in range(DEPTH):
        j = i // 2
        if i % 2 == 0:
            p = h @ ev_w_in[j]
            y_a = _rwkv7_time_mix(p[..., :RWKV_COLS], ev_mu[j], ev_w0[j], ev_w2[j], ev_a0[j], ev_a2[j],
                                  ev_g2[j], ev_k_k[j], ev_k_a[j], ev_r_k[j], ev_gn_g[j], ev_gn_b[j])
            y_b = _rglru_block(p[..., RWKV_COLS:RWKV_COLS + LRU_WIDTH], p[..., RWKV_COLS + LRU_WIDTH:],
                               ev_lru_conv_w[j], ev_lru_conv_b[j], ev_lru_wa[j], ev_lru_ba[j],
                               ev_lru_wx[j], ev_lru_bx[j], ev_lru_lam[j])
            mix = jnp.concatenate([y_a, y_b], axis=-1).astype(h.dtype) @ ev_w_out[j]
        else:
            p = h @ od_w_in[j]
            o1 = 2 * CONF_WIDTH
            o2 = o1 + SSM_INNER
            o3 = o2 + SSM_XBC
            y_c = _conformer_conv(p[..., :o1], od_cf_conv_w[j], od_cf_conv_b[j], od_cf_ln_g[j], od_cf_ln_b[j])
            y_d = _mamba2_ssd(p[..., o1:o2], p[..., o2:o3], p[..., o3:], od_ssm_conv_w[j], od_ssm_conv_b[j],
                              od_dt_bias[j], od_a_log[j], od_d_skip[j], od_ssm_norm_g[j])
            mix = jnp.concatenate([y_c, y_d], axis=-1).astype(h.dtype) @ od_w_out[j]
        h = _layer_norm(DN_ALPHA * h + mix, ln_mix_g[i], ln_mix_b[i])
        h = _layer_norm(DN_ALPHA * h + _mem_cross_attn(h, mem, xa_wq[i], xa_wk[i], xa_wv[i], xa_wo[i]),
                        ln_mem_g[i], ln_mem_b[i])
        ffn = jnp.square(jax.nn.relu(h @ ffn_w1[i])) @ ffn_w2[i]
        h = _layer_norm(DN_ALPHA * h + ffn, ln_ffn_g[i], ln_ffn_b[i])
    return h


_drawn_inputs = setup_inputs


def setup_inputs(seed=0):
    import zlib

    import numpy as np

    out = dict(_drawn_inputs(seed))
    spreads = {}
    factors = {'ev_w2': 8.0,
     'ev_a0': 8.0,
     'ev_a2': 8.0,
     'ev_k_k': 8.0,
     'ev_k_a': 7.021,
     'ev_gn_g': 7.656,
     'ev_gn_b': 45.101,
     'ev_lru_conv_b': 6.927,
     'ev_lru_ba': 200.0,
     'ev_lru_bx': 64.0,
     'od_cf_conv_b': 8.0,
     'od_cf_ln_g': 7.943,
     'od_cf_ln_b': 64.0,
     'od_ssm_conv_b': 8.0,
     'od_d_skip': 2.973,
     'od_ssm_norm_g': 3.867,
     'ln_mix_b': 3.895,
     'ln_mem_b': 3.635,
     'ln_ffn_b': 3.794}
    for name, (base, spread) in spreads.items():
        noise = np.random.default_rng([zlib.crc32(name.encode()), seed]).standard_normal(out[name].shape)
        drawn = base * np.exp(spread * noise) if base else spread * noise
        out[name] = __import__('jax').numpy.asarray(drawn.astype(out[name].dtype))
    for name, factor in factors.items():
        out[name] = (out[name] * factor).astype(out[name].dtype)
    return out
```

```python
from contextlib import ExitStack

import concourse.bass as bass
from concourse import mybir

F32 = mybir.dt.float32
F32R = mybir.dt.float32r
ALU = mybir.AluOpType
ACT = mybir.ActivationFunctionType
AX_X = mybir.AxisListType.X

P = 128
T = 512
D = 1024
KD = D // P
NT = T // P
MEM = 256
HALF = 512
CHUNK = 1024
W_SLOTS = 3
PAD = 4
PW = PAD + T
ALPHA = 4.0 ** 0.25
LN_EPS = 1e-5
GN_EPS = 64e-5
HEADS_XA = 4
D_FF = 4096
QUARTERS = 4
RC = 64
NRC = T // RC
RD = 64
SC = 128
NSC = T // SC
CONF_TAPS = 31
CP = 32
NEG_EXP_HALF = -0.6065306597126334

STREAM = []
for _l in range(2):
    STREAM += [(f"in{_l}", 22 if _l == 0 else 29), (f"out{_l}", 8 if _l == 0 else 12),
               (f"k{_l}", 8), (f"v{_l}", 8), (f"q{_l}", 8), (f"wo{_l}", 8)]
    for _q in range(QUARTERS):
        STREAM += [(f"up{_l}_{_q}", 8), (f"down{_l}_{_q}", 8)]
FIRST = {}
_n = 0
for _name, _count in STREAM:
    FIRST[_name] = _n
    _n += _count
N_CHUNKS = _n

VEC_TILES = [("mu", 14), ("w0", 4), ("a0", 4), ("kk", 4), ("ka", 4), ("rk", 4), ("gng", 4), ("gnb", 4),
             ("lcw", 16), ("lcb", 4), ("lba", 4), ("lbx", 4), ("lam", 4),
             ("ccw", CONF_TAPS * 4), ("ccb", 4), ("clg", 4), ("clb", 4),
             ("scw", 48), ("scb", 12), ("sng", 8), ("dsk", 8), ("lng", 48), ("lnb", 48), ("dtb", 1), ("alog", 1)]
VEC = {}
_n = 0
for _name, _count in VEC_TILES:
    VEC[_name] = _n
    _n += _count
N_VEC = _n

TILES = []
for _l in range(2):
    if _l == 0:
        TILES += [("in0", 22), ("rg", 4)]
        for _b in range(2):
            TILES += [(f"rdec{_b}", 2), (f"ra{_b}", 2), (f"rss{_b}", 2), (f"rbon{_b}", 2),
                      (f"rprod{_b}", 10), (f"rtok{_b}", 8)]
            for _v in range(1, 6):
                TILES += [(f"ryt{_b}_{_v}", 2), (f"rz{_b}_{_v}", 4 if _v < 5 else 2)]
            TILES += [(f"rgw{_b}", 4)]
            for _c in range(NRC):
                TILES += [(f"rsa{_b}_{_c}", 1), (f"rst{_b}_{_c}", 1), (f"ro{_b}_{_c}", 1)]
            TILES += [(f"rback{_b}", 2)]
        TILES += [("lru", 8), ("out0", 8)]
    else:
        TILES += [("in1", 29), ("cmean", 1), ("cvar", 1), ("stok", 2), ("slast", 1), ("sxt", 8), ("sbt", 2),
                  ("scb", 2), ("sst", 6)]
        for _h in range(8):
            TILES += [(f"sbc{_h}", 2), (f"sy{_h}", 1)]
        TILES += [("srms", 2), ("out1", 8)]
    TILES += [(f"k{_l}", 8), (f"lnt{_l}_0", 8), (f"v{_l}", 4), (f"q{_l}", 8), (f"s{_l}", 8),
              (f"pt{_l}_0", 4), (f"pv{_l}_0", 4), (f"pt{_l}_1", 4), (f"pv{_l}_1", 4), (f"wo{_l}", 8),
              (f"lnt{_l}_1", 8)]
    for _q in range(QUARTERS):
        TILES += [(f"up{_l}_{_q}", 8), (f"down{_l}_{_q}", 8)]
    if _l == 0:
        TILES += [("lnt0_2", 8)]
TILE0 = {}
TILE_OWNER = []
for _name, _count in TILES:
    TILE0[_name] = len(TILE_OWNER)
    TILE_OWNER += [(_name, _i + 1) for _i in range(_count)]
FAMILY, BEFORE = {}, {}
_seen = {}
for _name, _count in TILES:
    _kind = _name.rstrip("0123456789_")
    FAMILY[_name] = _kind
    BEFORE[_name] = _seen.get(_kind, 0)
    _seen[_kind] = BEFORE[_name] + _count


def build(nc, x_tok, x_feat, mem_feat, weights, vectors, lora, lru_w, ln_rows, out):
    with ExitStack() as ctx:
        base = (nc.sbuf_base + 31) // 32 * 32
        place = {"at": base}

        def sb(name, shape, dt=F32, at=None):
            size = 4
            for n in shape[1:]:
                size *= n
            if at is None:
                at = place["at"]
                place["at"] = at + (size + 31) // 32 * 32
            return nc.alloc_sbuf_tensor_at(name, shape, dt, offset=at)

        w_raw = sb("w_raw", [P, W_SLOTS, CHUNK])
        w_hi = sb("w_hi", [P, W_SLOTS, CHUNK], F32R)
        w_lo = sb("w_lo", [P, W_SLOTS, CHUNK], F32R)
        h = sb("h", [P, NT, D])
        act_at = place["at"]
        act_hi = sb("act_hi", [P, 12, T], F32R)
        act_lo = sb("act_lo", [P, 12, T], F32R)
        aux_at = place["at"]
        aux_hi = sb("aux_hi", [P, 8, T], F32R)
        aux_lo = sb("aux_lo", [P, 8, T], F32R)
        k_hi = sb("k_hi", [P, 8, MEM], F32R)
        k_lo = sb("k_lo", [P, 8, MEM], F32R)
        v_hi = sb("v_hi", [P, 2, D], F32R)
        v_lo = sb("v_lo", [P, 2, D], F32R)
        stage = sb("stage", [P, 8, T])
        mix_end = place["at"]
        gb = sb("gb", [P, 2, D])
        vec = sb("vec", [P, N_VEC])
        ident = sb("ident", [P, P])
        ones = sb("ones", [P, P])
        bdones = sb("bdones", [P, P])
        lastrow = sb("lastrow", [P, P])
        eye2 = sb("eye2", [P, RC])
        m_strict = sb("m_strict", [P, RC])
        m_incl = sb("m_incl", [P, RC])
        m_tri = sb("m_tri", [P, SC])
        m_lev = sb("m_lev", [P, 7, RC])
        m_scan = sb("m_scan", [P, T])
        small = sb("small", [P, 256])
        lnst = sb("lnst", [P, NT, 12])
        lnmv = sb("lnmv", [P, NT, 2])
        lnsd = sb("lnsd", [P, NT])
        lora_sb = sb("lora_sb", [P, 2, T])
        lru_sb = sb("lru_sb", [P, 8, P])
        assert place["at"] <= nc.sbuf_usable_end, place["at"]

        p0 = sb("p0", [P, 22, PW], at=aux_at)
        after_p0 = (aux_at + 22 * PW * 4 + 31) // 32 * 32
        ra = [sb(f"ra{i}", [P, 2, T], at=act_at + i * 4096) for i in range(12)]
        ra += [sb(f"ra{12 + i}", [P, 2, T], at=after_p0 + i * 4096) for i in range(6)]
        rh = sb("rh", [P, 2, 2, RD], at=after_p0 + 6 * 4096)
        rsa = sb("rsa", [P, 2, 2, RD], at=after_p0 + 6 * 4096 + 1024)
        assert after_p0 + 6 * 4096 + 2048 <= mix_end
        gts = sb("gts", [P, 4, T], at=after_p0 + 6 * 4096 + 2048)
        assert after_p0 + 6 * 4096 + 2048 + 8192 <= mix_end
        act_like, lr, li, lq, lt = (sb(n, [P, 4, T], at=act_at + i * 8192)
                                    for i, n in enumerate(["lconv", "lr", "li", "lq", "lt"]))
        YT0 = [0, 1, 2, 3, 14, 15, 16, 17]
        p1 = sb("p1", [P, 29, PW], at=aux_at)
        after_p1 = (aux_at + 29 * PW * 4 + 31) // 32 * 32
        cu = sb("cu", [P, 4, CP + T], at=act_at)
        cacc = sb("cacc", [P, 4, T], at=act_at + 4 * (CP + T) * 4)
        ctmp = sb("ctmp", [P, 4, T], at=act_at + 4 * (CP + T) * 4 + 8192)
        sconv = sb("sconv", [P, 2, T], at=act_at + 4 * (CP + T) * 4 + 16384)
        c_std = sb("c_std", [P, T], at=act_at + 4 * (CP + T) * 4 + 16384 + 4096)[:]
        YT1 = [0, 1, 2, 3] + list(range(8, 16))
        xdt = sb("xdt", [P, NSC, D], at=act_at)
        xdtd = sb("xdtd", [P, NSC, D], at=act_at + 16384)
        prev = sb("prev", [P, NSC, D], at=act_at + 32768)
        at1 = after_p1
        bt = sb("bt", [P, NSC, 256], at=at1)
        cbt = sb("cbt", [P, NSC, 2, SC], at=at1 + 4096)
        cs = sb("cs", [P, 2, T], at=at1 + 8192)
        mt = sb("mt", [P, 2, T], at=at1 + 12288)
        stm = sb("stm", [P, 6, NSC, 16], at=at1 + 16384)
        sdt = sb("sdt", [16, 2, T], at=at1 + 16384 + 1536)
        assert at1 + 16384 + 1536 + 4096 <= mix_end, (at1, mix_end)

        ps = [ctx.enter_context(nc.psum_tensor(f"bank{i}", [P, 512], F32)) for i in range(8)]

        sems = {}

        def S(name):
            if name not in sems:
                sems[name] = ctx.enter_context(nc.semaphore(name))
            return sems[name]

        def V(name, i):
            c = VEC[name] + i
            return vec[:, c:c + 1]

        def bank(stg, i):
            return ps[(TILE0[stg] + i) % 8]

        def of(stg, suffix, n):
            return S(FAMILY[stg] + suffix), BEFORE[stg] + n

        def out_sem(stg, n):
            return of(stg, "_out", n)

        landed = [S(f"w_landed{i}") for i in range(W_SLOTS)]
        block = ctx.enter_context(nc.Block())

        def bc(ap, n):
            return ap.unsqueeze(2).to_broadcast([ap.shape[0], ap.shape[1], n])

        def mid(ap, n):
            return ap.unsqueeze(1).to_broadcast([ap.shape[0], n, ap.shape[1]])

        @block.sync
        def _(sp):
            sp.dma_start(stage[:], x_feat).then_inc(S("x_in"), 16)
            sp.dma_start(w_raw[:, 0], weights[0]).then_inc(landed[0], 16)
            sp.dma_start(vec[:], vectors).then_inc(S("const_in"), 16)
            sp.dma_start(w_raw[:, 1], weights[1]).then_inc(landed[1], 16)
            sp.dma_start(h[:], x_tok).then_inc(S("h_in"), 16)
            sp.dma_start(lora_sb[:], lora).then_inc(S("const_in"), 16)
            sp.dma_start(lru_sb[:], lru_w).then_inc(S("const_in"), 16)
            ln_at = {FIRST["out0"] + 3: 0, FIRST["wo0"] + 3: 1, FIRST["down0_3"] + 1: 2,
                     FIRST["out1"] + 3: 3, FIRST["wo1"] + 3: 4, FIRST["down1_3"] + 1: 5}
            for c in range(2, N_CHUNKS):
                if c >= W_SLOTS:
                    sp.wait_ge(S("w_split"), c - W_SLOTS + 1)
                sp.dma_start(w_raw[:, c % W_SLOTS], weights[c]).then_inc(landed[c % W_SLOTS], 16)
                if c in ln_at:
                    n = ln_at[c]
                    if n:
                        sp.wait_ge(S("ln_used"), n)
                    sp.dma_start(gb[:], ln_rows[n:n + 1].to_broadcast([P, 2, D])).then_inc(S("gb_in"), 16)
                for l in range(2):
                    if c == FIRST[f"k{l}"]:
                        sp.wait_ge(S("mix_done"), l + 1)
                        sp.dma_start(stage[:].rearrange("p a t -> p (a t)")[:, 0:8 * MEM], mem_feat)\
                            .then_inc(S("mem_in"), 16)
            for t in range(NT):
                sp.wait_ge(S("out_rows"), t + 1)
                sp.dma_start(out[:, t], h[:, t]).then_inc(S("stored"), 16)
            sp.wait_ge(S("stored"), 16 * NT)

        @block.gpsimd
        def _(pool):
            def fill(t, value):
                pool.memset(t, value).then_inc(S("pool_step"), 1)
                fill.n += 1
                pool.wait_ge(S("pool_step"), fill.n)
            fill.n = 0

            def sel(t, op, base, pattern, mult, fillv, inner=None):
                pool.affine_select(out=t, in_=t, compare_op=op, fill=fillv, base=base, pattern=pattern,
                                   channel_multiplier=mult).then_inc(S("pool_step"), 1)
                fill.n += 1
                pool.wait_ge(S("pool_step"), fill.n)

            fill(ident[:], 0.0)
            sel(ident[:], ALU.not_equal, 0, [[-1, P]], 1, 1.0)
            fill(ones[:], 1.0)
            fill(bdones[:], 0.0)
            fill(bdones[0:64, 0:64], 1.0)
            fill(bdones[64:128, 64:128], 1.0)
            fill(lastrow[:], 0.0)
            sel(lastrow[:], ALU.not_equal, -(P - 1), [[0, P]], 1, 1.0)
            fill(m_tri[:], 1.0)
            sel(m_tri[:], ALU.is_ge, 0, [[1, SC]], -1, 0.0)
            fill(eye2[:], 0.0)
            sel(eye2[:], ALU.not_equal, 0, [[-1, RC]], 1, 1.0)
            sel(eye2[:], ALU.not_equal, -RC, [[-1, RC]], 1, 1.0)
            fill(m_strict[:], 1.0)
            fill(m_incl[:], 1.0)
            for q in range(2):
                rows = slice(RC * q, RC * q + RC)
                sel(m_strict[rows], ALU.is_gt, 0, [[1, RC]], -1, 0.0)
                sel(m_incl[rows], ALU.is_ge, 0, [[1, RC]], -1, 0.0)
            fill(m_lev[:], 1.0)
            for v in range(6):
                n = 1 << v
                for q in range(2):
                    rows = slice(RC * q, RC * q + RC)
                    view = m_lev[rows, v].rearrange("p (b u) -> p b u", u=2 * n)
                    sel(view, ALU.is_ge, -n, [[-2 * n, RC // (2 * n)], [0, 2 * n]], 1, 0.0)
                    sel(view, ALU.is_ge, 2 * n - 1, [[2 * n, RC // (2 * n)], [0, 2 * n]], -1, 0.0)
                    sel(view, ALU.is_ge, n - 1, [[0, RC // (2 * n)], [-1, 2 * n]], 0, 0.0)
            for q in range(2):
                rows = slice(RC * q, RC * q + RC)
                view = m_lev[rows, 6].rearrange("p (b u) -> p b u", u=2)
                sel(view, ALU.is_equal, 0, [[-2, RC // 2], [0, 2]], 1, 0.0)
                sel(view, ALU.is_ge, -1, [[0, RC // 2], [1, 2]], 0, 0.0)
            fill(m_scan[:], 1.0)
            fill(m_scan[:].rearrange("p (c t) -> p c t", t=RC)[:, :, 0:1], 0.0)
            pool.memset(small[:], 0.0).then_inc(S("masks"), 1)

            def affine(n):
                pool.wait_ge(S("gb_in"), 16 * (n + 1))
                l, which = divmod(n, 3)
                pool.wait_ge(*of(f"lnt{l}_{which}", "_mm", 8))
                for t in range(NT):
                    pool.tensor_tensor(h[:, t], h[:, t], gb[:, 0], ALU.mult).then_inc(S("pool_step"), 1)
                    fill.n += 1
                    pool.wait_ge(S("pool_step"), fill.n)
                    pool.tensor_tensor(h[:, t], h[:, t], gb[:, 1], ALU.add).then_inc(S("h_ready"), 1)
                pool.wait_ge(S("h_ready"), NT * (n + 1))
                pool.memset(small[:, 253:254], 0.0).then_inc(S("ln_used"), 1)
                pool.wait_ge(S("ln_used"), n + 1)

            pool.wait_ge(S("mix_done"), 1)
            fill(m_scan[:], 1.0)
            pool.memset(m_scan[:].rearrange("p (c t) -> p c t", t=SC)[:, :, 0:1], 0.0).then_inc(S("masks"), 1)
            for n in range(5):
                affine(n)

        @block.tensor
        def _(pe):
            def take(stg, i):
                n = TILE0[stg] + i
                if n >= 8:
                    owner, k = TILE_OWNER[n - 8]
                    pe.wait_ge(*out_sem(owner, k))
                return ps[n % 8]

            def mm3(o, whi, wlo, xhi, xlo, first, last):
                pe.matmul(o, whi, xlo, start=first, stop=False)
                pe.matmul(o, wlo, xhi, start=False, stop=False)
                return pe.matmul(o, whi, xhi, start=False, stop=last)

            def feature_major(stg, count, xhi, xlo, n, ready=None):
                for i in range(count):
                    c = FIRST[stg] + i
                    s = c % W_SLOTS
                    o = take(stg, i)
                    pe.wait_ge(S("w_split"), c + 1)
                    for k in range(KD):
                        if ready and i == 0:
                            pe.wait_ge(*of(ready, "_out", k + 1))
                        cols = slice(k * P, k * P + P)
                        last = mm3(o[:, 0:n], w_hi[:, s, cols], w_lo[:, s, cols], xhi[:, k, 0:n], xlo[:, k, 0:n],
                                   k == 0, k == KD - 1)
                    last.then_inc(S("chunk_done"), 1)

            def token_major(stg, tiles, kts, xhi, xlo, ready=None):
                for half in range(2):
                    o = [take(stg, half * tiles + t) for t in range(tiles)]
                    for i in range(kts // 2):
                        c = FIRST[stg] + half * (kts // 2) + i
                        s = c % W_SLOTS
                        pe.wait_ge(S("w_split"), c + 1)
                        for kk in range(2):
                            k = 2 * i + kk
                            if ready and half == 0:
                                pe.wait_ge(*of(*ready, k + 1))
                            cols = slice(kk * HALF, kk * HALF + HALF)
                            for t in range(tiles):
                                tok = slice(t * P, t * P + P)
                                last = mm3(o[t][:, 0:HALF], xhi[:, k, tok], xlo[:, k, tok], w_hi[:, s, cols],
                                           w_lo[:, s, cols], k == 0, k == kts - 1)
                        last.then_inc(S("chunk_done"), 1)

            def heads2(o, lhs, rhs, n, **kw):
                for q in range(2):
                    rows = slice(64 * q, 64 * q + 64)
                    last = pe.matmul(o[rows, 0:n], lhs[rows], rhs[rows], **kw)
                return last

            def rwkv():
                pe.wait_ge(S("r_lora"), 1)
                for j in range(4):
                    o = take("rg", j)
                    pe.matmul(o[:], lora_sb[:, 1, j * P:j * P + P], p0[:, 13, PAD:PW], start=True, stop=True)\
                        .then_inc(S("rg_mm"), 1)
                for b in range(2):
                    for j in range(2):
                        o = take(f"rdec{b}", j)
                        col = slice((2 * b + j) * P, (2 * b + j) * P + P)
                        pe.matmul(o[:], lora_sb[0:64, 0, col], p0[0:64, 12, PAD:PW], start=True, stop=True)\
                            .then_inc(S("rlora_mm"), 1)
                    for j in range(2):
                        o = take(f"ra{b}", j)
                        col = slice((2 * b + j) * P, (2 * b + j) * P + P)
                        pe.matmul(o[:], lora_sb[64:128, 0, col], p0[64:128, 12, PAD:PW], start=True, stop=True)\
                            .then_inc(S("rlora_mm"), 1)
                    pe.wait_ge(S("r_kksq"), b + 1)
                    for j in range(2):
                        o = take(f"rss{b}", j)
                        pe.matmul(o[:], bdones[:], ra[4][:, j], start=True, stop=True).then_inc(S("rss_mm"), 1)
                    pe.wait_ge(S("r_rkr"), b + 1)
                    for j in range(2):
                        o = take(f"rbon{b}", j)
                        pe.matmul(o[:], bdones[:], ra[5][:, j], start=True, stop=True).then_inc(S("rbon_mm"), 1)
                    pe.wait_ge(S("r_ops"), b + 1)
                    r_, k_, v_ = (p0[:, 4 * m + 2 * b:4 * m + 2 * b + 2, PAD:PW] for m in range(3))
                    alpha, nbh, kh, rho, nbt, kt = ra[4], ra[6], ra[7], r_, ra[3], k_
                    for n, (lhs, rhs) in enumerate([(alpha, nbh), (nbh, alpha), (kh, alpha), (nbh, rho), (kh, rho)]):
                        for j in range(2):
                            o = take(f"rprod{b}", 2 * n + j)
                            for c in range(NRC):
                                cs_ = slice(c * RC, c * RC + RC)
                                last = heads2(o[:, cs_], lhs[:, j, cs_], rhs[:, j, cs_], RC, start=True, stop=True)
                            last.then_inc(S("rprod_mm"), 1)
                    for n, src in enumerate([alpha, nbt, kt, v_]):
                        for j in range(2):
                            o = take(f"rtok{b}", 2 * n + j)
                            for c in range(NRC):
                                cs_ = slice(c * RC, c * RC + RC)
                                last = heads2(o[:, cs_], src[:, j, cs_], eye2[:], RC, start=True, stop=True)
                            last.then_inc(S("rtok_mm"), 1)
                    X, XT, YT, MO = ra[1], ra[2], ra[6], ra[7]
                    for v in range(1, 6):
                        pe.wait_ge(S("r_moff"), 5 * b + v)
                        for j in range(2):
                            o = take(f"ryt{b}_{v}", j)
                            for c in range(NRC):
                                cs_ = slice(c * RC, c * RC + RC)
                                last = heads2(o[:, cs_], MO[:, j, cs_], XT[:, j, cs_], RC, start=True, stop=True)
                            last.then_inc(S("ryt_mm"), 1)
                        for j in range(2):
                            pe.wait_ge(*out_sem(f"ryt{b}_{v}", j + 1))
                            if v < 5:
                                o = take(f"rz{b}_{v}", 2 * j)
                                for c in range(NRC):
                                    cs_ = slice(c * RC, c * RC + RC)
                                    last = heads2(o[:, cs_], YT[:, j, cs_], X[:, j, cs_], RC, start=True, stop=True)
                                last.then_inc(S("rz_mm"), 1)
                            o = take(f"rz{b}_{v}", 2 * j + 1 if v < 5 else j)
                            for c in range(NRC):
                                cs_ = slice(c * RC, c * RC + RC)
                                last = heads2(o[:, cs_], X[:, j, cs_], YT[:, j, cs_], RC, start=True, stop=True)
                            last.then_inc(S("rz_mm"), 1)
                    pe.wait_ge(*out_sem(f"rz{b}_5", 2))
                    pe.wait_ge(*out_sem(f"rtok{b}", 8))
                    for j in range(2):
                        o = take(f"rgw{b}", 2 * j)
                        for c in range(NRC):
                            cs_ = slice(c * RC, c * RC + RC)
                            last = heads2(o[:, cs_], ra[9][:, j, cs_], ra[15][:, j, cs_], RC, start=True, stop=True)
                        last.then_inc(S("rgw_mm"), 1)
                        o = take(f"rgw{b}", 2 * j + 1)
                        for c in range(NRC):
                            cs_ = slice(c * RC, c * RC + RC)
                            last = heads2(o[:, cs_], ra[12][:, j, cs_], XT[:, j, cs_], RC, start=True, stop=True)
                        last.then_inc(S("rgw_mm"), 1)
                    W, GT, nbtok, ktok, vtok = ra[5], ra[0], ra[13], ra[14], ra[15]
                    prb, prk = ra[10], ra[11]
                    pe.wait_ge(*out_sem(f"rgw{b}", 4))
                    for c in range(NRC):
                        cs_ = slice(c * RC, c * RC + RC)
                        hin, hout = rh[:, c % 2], rh[:, (c + 1) % 2]
                        o = take(f"rsa{b}_{c}", 0)
                        for j in range(2):
                            oj = o[:, j * RD:j * RD + RD]
                            last = heads2(oj, XT[:, j, cs_], W[:, j, cs_], RD, start=True, stop=(c == 0))
                            if c:
                                if j == 0:
                                    pe.wait_ge(*out_sem(f"rst{b}_{c - 1}", 1))
                                last = heads2(oj, GT[:, j, cs_], hin[:, j], RD, start=False, stop=True)
                        last.then_inc(S("rsa_mm"), 1)
                        o = take(f"rst{b}_{c}", 0)
                        pe.wait_ge(*out_sem(f"rsa{b}_{c}", 1))
                        for j in range(2):
                            oj = o[:, j * RD:j * RD + RD]
                            heads2(oj, ktok[:, j, cs_], vtok[:, j, cs_], RD, start=True, stop=False)
                            last = heads2(oj, nbtok[:, j, cs_], rsa[:, c % 2, j], RD, start=False, stop=True)
                        last.then_inc(S("rst_mm"), 1)
                        o = take(f"ro{b}_{c}", 0)
                        for j in range(2):
                            oj = o[:, j * RD:j * RD + RD]
                            if c:
                                heads2(oj, rho[:, j, cs_], hin[:, j], RD, start=True, stop=False)
                            heads2(oj, prb[:, j, cs_], rsa[:, c % 2, j], RD, start=(c == 0), stop=False)
                            last = heads2(oj, prk[:, j, cs_], vtok[:, j, cs_], RD, start=False, stop=True)
                        last.then_inc(S("ro_mm"), 1)
                    pe.wait_ge(S("r_gn"), b + 1)
                    for j in range(2):
                        o = take(f"rback{b}", j)
                        for c in range(NRC):
                            cs_ = slice(c * RC, c * RC + RC)
                            last = heads2(o[:, cs_], ra[12][:, j, cs_], eye2[:], RC, start=True, stop=True)
                        last.then_inc(S("rback_mm"), 1)

            def lru():
                pe.wait_ge(S("l_conv"), 4)
                for j in range(4):
                    for m in range(2):
                        o = take("lru", 2 * j + m)
                        pe.matmul(o[:], lru_sb[:, 4 * m + j], act_like[:, j], start=True, stop=True)\
                            .then_inc(S("lru_mm"), 1)

            def odd_mixer():
                pe.wait_ge(S("c_conv"), 4)
                o = take("cmean", 0)
                for j in range(4):
                    last = pe.matmul(o[:], ones[:], cacc[:, j], start=(j == 0), stop=(j == 3))
                last.then_inc(S("c_mm"), 1)
                pe.wait_ge(S("c_sq"), 1)
                o = take("cvar", 0)
                for j in range(4):
                    last = pe.matmul(o[:], ones[:], ctmp[:, j], start=(j == 0), stop=(j == 3))
                last.then_inc(S("c_mm"), 1)
                pe.wait_ge(S("s_acum"), 1)
                for m in range(2):
                    o = take("stok", m)
                    for c in range(NSC):
                        last = pe.transpose(o[:, c * 16:c * 16 + 16], sdt[:, m, c * SC:c * SC + SC], ident[0:16, 0:16])
                    last.then_inc(S("stok_mm"), 1)
                o = take("slast", 0)
                pe.wait_ge(*out_sem("stok", 2))
                pe.matmul(o[:, 0:64], lastrow[:], stm[:, 1].rearrange("p c h -> p (c h)"), start=True, stop=True)\
                    .then_inc(S("slast_mm"), 1)
                xs = p1[:, 16:24, PAD:PW]
                pe.wait_ge(S("s_conv"), 12)
                for c in range(NSC):
                    for q in range(2):
                        o = take("sxt", 2 * c + q)
                        for j in range(4):
                            last = pe.transpose(o[:, j * P:j * P + P], xs[:, 4 * q + j, c * SC:c * SC + SC], ident[:])
                        last.then_inc(S("sxt_mm"), 1)
                for q in range(2):
                    o = take("sbt", q)
                    for c in range(2):
                        for g in range(2):
                            n = 2 * c + g
                            last = pe.transpose(o[:, n * P:n * P + P],
                                                p1[:, 24 + g, PAD + (2 * q + c) * SC:PAD + (2 * q + c + 1) * SC], ident[:])
                    last.then_inc(S("sbt_mm"), 1)
                for g in range(2):
                    o = take("scb", g)
                    for c in range(NSC):
                        cols = slice(PAD + c * SC, PAD + c * SC + SC)
                        last = pe.matmul(o[:, c * SC:c * SC + SC], p1[:, 24 + g, cols], p1[:, 26 + g, cols],
                                         start=True, stop=True)
                    last.then_inc(S("scb_mm"), 1)
                pe.wait_ge(*out_sem("sbt", 2))
                pe.wait_ge(*out_sem("sxt", 8))
                for c in range(NSC - 1):
                    for g in range(2):
                        o = take("sst", 2 * c + g)
                        pe.matmul(o[:], bt[:, c, g * P:g * P + P], xdtd[:, c, g * 512:g * 512 + 512],
                                  start=True, stop=True).then_inc(S("sst_mm"), 1)
                for hp in range(8):
                    for q in range(2):
                        hd = 2 * hp + q
                        o = take(f"sbc{hp}", q)
                        pe.matmul(o[:], ident[0:16, hd:hd + 1].to_broadcast([16, P]), sdt[:, 1, :], start=True, stop=True)\
                            .then_inc(S("sbc_mm"), 1)
                    o = take(f"sy{hp}", 0)
                    pe.wait_ge(*out_sem("sst", 6))
                    for q in range(2):
                        hd = 2 * hp + q
                        pe.wait_ge(S("s_mt"), 2 * hp + q + 1)
                        for c in range(NSC):
                            rows = slice(64 * q, 64 * q + 64)
                            cols = slice(c * SC, c * SC + SC)
                            last = pe.matmul(o[rows, cols], xdt[:, c, hd * 64:hd * 64 + 64], mt[:, q, cols],
                                             start=True, stop=(c == 0))
                            if c:
                                last = pe.matmul(o[rows, cols], prev[:, c, hd * 64:hd * 64 + 64], cs[:, q, cols],
                                                 start=False, stop=True)
                    last.then_inc(S("sy_mm"), 1)
                for g in range(2):
                    o = take("srms", g)
                    for j in range(4):
                        pe.wait_ge(S("s_ysq"), 4 * g + j + 1)
                        last = pe.matmul(o[:], ones[:], p1[:, 16 + 4 * g + j, PAD:PW], start=(j == 0), stop=(j == 3))
                    last.then_inc(S("srms_mm"), 1)

            def to_features(l, which):
                n = 3 * l + which
                pe.wait_ge(S("ln_rows"), NT * (n + 1))
                for k in range(KD):
                    o = take(f"lnt{l}_{which}", k)
                    for t in range(NT):
                        last = pe.transpose(o[:, t * P:t * P + P], h[:, t, k * P:k * P + P], ident[:])
                    last.then_inc(S("lnt_mm"), 1)

            def attention(l):
                pe.wait_ge(S("mem_split"), l + 1)
                memv = [a[:].rearrange("p a t -> p (a t)")[:, 0:8 * MEM].rearrange("p (a t) -> p a t", a=8)
                        for a in (aux_hi, aux_lo)]
                feature_major(f"k{l}", 8, memv[0], memv[1], MEM)
                to_features(l, 0)
                token_major(f"v{l}", 2, KD, memv[0], memv[1])
                feature_major(f"q{l}", 8, act_hi, act_lo, T, ready=f"lnt{l}_0")
                pe.wait_ge(*out_sem(f"q{l}", 8))
                pe.wait_ge(*out_sem(f"k{l}", 8))
                for hp in range(2):
                    for t in range(NT):
                        o = take(f"s{l}", 4 * hp + t)
                        tok = slice(t * P, t * P + P)
                        for q in range(2):
                            hd = 2 * hp + q
                            for k in range(2):
                                last = mm3(o[:, q * MEM:q * MEM + MEM], aux_hi[:, 2 * hd + k, tok],
                                           aux_lo[:, 2 * hd + k, tok], k_hi[:, 2 * hd + k], k_lo[:, 2 * hd + k],
                                           k == 0, k == 1)
                        last.then_inc(S("s_mm"), 1)
                pe.wait_ge(*out_sem(f"v{l}", 4))
                for hp in range(2):
                    for t in range(NT):
                        pe.wait_ge(S("p_ready"), 8 * l + 4 * hp + t + 1)
                        o = take(f"pt{l}_{hp}", t)
                        for q in range(2):
                            for m in range(2):
                                n = 2 * q + m
                                last = pe.transpose(o[:, n * P:n * P + P],
                                                    stage[:, 4 * hp + t, q * MEM + m * P:q * MEM + m * P + P], ident[:])
                        last.then_inc(S("pt_mm"), 1)
                    pe.wait_ge(*out_sem(f"pt{l}_{hp}", 4))
                    for q in range(2):
                        for dt in range(2):
                            o = take(f"pv{l}_{hp}", 2 * q + dt)
                            col = slice((2 * hp + q) * 256 + dt * P, (2 * hp + q) * 256 + dt * P + P)
                            for m in range(2):
                                last = mm3(o[:], v_hi[:, m, col], v_lo[:, m, col], act_hi[:, 8 + 2 * q + m],
                                           act_lo[:, 8 + 2 * q + m], m == 0, m == 1)
                            last.then_inc(S("pv_mm"), 1)
                pe.wait_ge(*out_sem(f"pv{l}_1", 4))
                token_major(f"wo{l}", NT, KD, act_hi, act_lo)

            def mlp(l):
                for q in range(QUARTERS):
                    feature_major(f"up{l}_{q}", 8, act_hi, act_lo, T, ready=f"lnt{l}_1" if q == 0 else None)
                    token_major(f"down{l}_{q}", NT, KD, aux_hi, aux_lo, ready=(f"up{l}_{q}", "_lo"))

            pe.wait_ge(S("masks"), 1)
            for l in range(2):
                if l == 0:
                    pe.wait_ge(S("x_split"), 1)
                feature_major(f"in{l}", 22 if l == 0 else 29, act_hi, act_lo, T, ready="lnt0_2" if l else None)
                if l == 0:
                    pe.wait_ge(S("const_in"), 48)
                    rwkv()
                    lru()
                else:
                    pe.wait_ge(S("masks"), 2)
                    odd_mixer()
                pe.wait_ge(S("mix_split"), 1 + l)
                token_major(f"out{l}", NT, 8 if l == 0 else 12, act_hi, act_lo)
                attention(l)
                to_features(l, 1)
                mlp(l)
                if l == 0:
                    to_features(0, 2)

        @block.scalar
        def _(act):
            n_split = [0]
            n_step = [0]

            def step(ins):
                n_step[0] += 1
                ins.then_inc(S("act_step"), 1)
                act.wait_ge(S("act_step"), n_step[0])

            counts = {}

            def done(ins, name):
                counts[name] = counts.get(name, 0) + 1
                ins.then_inc(S(name), 1)
                act.wait_ge(S(name), counts[name])

            def split(upto):
                while n_split[0] < min(upto, N_CHUNKS):
                    c = n_split[0]
                    s = c % W_SLOTS
                    act.wait_ge(landed[s], 16 * (c // W_SLOTS + 1))
                    if c >= W_SLOTS:
                        act.wait_ge(S("chunk_done"), c - W_SLOTS + 1)
                    act.activation(w_hi[:, s], w_raw[:, s], ACT.Copy).then_inc(S("w_hi_done"), 1)
                    n_split[0] += 1

            def chunk(stg, i):
                c = FIRST[stg] + i
                split(c + W_SLOTS)
                act.wait_ge(S("chunk_done"), c + 1)

            def copy_hi(stg, i, dst, n=T):
                done(act.activation(dst, bank(stg, i)[:, 0:n], ACT.Copy), FAMILY[stg] + "_hi")

            act.wait_ge(S("x_in"), 16)
            done(act.activation(act_hi[:, 0:8], stage[:], ACT.Copy), "x_hi")
            for i in range(22):
                chunk("in0", i)
                done(act.activation(p0[:, i, PAD:PW], bank("in0", i)[:], ACT.Copy), "in_out")
            split(FIRST["out0"] + W_SLOTS)
            act.wait_ge(S("r_shift"), 1)
            step(act.activation(p0[0:64, 12, PAD:PW], p0[0:64, 12, PAD:PW], ACT.Tanh))
            done(act.activation(p0[:, 13, PAD:PW], p0[:, 13, PAD:PW], ACT.Sigmoid), "r_lora")
            act.wait_ge(S("rg_mm"), 4)
            for j in range(4):
                done(act.activation(gts[:, j], bank("rg", j)[:], ACT.Copy), "rg_out")
            for b in range(2):
                for j in range(2):
                    act.wait_ge(S("rlora_mm"), 4 * b + j + 1)
                    done(act.activation(ra[1][:, j], bank(f"rdec{b}", j)[:], ACT.Sigmoid, bias=V("w0", 2 * b + j)), "rdec_out")
                for j in range(2):
                    act.wait_ge(S("rlora_mm"), 4 * b + 2 + j + 1)
                    done(act.activation(ra[0][:, j], bank(f"ra{b}", j)[:], ACT.Sigmoid, bias=V("a0", 2 * b + j)), "ra_out")
                for j in range(2):
                    act.wait_ge(S("rss_mm"), 2 * b + j + 1)
                    done(act.activation(ra[5][:, j], bank(f"rss{b}", j)[:], ACT.Sqrt), "rss_out")
                act.wait_ge(S("r_cum"), b + 1)
                done(act.activation(ra[4][:], ra[8][:], ACT.Exp), "r_e")
                done(act.activation(ra[6][:], ra[2][:], ACT.Exp, scale=-1.0), "r_e")
                done(act.activation(ra[8][:], ra[2][:], ACT.Exp), "r_e")
                act.wait_ge(S("r_cend"), b + 1)
                done(act.activation(ra[9][:], ra[9][:], ACT.Exp), "r_e")
                for n in range(8):
                    act.wait_ge(S("rtok_mm"), 8 * b + n + 1)
                    dst = ra[12 + n // 2]
                    done(act.activation(dst[:, n % 2], bank(f"rtok{b}", n)[:], ACT.Copy), "rtok_out")
                for v in range(1, 6):
                    for j in range(2):
                        act.wait_ge(S("ryt_mm"), 10 * b + 2 * (v - 1) + j + 1)
                        done(act.activation(ra[6][:, j], bank(f"ryt{b}_{v}", j)[:], ACT.Copy), "ryt_out")
                for n in range(4):
                    act.wait_ge(S("rgw_mm"), 4 * b + n + 1)
                    dst = (ra[5], ra[0])[n % 2]
                    done(act.activation(dst[:, n // 2], bank(f"rgw{b}", n)[:], ACT.Copy), "rgw_out")
                for c in range(NRC):
                    act.wait_ge(S("rsa_mm"), 8 * b + c + 1)
                    done(act.activation(rsa[:, c % 2], bank(f"rsa{b}_{c}", 0)[:, 0:128].rearrange("p (j v) -> p j v", j=2),
                                   ACT.Copy), "rsa_out")
                    act.wait_ge(S("ro_mm"), 8 * b + c + 1)
                    done(act.activation(ra[7][:, :, c * RC:c * RC + RC],
                                   bank(f"ro{b}_{c}", 0)[:, 0:128].rearrange("p (j v) -> p j v", j=2),
                                   ACT.Copy), "ro_out")
                act.wait_ge(S("r_gvar"), b + 1)
                done(act.activation(small[:, 64:80], small[:, 48:64], ACT.Sqrt), "r_gstd")
            act.wait_ge(S("const_in"), 48)
            step(act.activation(small[:, 80:84], vec[:, VEC["lam"]:VEC["lam"] + 4], ACT.Exp, scale=-1.0))
            step(act.activation(small[:, 80:84], small[:, 80:84], ACT.Ln, bias=1.0))
            done(act.activation(small[:, 80:84], small[:, 80:84], ACT.Copy, scale=-8.0), "l_lam")
            for j in range(4):
                act.wait_ge(S("lru_mm"), 2 * j + 2)
                done(act.activation(lr[:, j], bank("lru", 2 * j)[:], ACT.Sigmoid, bias=V("lba", j)), "lru_out")
                done(act.activation(li[:, j], bank("lru", 2 * j + 1)[:], ACT.Sigmoid, bias=V("lbx", j)), "lru_out")
            act.wait_ge(S("l_loga"), 1)
            done(act.activation(lt[:], lr[:], ACT.Tanh), "l_tanh")
            act.wait_ge(S("l_tanh"), 1)
            done(act.activation(lr[:], lr[:], ACT.Exp), "l_tanh")
            act.wait_ge(S("l_var"), 1)
            done(act.activation(lt[:], lt[:], ACT.Sqrt), "l_sqrt")
            act.wait_ge(S("l_gin"), 1)
            done(act.activation(lt[:], lt[:], ACT.Tanh, scale=0.7978845608028654), "l_gtanh")
            act.wait_ge(S("mix_f"), 8)
            for i in range(8):
                done(act.activation(act_hi[:, i], p0[:, YT0[i], PAD:PW], ACT.Copy), "mix_hi")

            def ln_std(n):
                act.wait_ge(S("ln_var"), n + 1)
                done(act.activation(lnsd[:], lnsd[:], ACT.Sqrt), "ln_std")

            def feature_hi(l, which, k):
                stg = f"lnt{l}_{which}"
                c = 8 * (3 * l + which) + k
                act.wait_ge(*of(stg, "_mm", k + 1))
                done(act.activation(act_hi[:, k], bank(stg, k)[:], ACT.Identity, bias=V("lnb", c), scale=V("lng", c)),
                     "lnt_hi")

            def attention(l):
                act.wait_ge(S("mem_in"), 16 * (l + 1))
                memv = aux_hi[:].rearrange("p a t -> p (a t)")[:, 0:8 * MEM]
                done(act.activation(memv, stage[:].rearrange("p a t -> p (a t)")[:, 0:8 * MEM], ACT.Copy), "mem_hi")
                ln_std(3 * l)
                for i in range(8):
                    chunk(f"k{l}", i)
                    copy_hi(f"k{l}", i, k_hi[:, i], MEM)
                for half in range(2):
                    for i in range(4):
                        for k in range(4 * half + i + (half + i > 0), min(4 * half + i + 2, KD)):
                            feature_hi(l, 0, k)
                        chunk(f"v{l}", 4 * half + i)
                    for m in range(2):
                        copy_hi(f"v{l}", 2 * half + m, v_hi[:, m, half * HALF:half * HALF + HALF])
                for i in range(8):
                    chunk(f"q{l}", i)
                    copy_hi(f"q{l}", i, aux_hi[:, i])
                split(FIRST[f"wo{l}"] + W_SLOTS)
                for n in range(8):
                    act.wait_ge(S("p_max"), 8 * l + n + 1)
                    for q in range(2):
                        ins = act.activation(stage[:, n, q * MEM:q * MEM + MEM], bank(f"s{l}", n)[:, q * MEM:q * MEM + MEM],
                                             ACT.Exp, bias=small[:, 128 + 2 * n + q:129 + 2 * n + q], scale=1.0 / 16,
                                             accum_out=small[:, 144 + 2 * n + q:145 + 2 * n + q])
                        if q == 0:
                            step(ins)
                        else:
                            done(ins, "s_out")
                for hp in range(2):
                    for t in range(NT):
                        act.wait_ge(*of(f"pt{l}_{hp}", "_mm", t + 1))
                        if hp and t == 0:
                            act.wait_ge(*of(f"pv{l}_0", "_mm", 4))
                        done(act.activation(act_hi[:, 8:12, t * P:t * P + P],
                                       bank(f"pt{l}_{hp}", t)[:].rearrange("p (a t) -> p a t", a=4), ACT.Copy), "pt_hi")
                    for n in range(4):
                        act.wait_ge(*of(f"pv{l}_{hp}", "_mm", n + 1))
                        done(act.activation(act_hi[:, 4 * hp + n], bank(f"pv{l}_{hp}", n)[:], ACT.Copy), "pv_hi")
                for i in range(8):
                    chunk(f"wo{l}", i)
                ln_std(3 * l + 1)
                for k in range(KD):
                    feature_hi(l, 1, k)

            def mlp(l):
                for q in range(QUARTERS):
                    for i in range(8):
                        chunk(f"up{l}_{q}", i)
                        n = 8 * q + i
                        done(act.activation(stage[:, n % 2], bank(f"up{l}_{q}", i)[:], ACT.Relu), "up_out")
                        act.wait_ge(*of(f"up{l}_{q}", "_sq", i + 1))
                        done(act.activation(aux_hi[:, i], stage[:, 2 + n % 2], ACT.Copy), "up_hi")
                    for i in range(8):
                        chunk(f"down{l}_{q}", i)
                ln_std(3 * l + 2)

            for i in range(8):
                chunk("out0", i)
            attention(0)
            mlp(0)
            for k in range(KD):
                feature_hi(0, 2, k)
            for i in range(29):
                chunk("in1", i)
                done(act.activation(p1[:, i, PAD:PW], bank("in1", i)[:], ACT.Copy), "in_out")
            split(FIRST["out1"] + W_SLOTS)
            done(act.activation(p1[:, 4:8, PAD:PW], p1[:, 4:8, PAD:PW], ACT.Sigmoid), "c_gate")
            act.wait_ge(S("c_var"), 1)
            done(act.activation(c_std, c_std, ACT.Sqrt), "c_stdd")
            for j in range(4):
                act.wait_ge(S("c_norm"), j + 1)
                done(act.activation(ctmp[:, j], cacc[:, j], ACT.Sigmoid), "c_sig")
            step(act.activation(p1[0:16, 28, PAD:PW], p1[0:16, 28, PAD:PW], ACT.Identity,
                                bias=vec[0:16, VEC["dtb"]:VEC["dtb"] + 1]))
            step(act.activation(sdt[:, 0], p1[0:16, 28, PAD:PW], ACT.Abs))
            step(act.activation(sdt[:, 0], sdt[:, 0], ACT.Exp, scale=-1.0))
            step(act.activation(small[0:16, 200:201], vec[0:16, VEC["alog"]:VEC["alog"] + 1], ACT.Exp))
            done(act.activation(sdt[:, 0], sdt[:, 0], ACT.Ln, bias=1.0), "s_sp")
            for i in range(12):
                act.wait_ge(S("s_cv"), i + 1)
                done(act.activation(cacc[:, i % 4], sconv[:, i % 2], ACT.Sigmoid), "s_sig")
            act.wait_ge(S("s_z0"), 1)
            for hp in range(4):
                done(act.activation(p1[:, 4 + hp, PAD:PW], p1[:, 8 + hp, PAD:PW], ACT.Sigmoid), "s_zsig")
            act.wait_ge(S("slast_mm"), 1)
            done(act.activation(stm[:, 3], bank("slast", 0)[:, 0:64].rearrange("p (c h) -> p c h", c=NSC), ACT.Copy), "slast_out")
            act.wait_ge(S("s_dte"), 1)
            step(act.activation(stm[:, 2], stm[:, 2], ACT.Exp))
            done(act.activation(stm[:, 3], stm[:, 3], ACT.Exp), "s_dtee")
            for q in range(2):
                act.wait_ge(S("sbt_mm"), q + 1)
                done(act.activation(bt[:, 2 * q:2 * q + 2].rearrange("p c n -> p (c n)"), bank("sbt", q)[:], ACT.Copy), "sbt_out")
            for n in range(16):
                if n >= 8 and n % 2 == 0:
                    hp = n // 2
                    act.wait_ge(S("s_ysq"), hp - 3)
                    done(act.activation(p1[:, 4 + hp % 4, PAD:PW], p1[:, 8 + hp, PAD:PW], ACT.Sigmoid), "s_zsig")
                act.wait_ge(S("s_diff"), n + 1)
                if n >= 2:
                    act.wait_ge(S("sy_mm"), (n - 2) // 2 + 1)
                done(act.activation(cs[:, n % 2], bank(f"sbc{n // 2}", n % 2)[:], ACT.Exp), "sbc_out")
                done(act.activation(mt[:, n % 2], mt[:, n % 2], ACT.Exp), "s_exp")
            for g in range(2):
                act.wait_ge(S("srms_v"), g + 1)
                done(act.activation(p1[:, 24 + g, PAD:PW], p1[:, 24 + g, PAD:PW], ACT.Sqrt), "s_rstd")
            act.wait_ge(S("mix_f1"), 12)
            for i in range(12):
                done(act.activation(act_hi[:, i], p1[:, YT1[i], PAD:PW], ACT.Copy), "mix_hi")
            for i in range(12):
                chunk("out1", i)
            attention(1)
            mlp(1)

        @block.vector
        def _(dve):
            n_split = [0]
            n_step = [0]

            def step(ins):
                n_step[0] += 1
                ins.then_inc(S("dve_step"), 1)
                dve.wait_ge(S("dve_step"), n_step[0])

            counts = {}

            def done(ins, name):
                counts[name] = counts.get(name, 0) + 1
                ins.then_inc(S(name), 1)
                dve.wait_ge(S(name), counts[name])

            def f(ap):
                return ap.bitcast(F32)

            def split(upto):
                while n_split[0] < min(upto, N_CHUNKS):
                    c = n_split[0]
                    s = c % W_SLOTS
                    dve.wait_ge(S("w_hi_done"), c + 1)
                    dve.tensor_tensor(w_lo[:, s], w_raw[:, s], f(w_hi[:, s]), ALU.subtract).then_inc(S("w_split"), 1)
                    n_split[0] += 1

            def chunk(stg, i):
                c = FIRST[stg] + i
                split(c + W_SLOTS)
                dve.wait_ge(S("chunk_done"), c + 1)

            def tt(o, a, b_, op):
                return dve.tensor_tensor(o, a, b_, op)

            def stt(o, a, s, b_, op0, op1):
                return dve.scalar_tensor_tensor(out=o, in0=a, scalar=s, in1=b_, op0=op0, op1=op1)

            MUL, ADD, SUB = ALU.mult, ALU.add, ALU.subtract

            dve.wait_ge(S("x_hi"), 1)
            dve.wait_ge(S("x_in"), 16)
            tt(act_lo[:, 0:8], stage[:], f(act_hi[:, 0:8]), SUB).then_inc(S("x_split"), 1)
            dve.wait_ge(S("x_split"), 1)
            step(dve.memset(p0[:, :, 0:PAD], 0.0))
            for i in range(22):
                split(FIRST["in0"] + i + W_SLOTS)
            split(FIRST["out0"] + W_SLOTS)
            dve.wait_ge(S("const_in"), 48)
            dve.wait_ge(S("masks"), 1)

            def shift(i, tmp):
                step(tt(tmp, p0[:, i, PAD - 1:PW - 1], p0[:, i, PAD:PW], SUB))
                return stt(p0[:, i, PAD:PW], tmp, V("mu", i), p0[:, i, PAD:PW], MUL, ADD)

            dve.wait_ge(*out_sem("in0", 22))
            dve.wait_ge(S("chunk_done"), FIRST["in0"] + 22)
            step(shift(12, ra[8][:, 0]))
            done(shift(13, ra[8][:, 1]), "r_shift")
            step(dve.tensor_scalar(small[:, 84:88], vec[:, VEC["ka"]:VEC["ka"] + 4], -1.0, 1.0, MUL, ADD))

            def rwkv(b):
                r_, k_, v_ = (p0[:, 4 * m + 2 * b:4 * m + 2 * b + 2, PAD:PW] for m in range(3))
                for m in range(3):
                    for j in range(2):
                        step(shift(4 * m + 2 * b + j, ra[8][:, j]))
                for j in range(2):
                    step(dve.tensor_scalar(ra[3][:, j], k_[:, j], V("kk", 2 * b + j), None, MUL))
                done(tt(ra[4][:], ra[3][:], ra[3][:], MUL), "r_kksq")
                dve.wait_ge(S("rdec_out"), 2 * b + 2)
                step(dve.tensor_scalar(ra[1][:], ra[1][:], NEG_EXP_HALF, None, MUL))
                for j in range(2):
                    step(dve.tensor_tensor_scan(ra[2][:, j], m_scan[:], ra[1][:, j], 0.0, MUL, ADD))
                dve.wait_ge(S("rss_out"), 2 * b + 2)
                step(dve.tensor_scalar(ra[5][:], ra[5][:], 1e-12, None, ALU.max))
                step(dve.reciprocal(ra[5][:], ra[5][:]))
                step(tt(ra[3][:], ra[3][:], ra[5][:], MUL))
                done(tt(ra[8][:], ra[2][:], ra[1][:], SUB), "r_cum")
                dve.wait_ge(S("ra_out"), 2 * b + 2)
                for j in range(2):
                    step(dve.tensor_scalar(ra[1][:, j], ra[0][:, j], V("ka", 2 * b + j),
                                           small[:, 84 + 2 * b + j:85 + 2 * b + j], MUL, ADD))
                step(tt(k_, k_, ra[1][:], MUL))
                step(tt(ra[1][:], r_, k_, MUL))
                for j in range(2):
                    ins = dve.tensor_scalar(ra[5][:, j], ra[1][:, j], V("rk", 2 * b + j), None, MUL)
                    if j:
                        done(ins, "r_rkr")
                    else:
                        step(ins)
                cum = ra[2][:].rearrange("p j (c t) -> p (j c) t", t=RC)
                ends = small[:, 88:104]
                step(dve.tensor_copy(ends, cum[:, :, RC - 1]))
                done(tt(ra[9][:].rearrange("p j (c t) -> p (j c) t", t=RC), bc(ends, RC), cum, SUB), "r_cend")
                dve.wait_ge(S("r_e"), 4 * b + 4)
                step(tt(ra[4][:], ra[4][:], ra[3][:], MUL))
                step(stt(ra[3][:], ra[3][:], -1.0, ra[0][:], MUL, MUL))
                step(tt(ra[7][:], k_, ra[6][:], MUL))
                step(tt(ra[6][:], ra[3][:], ra[6][:], MUL))
                step(tt(r_, r_, ra[8][:], MUL))
                step(dve.tensor_copy(small[:, 104:120], ra[8][:].rearrange("p j (c t) -> p (j c) t", t=RC)[:, :, RC - 1]))
                step(tt(ra[3][:], ra[3][:], ra[9][:], MUL))
                done(tt(k_, k_, ra[9][:], MUL), "r_ops")
                for j in range(2):
                    dve.wait_ge(S("rbon_mm"), 2 * b + j + 1)
                    done(tt(ra[16][:, j], bank(f"rbon{b}", j)[:], v_[:, j], MUL), "rbon_out")
                M, PAK, PRB, PRK = ra[17], ra[9], ra[10], ra[11]
                X, XT, YT, MO = ra[1], ra[2], ra[6], ra[7]

                def three(ap):
                    return ap.rearrange("p (c t) -> p c t", t=RC)

                for n, (dst, mask) in enumerate([(M, None), (XT, m_lev[:, 6]), (PAK, m_strict[:]), (PRB, m_incl[:]),
                                                 (PRK, m_incl[:])]):
                    for j in range(2):
                        dve.wait_ge(S("rprod_mm"), 10 * b + 2 * n + j + 1)
                        src = bank(f"rprod{b}", 2 * n + j)[:]
                        if mask is None:
                            done(dve.tensor_copy(dst[:, j], src), "rprod_out")
                        else:
                            done(tt(three(dst[:, j]), three(src), mid(mask, NRC), MUL), "rprod_out")
                for j in range(2):
                    done(tt(three(XT[:, j]), three(XT[:, j]), mid(eye2[:], NRC), ADD), "r_xt0")
                    step(tt(three(X[:, j]), three(M[:, j]), mid(m_lev[:, 0], NRC), MUL))
                    step(tt(three(X[:, j]), three(X[:, j]), mid(eye2[:], NRC), ADD))
                zn = 0
                for v in range(1, 6):
                    if v > 1:
                        dve.wait_ge(S("ryt_mm"), 10 * b + 2 * (v - 1))
                    for j in range(2):
                        ins = tt(three(MO[:, j]), three(M[:, j]), mid(m_lev[:, v], NRC), MUL)
                        if j:
                            done(ins, "r_moff")
                        else:
                            step(ins)
                    for j in range(2):
                        if v < 5:
                            dve.wait_ge(S("rz_mm"), 18 * b + zn + 2)
                            done(tt(X[:, j], X[:, j], bank(f"rz{b}_{v}", 2 * j)[:], ADD), "rz_out")
                            zn += 2
                            done(tt(XT[:, j], XT[:, j], bank(f"rz{b}_{v}", 2 * j + 1)[:], ADD), "rz_out")
                        else:
                            dve.wait_ge(S("rz_mm"), 18 * b + zn + 1)
                            zn += 1
                            done(tt(XT[:, j], XT[:, j], bank(f"rz{b}_{v}", j)[:], ADD), "rz_out")
                for c in range(NRC):
                    dve.wait_ge(S("rst_mm"), 8 * b + c + 1)
                    if c:
                        dve.wait_ge(S("ro_mm"), 8 * b + c)
                    src = bank(f"rst{b}_{c}", 0)
                    for j in range(2):
                        if c == 0:
                            ins = dve.tensor_copy(rh[:, 1, j], src[:, j * RD:j * RD + RD])
                        else:
                            ins = stt(rh[:, (c + 1) % 2, j], rh[:, c % 2, j],
                                      small[:, 104 + 8 * j + c:105 + 8 * j + c], src[:, j * RD:j * RD + RD], MUL, ADD)
                        if j:
                            done(ins, "rst_out")
                        else:
                            step(ins)
                dve.wait_ge(S("ro_out"), 8 * b + 8)
                O = ra[7][:].rearrange("p j (c v) -> p (j c) v", v=RD)
                Q = ra[12][:].rearrange("p j (c v) -> p (j c) v", v=RD)
                Z = ra[6][:].rearrange("p j (c v) -> p (j c) v", v=RD)
                mean, var = small[:, 32:48], small[:, 48:64]
                step(dve.tensor_reduce(mean, O, AX_X, ADD))
                step(dve.tensor_scalar(mean, mean, 1.0 / RD, None, MUL))
                step(tt(O, O, bc(mean, RD), SUB))
                step(tt(Z, O, O, MUL))
                step(dve.tensor_reduce(var, Z, AX_X, ADD))
                done(dve.tensor_scalar(var, var, 1.0 / RD, GN_EPS, MUL, ADD), "r_gvar")
                dve.wait_ge(S("r_gstd"), b + 1)
                step(dve.reciprocal(small[:, 64:80], small[:, 64:80]))
                done(tt(Q, O, bc(small[:, 64:80], RD), MUL), "r_gn")
                for j in range(2):
                    jj = 2 * b + j
                    dve.wait_ge(S("rback_mm"), 2 * b + j + 1)
                    done(dve.tensor_scalar(ra[6][:, j], bank(f"rback{b}", j)[:], V("gng", jj), V("gnb", jj), MUL, ADD),
                         "rback_out")
                    step(tt(ra[6][:, j], ra[6][:, j], ra[16][:, j], ADD))
                    done(tt(p0[:, YT0[jj], PAD:PW], ra[6][:, j], gts[:, jj], MUL), "mix_f")

            dve.wait_ge(S("rg_out"), 4)
            for b in range(2):
                rwkv(b)

            for j in range(4):
                x_ = p0[:, 14 + j]
                step(dve.tensor_scalar(act_like[:, j], x_[:, 1:1 + T], V("lcw", j), V("lcb", j), MUL, ADD))
                for k in range(1, 4):
                    ins = stt(act_like[:, j], x_[:, 1 + k:1 + k + T], V("lcw", 4 * k + j), act_like[:, j], MUL, ADD)
                    if k < 3:
                        step(ins)
                    else:
                        done(ins, "l_conv")
            dve.wait_ge(S("l_lam"), 1)
            dve.wait_ge(S("lru_out"), 8)
            for j in range(4):
                ins = dve.tensor_scalar(lr[:, j], lr[:, j], small[:, 80 + j:81 + j], None, MUL)
                if j == 3:
                    done(ins, "l_loga")
                else:
                    step(ins)
            dve.wait_ge(S("l_tanh"), 2)
            step(dve.tensor_scalar(lq[:], lt[:], -1.0, 1.0, MUL, ADD))
            step(dve.reciprocal(lq[:], lq[:]))
            done(stt(lt[:], lt[:], -2.0, lq[:], MUL, MUL), "l_var")
            step(tt(li[:], li[:], act_like[:], MUL))
            dve.wait_ge(S("l_sqrt"), 1)
            step(tt(li[:], li[:], lt[:], MUL))
            for j in range(4):
                step(dve.tensor_tensor_scan(lq[:, j], lr[:, j], li[:, j], 0.0, MUL, ADD))
            g_ = p0[:, 18:22, PAD:PW]
            step(tt(lt[:], g_, g_, MUL))
            step(dve.tensor_scalar(lt[:], lt[:], 0.044715, 1.0, MUL, ADD))
            done(tt(lt[:], lt[:], g_, MUL), "l_gin")
            dve.wait_ge(S("l_gtanh"), 1)
            step(dve.tensor_scalar(lt[:], lt[:], 1.0, 0.5, ADD, MUL))
            step(tt(lt[:], lt[:], g_, MUL))
            for j in range(4):
                done(tt(p0[:, YT0[4 + j], PAD:PW], lt[:, j], lq[:, j], MUL), "mix_f")
            dve.wait_ge(S("mix_hi"), 8)
            for i in range(8):
                ins = tt(act_lo[:, i], p0[:, YT0[i], PAD:PW], f(act_hi[:, i]), SUB)
                if i == 7:
                    done(ins, "mix_split")
                else:
                    step(ins)
            step(dve.tensor_copy(small[:, 255:256], small[:, 254:255]))
            done(dve.tensor_copy(small[:, 255:256], small[:, 254:255]), "mix_done")

            def residual(stg, half, first, final):
                cols = slice(half * HALF, half * HALF + HALF)
                for t in range(NT):
                    if first:
                        ins = stt(h[:, t, cols], h[:, t, cols], ALPHA, bank(stg, half * NT + t)[:], MUL, ADD)
                    else:
                        ins = tt(h[:, t, cols], h[:, t, cols], bank(stg, half * NT + t)[:], ADD)
                    done(ins, FAMILY[stg] + "_out")
                    if final:
                        step(dve.bn_stats(lnst[:, t, 6 * half:6 * half + 6], h[:, t, cols]))

            def layer_norm(n):
                for t in range(NT):
                    step(dve.bn_aggr(lnmv[:, t], lnst[:, t]))
                done(dve.tensor_scalar(lnsd[:], lnmv[:, :, 1], LN_EPS, None, ADD), "ln_var")
                dve.wait_ge(S("ln_std"), n + 1)
                step(dve.reciprocal(lnsd[:], lnsd[:]))
                if n == 5:
                    dve.wait_ge(S("gb_in"), 16 * 6)
                for t in range(NT):
                    done(dve.tensor_scalar(h[:, t], h[:, t], lnmv[:, t, 0:1], lnsd[:, t:t + 1], SUB, MUL), "ln_rows")
                    if n == 5:
                        step(tt(h[:, t], h[:, t], gb[:, 0], MUL))
                        done(tt(h[:, t], h[:, t], gb[:, 1], ADD), "out_rows")

            def feature_lo(l, which, k):
                stg = f"lnt{l}_{which}"
                c = 8 * (3 * l + which) + k
                dve.wait_ge(*of(stg, "_hi", k + 1))
                tmp = stage[:, 6 + k % 2]
                step(dve.tensor_scalar(tmp, bank(stg, k)[:], V("lng", c), V("lnb", c), MUL, ADD))
                done(tt(act_lo[:, k], tmp, f(act_hi[:, k]), SUB), "lnt_out")

            def attention(l):
                dve.wait_ge(S("mem_hi"), l + 1)
                n8 = 8 * MEM
                done(tt(aux_lo[:].rearrange("p a t -> p (a t)")[:, 0:n8], stage[:].rearrange("p a t -> p (a t)")[:, 0:n8],
                        f(aux_hi[:].rearrange("p a t -> p (a t)")[:, 0:n8]), SUB), "mem_split")
                layer_norm(3 * l)
                for i in range(8):
                    chunk(f"k{l}", i)
                    dve.wait_ge(*of(f"k{l}", "_hi", i + 1))
                    done(tt(k_lo[:, i], bank(f"k{l}", i)[:, 0:MEM], f(k_hi[:, i]), SUB), "k_out")
                for half in range(2):
                    for i in range(4):
                        for k in range(4 * half + i + (half + i > 0), min(4 * half + i + 2, KD)):
                            feature_lo(l, 0, k)
                        chunk(f"v{l}", 4 * half + i)
                    for m in range(2):
                        cols = slice(half * HALF, half * HALF + HALF)
                        dve.wait_ge(*of(f"v{l}", "_hi", 2 * half + m + 1))
                        done(tt(v_lo[:, m, cols], bank(f"v{l}", 2 * half + m)[:], f(v_hi[:, m, cols]), SUB), "v_out")
                for i in range(8):
                    chunk(f"q{l}", i)
                    dve.wait_ge(*of(f"q{l}", "_hi", i + 1))
                    done(tt(aux_lo[:, i], bank(f"q{l}", i)[:], f(aux_hi[:, i]), SUB), "q_out")
                split(FIRST[f"wo{l}"] + W_SLOTS)

                def row_max(n):
                    dve.wait_ge(*of(f"s{l}", "_mm", n + 1))
                    step(dve.tensor_reduce(small[:, 160 + 2 * n:162 + 2 * n],
                                           bank(f"s{l}", n)[:].rearrange("p (q m) -> p q m", q=2), AX_X, ALU.max))
                    done(dve.tensor_scalar(small[:, 128 + 2 * n:130 + 2 * n], small[:, 160 + 2 * n:162 + 2 * n],
                                           -1.0 / 16, None, MUL), "p_max")

                def probs(n):
                    dve.wait_ge(*of(f"s{l}", "_out", n + 1))
                    step(dve.reciprocal(small[:, 176 + 2 * n:178 + 2 * n], small[:, 144 + 2 * n:146 + 2 * n]))
                    for q in range(2):
                        pr = stage[:, n, q * MEM:q * MEM + MEM]
                        ins = dve.tensor_scalar(pr, pr, small[:, 176 + 2 * n + q:177 + 2 * n + q], None, MUL)
                        if q:
                            done(ins, "p_ready")
                        else:
                            step(ins)

                for n in range(9):
                    if n < 8:
                        row_max(n)
                    if n:
                        probs(n - 1)
                for hp in range(2):
                    for t in range(NT):
                        dve.wait_ge(*of(f"pt{l}_{hp}", "_hi", t + 1))
                        dst = slice(t * P, t * P + P)
                        ins = tt(act_lo[:, 8:12, dst], bank(f"pt{l}_{hp}", t)[:].rearrange("p (a t) -> p a t", a=4),
                                 f(act_hi[:, 8:12, dst]), SUB)
                        done(ins, "pt_out")
                    for n in range(4):
                        dve.wait_ge(*of(f"pv{l}_{hp}", "_hi", n + 1))
                        i = 4 * hp + n
                        done(tt(act_lo[:, i], bank(f"pv{l}_{hp}", n)[:], f(act_hi[:, i]), SUB), "pv_out")
                dve.wait_ge(S("h_ready"), NT * (3 * l + 1))
                for half in range(2):
                    for i in range(4):
                        chunk(f"wo{l}", 4 * half + i)
                    residual(f"wo{l}", half, True, True)
                layer_norm(3 * l + 1)
                for k in range(KD):
                    feature_lo(l, 1, k)

            def mlp(l):
                for q in range(QUARTERS):
                    for i in range(8):
                        chunk(f"up{l}_{q}", i)
                        n = 8 * q + i
                        dve.wait_ge(*of(f"up{l}_{q}", "_out", i + 1))
                        done(tt(stage[:, 2 + n % 2], stage[:, n % 2], stage[:, n % 2], MUL), "up_sq")
                        dve.wait_ge(*of(f"up{l}_{q}", "_hi", i + 1))
                        done(tt(aux_lo[:, i], stage[:, 2 + n % 2], f(aux_hi[:, i]), SUB), "up_lo")
                    for half in range(2):
                        for i in range(4):
                            chunk(f"down{l}_{q}", 4 * half + i)
                        if q == 0 and half == 0:
                            dve.wait_ge(S("h_ready"), NT * (3 * l + 2))
                        residual(f"down{l}_{q}", half, q == 0, q == QUARTERS - 1)
                layer_norm(3 * l + 2)

            dve.wait_ge(S("h_in"), 16)
            for half in range(2):
                for i in range(4):
                    chunk("out0", 4 * half + i)
                residual("out0", half, True, True)
            attention(0)
            mlp(0)
            for k in range(KD):
                feature_lo(0, 2, k)
            for i in range(29):
                split(FIRST["in1"] + i + W_SLOTS)
            split(FIRST["out1"] + W_SLOTS)
            dve.wait_ge(*out_sem("in1", 29))
            dve.wait_ge(S("chunk_done"), FIRST["in1"] + 29)
            dve.wait_ge(S("masks"), 2)

            step(dve.memset(p1[:, :, 0:PAD], 0.0))
            step(dve.memset(cu[:, :, 0:CP], 0.0))
            dve.wait_ge(S("c_gate"), 1)
            step(tt(cu[:, :, CP:CP + T], p1[:, 0:4, PAD:PW], p1[:, 4:8, PAD:PW], MUL))
            for k in range(CONF_TAPS):
                for j in range(4):
                    src = cu[:, j, CP - (CONF_TAPS - 1) + k:CP - (CONF_TAPS - 1) + k + T]
                    w_ = V("ccw", 4 * k + j)
                    if k == 0:
                        ins = dve.tensor_scalar(cacc[:, j], src, w_, V("ccb", j), MUL, ADD)
                    else:
                        ins = stt(cacc[:, j], src, w_, cacc[:, j], MUL, ADD)
                    if k == CONF_TAPS - 1:
                        done(ins, "c_conv")
                    else:
                        step(ins)
            cmean = p1[:, 0, PAD:PW]
            dve.wait_ge(S("c_mm"), 1)
            done(dve.tensor_scalar(cmean, bank("cmean", 0)[:], 1.0 / 512, None, MUL), "cmean_out")
            for j in range(4):
                step(tt(cacc[:, j], cacc[:, j], cmean, SUB))
            done(tt(ctmp[:], cacc[:], cacc[:], MUL), "c_sq")
            dve.wait_ge(S("c_mm"), 2)
            done(dve.tensor_scalar(c_std, bank("cvar", 0)[:], 1.0 / 512, LN_EPS, MUL, ADD), "cvar_out")
            done(dve.tensor_copy(small[:, 255:256], small[:, 254:255]), "c_var")
            dve.wait_ge(S("c_stdd"), 1)
            step(dve.reciprocal(c_std, c_std))
            for j in range(4):
                step(tt(cacc[:, j], cacc[:, j], c_std, MUL))
                done(dve.tensor_scalar(cacc[:, j], cacc[:, j], V("clg", j), V("clb", j), MUL, ADD), "c_norm")
            for j in range(4):
                dve.wait_ge(S("c_sig"), j + 1)
                done(tt(p1[:, YT1[j], PAD:PW], cacc[:, j], ctmp[:, j], MUL), "mix_f1")
            for i in range(12):
                x_ = p1[:, 16 + i]
                d_ = sconv[:, i % 2]
                step(dve.tensor_scalar(d_, x_[:, 1:1 + T], V("scw", i), V("scb", i), MUL, ADD))
                for k in range(1, 4):
                    ins = stt(d_, x_[:, 1 + k:1 + k + T], V("scw", 12 * k + i), d_, MUL, ADD)
                    if k < 3:
                        step(ins)
                    else:
                        done(ins, "s_cv")
                dve.wait_ge(S("s_sig"), i + 1)
                done(tt(x_[:, PAD:PW], d_, cacc[:, i % 4], MUL), "s_conv")
            dve.wait_ge(S("s_sp"), 1)
            step(stt(sdt[:, 0], p1[0:16, 28, PAD:PW], 0.0, sdt[:, 0], ALU.max, ADD))
            step(dve.tensor_scalar(p1[0:16, 28, PAD:PW], sdt[:, 0], small[0:16, 200:201], -1.0, MUL, MUL))
            done(dve.tensor_tensor_scan(sdt[:, 1], m_scan[0:16], p1[0:16, 28, PAD:PW], 0.0, MUL, ADD), "s_acum")
            for m in range(2):
                dve.wait_ge(S("stok_mm"), m + 1)
                done(dve.tensor_copy(stm[:, m].rearrange("p c h -> p (c h)"), bank("stok", m)[:, 0:64]), "stok_out")
            done(dve.tensor_copy(small[:, 255:256], small[:, 254:255]), "s_z0")
            dve.wait_ge(S("slast_out"), 1)
            done(tt(stm[:, 2], stm[:, 3], stm[:, 1], SUB), "s_dte")
            dve.wait_ge(S("s_dtee"), 1)
            for c in range(NSC):
                for q in range(2):
                    dve.wait_ge(S("sxt_mm"), 2 * c + q + 1)
                    dst = xdt[:, c, q * 512:q * 512 + 512].rearrange("p (h v) -> p h v", v=64)
                    done(tt(dst, bank("sxt", 2 * c + q)[:].rearrange("p (h v) -> p h v", v=64),
                            bc(stm[:, 0, c, 8 * q:8 * q + 8], 64), MUL), "sxt_x")
                    done(tt(xdtd[:, c, q * 512:q * 512 + 512].rearrange("p (h v) -> p h v", v=64), dst,
                            bc(stm[:, 2, c, 8 * q:8 * q + 8], 64), MUL), "sxt_out")
            for g in range(2):
                dve.wait_ge(S("scb_mm"), g + 1)
                done(tt(cbt[:, :, g], bank("scb", g)[:].rearrange("p (c t) -> p c t", c=NSC), mid(m_tri[:], NSC), MUL),
                     "scb_out")
            for c in range(NSC - 1):
                for g in range(2):
                    dve.wait_ge(S("sst_mm"), 2 * c + g + 1)
                    nxt = prev[:, c + 1, g * 512:g * 512 + 512].rearrange("p (h v) -> p h v", v=64)
                    src = bank("sst", 2 * c + g)[:].rearrange("p (h v) -> p h v", v=64)
                    if c == 0:
                        done(dve.tensor_copy(nxt, src), "sst_out")
                    else:
                        cur = prev[:, c, g * 512:g * 512 + 512].rearrange("p (h v) -> p h v", v=64)
                        step(tt(nxt, cur, bc(stm[:, 3, c, 8 * g:8 * g + 8], 64), MUL))
                        done(tt(nxt, nxt, src, ADD), "sst_out")
            for hp in range(8):
                g = hp // 4
                for q in range(2):
                    n = 2 * hp + q
                    dve.wait_ge(S("sbc_mm"), n + 1)
                    if n >= 2:
                        dve.wait_ge(S("sy_mm"), (n - 2) // 2 + 1)
                    for c in range(NSC):
                        cols = slice(c * SC, c * SC + SC)
                        ins = dve.tensor_scalar(mt[:, q, cols], bank(f"sbc{hp}", q)[:, cols], stm[:, 1, c, n:n + 1], 0.0,
                                                SUB, ALU.min)
                        if c < NSC - 1:
                            step(ins)
                        else:
                            done(ins, "s_diff")
                    dve.wait_ge(S("s_exp"), n + 1)
                    step(tt(cs[:, q], cs[:, q], p1[:, 26 + g, PAD:PW], MUL))
                    done(tt(mt[:, q].rearrange("p (c t) -> p c t", c=NSC), mt[:, q].rearrange("p (c t) -> p c t", c=NSC),
                            cbt[:, :, g], MUL), "s_mt")
                dve.wait_ge(S("sy_mm"), hp + 1)
                xs = p1[:, 16 + hp, PAD:PW]
                z_ = p1[:, 8 + hp, PAD:PW]
                done(stt(xs, xs, V("dsk", hp), bank(f"sy{hp}", 0)[:], MUL, ADD), "sy_out")
                step(tt(xs, xs, z_, MUL))
                dve.wait_ge(S("s_zsig"), hp + 1)
                step(tt(z_, xs, p1[:, 4 + hp % 4, PAD:PW], MUL))
                done(tt(xs, z_, z_, MUL), "s_ysq")
            for g in range(2):
                dve.wait_ge(S("srms_mm"), g + 1)
                done(dve.tensor_scalar(p1[:, 24 + g, PAD:PW], bank("srms", g)[:], 1.0 / 512, LN_EPS, MUL, ADD), "srms_out")
                done(dve.tensor_copy(small[:, 255:256], small[:, 254:255]), "srms_v")
            for g in range(2):
                dve.wait_ge(S("s_rstd"), g + 1)
                step(dve.reciprocal(p1[:, 24 + g, PAD:PW], p1[:, 24 + g, PAD:PW]))
                for j in range(4):
                    i = 4 * g + j
                    z_ = p1[:, 8 + i, PAD:PW]
                    done(stt(z_, z_, V("sng", i), p1[:, 24 + g, PAD:PW], MUL, MUL), "mix_f1")
            dve.wait_ge(S("mix_hi"), 20)
            for i in range(12):
                ins = tt(act_lo[:, i], p1[:, YT1[i], PAD:PW], f(act_hi[:, i]), SUB)
                if i == 11:
                    done(ins, "mix_split")
                else:
                    step(ins)
            done(dve.tensor_copy(small[:, 255:256], small[:, 254:255]), "mix_done")
            for half in range(2):
                for i in range(6):
                    chunk("out1", 6 * half + i)
                if half == 0:
                    dve.wait_ge(S("h_ready"), NT * 3)
                residual("out1", half, True, True)
            attention(1)
            mlp(1)


_OUT = (1, T, D)


def kernel(**inputs):
    import numpy as _np
    import concourse.bacc as _bacc
    from concourse import mybir as _mybir
    from concourse.bass_utils import run_bass_kernel_spmd as _run

    a = {k: _np.asarray(v) for k, v in inputs.items()}

    def by_feature(w):
        k, m = w.shape
        return w.reshape(k // P, P, m // P, P).transpose(2, 1, 0, 3).reshape(m // P, P, CHUNK)

    def by_token(w):
        k, _ = w.shape
        return w.reshape(k // 256, 2, P, 2, HALF).transpose(3, 0, 2, 1, 4).reshape(k // P, P, CHUNK)

    def padded(w, rows, cols):
        z = _np.zeros((rows, cols), w.dtype)
        z[:w.shape[0], :w.shape[1]] = w
        return z

    stream = []
    for l in range(2):
        if l == 0:
            stream += [by_feature(a["ev_w_in"][0]), by_token(a["ev_w_out"][0])]
        else:
            stream += [by_feature(padded(a["od_w_in"][0], D, 29 * P)), by_token(a["od_w_out"][0])]
        stream += [by_feature(a["xa_wk"][l]), by_token(a["xa_wv"][l]), by_feature(a["xa_wq"][l]),
                   by_token(a["xa_wo"][l])]
        for q in range(QUARTERS):
            cut = slice(q * D, q * D + D)
            stream += [by_feature(a["ffn_w1"][l][:, cut]), by_token(a["ffn_w2"][l][cut])]

    def tiles(v):
        v = v.reshape(-1, v.shape[-1])
        return v.reshape(v.shape[0] * v.shape[1] // P, P).T

    vecs = {"mu": a["ev_mu"], "w0": a["ev_w0"], "a0": a["ev_a0"], "kk": a["ev_k_k"], "ka": a["ev_k_a"],
            "rk": a["ev_r_k"].reshape(1, -1), "gng": a["ev_gn_g"], "gnb": a["ev_gn_b"],
            "lcw": a["ev_lru_conv_w"][0], "lcb": a["ev_lru_conv_b"], "lba": a["ev_lru_ba"], "lbx": a["ev_lru_bx"],
            "lam": a["ev_lru_lam"], "ccw": a["od_cf_conv_w"][0], "ccb": a["od_cf_conv_b"],
            "clg": a["od_cf_ln_g"], "clb": a["od_cf_ln_b"], "scw": a["od_ssm_conv_w"][0],
            "lng": _np.concatenate([a[f"ln_{w}_g"][l] for l in range(2) for w in ("mix", "mem", "ffn")])[None],
            "lnb": _np.concatenate([a[f"ln_{w}_b"][l] for l in range(2) for w in ("mix", "mem", "ffn")])[None],
            "scb": a["od_ssm_conv_b"], "sng": a["od_ssm_norm_g"], "dsk": _np.repeat(a["od_d_skip"], 64, axis=1)}
    table = [tiles(vecs[n]) for n, _ in VEC_TILES[:-2]]
    table += [padded(a["od_dt_bias"].T, P, 1), padded(a["od_a_log"].T, P, 1)]
    lora = _np.stack([_np.concatenate([a["ev_w2"][0], a["ev_a2"][0]]), a["ev_g2"][0]], axis=1)
    lru = _np.zeros((P, 8, P), _np.float32)
    for m, name in enumerate(["ev_lru_wa", "ev_lru_wx"]):
        for n in range(8):
            rows = slice(64 * (n % 2), 64 * (n % 2) + 64)
            lru[rows, 4 * m + n // 2, rows] = a[name][0, n]
    rows = [_np.stack([a[f"ln_{w}_g"][l], a[f"ln_{w}_b"][l]]) for l in range(2) for w in ("mix", "mem", "ffn")]
    x, mem = a["x"][0], a["mem"][0]
    arrays = {
        "x_tok": x.reshape(NT, P, D).transpose(1, 0, 2),
        "x_feat": x.T.reshape(KD, P, T).transpose(1, 0, 2),
        "mem_feat": mem.T.reshape(KD, P, MEM).transpose(1, 0, 2).reshape(P, KD * MEM),
        "weights": _np.concatenate(stream),
        "vectors": _np.concatenate(table, axis=1),
        "lora": lora,
        "lru_w": lru,
        "ln_rows": _np.stack(rows),
    }
    arrays = {k: _np.ascontiguousarray(v) for k, v in arrays.items()}
    nc = _bacc.Bacc("TRN2", target_bir_lowering=False, num_devices=1)
    args = [nc.dram_tensor(k, v.shape, _mybir.dt.float32, kind="ExternalInput").ap() for k, v in arrays.items()]
    out = nc.dram_tensor("out", _OUT, _mybir.dt.float32, kind="ExternalOutput").ap()
    build(nc, *args, out.rearrange("a (t p) d -> p (a t) d", p=P))
    r = _run(nc, [arrays], core_ids=[0])
    return r.results[0]["out"]
```

```python
from contextlib import ExitStack

import concourse.bass as bass
from concourse import mybir

F32 = mybir.dt.float32
F32R = mybir.dt.float32r
ALU = mybir.AluOpType
ACT = mybir.ActivationFunctionType
AX_X = mybir.AxisListType.X

P = 128
T = 512
D = 1024
KD = D // P
NT = T // P
MEM = 256
HALF = 512
CHUNK = 1024
W_SLOTS = 3
PAD = 4
PW = PAD + T
ALPHA = 4.0 ** 0.25
LN_EPS = 1e-5
GN_EPS = 64e-5
HEADS_XA = 4
D_FF = 4096
QUARTERS = 4
RC = 64
NRC = T // RC
RD = 64
SC = 128
NSC = T // SC
CONF_TAPS = 31
CP = 32
NEG_EXP_HALF = -0.6065306597126334

ORDER0 = [12, 13, 0, 1, 4, 5, 8, 9, 2, 3, 6, 7, 10, 11, 14, 15, 16, 17, 18, 19, 20, 21]
IN0 = [("in0_0", 2), ("in0_1", 4), ("in0_2", 4), ("in0_3", 2), ("in0_4", 2), ("in0_5", 4), ("in0_6", 4)]
PLACE0 = [(_name, _i) for _name, _count in IN0 for _i in range(_count)]

STREAM = []
for _l in range(2):
    STREAM += IN0 if _l == 0 else [("in1", 29)]
    STREAM += [(f"out{_l}", 8 if _l == 0 else 12),
               (f"k{_l}", 8), (f"v{_l}", 8), (f"q{_l}", 8), (f"wo{_l}", 8)]
    for _q in range(QUARTERS):
        STREAM += [(f"up{_l}_{_q}", 8), (f"down{_l}_{_q}", 8)]
FIRST = {}
_n = 0
for _name, _count in STREAM:
    FIRST[_name] = _n
    _n += _count
N_CHUNKS = _n

VEC_TILES = [("mu", 14), ("w0", 4), ("a0", 4), ("kk", 4), ("ka", 4), ("rk", 4), ("gng", 4), ("gnb", 4),
             ("lcw", 16), ("lcb", 4), ("lba", 4), ("lbx", 4), ("lam", 4),
             ("ccw", CONF_TAPS * 4), ("ccb", 4), ("clg", 4), ("clb", 4),
             ("scw", 48), ("scb", 12), ("sng", 8), ("dsk", 8), ("lng", 48), ("lnb", 48), ("dtb", 1), ("alog", 1)]
VEC = {}
_n = 0
for _name, _count in VEC_TILES:
    VEC[_name] = _n
    _n += _count
N_VEC = _n

TILES = []
for _l in range(2):
    if _l == 0:
        TILES += [IN0[0], IN0[1], ("rdec0", 2), ("ra0", 2), IN0[2], ("rss0", 2), IN0[3], ("rbon0", 2), IN0[4],
                  ("rdec1", 2), ("ra1", 2), IN0[5], IN0[6], ("rss1", 2), ("rprod0", 10), ("rtok0", 8), ("rw0", 2),
                  ("rbon1", 2), ("rprod1", 10), ("rtok1", 8), ("rw1", 2), ("lru", 8)]
        for _v in range(1, 6):
            TILES += [(f"ryt0_{_v}", 1), (f"ryt1_{_v}", 1)]
            TILES += [(f"rz0_{_v}", 2 if _v < 5 else 1), (f"rz1_{_v}", 2 if _v < 5 else 1)]
        TILES += [("rgt0", 2), ("rtw0", 2), ("rgt1", 2), ("rtw1", 2), ("rat0", 2), ("rrho0", 2), ("rat1", 2),
                  ("rrho1", 2)]
        for _c in range(NRC):
            TILES += [(f"rst{_c}", 1)] * (_c < NRC - 1) + [(f"ro{_c // 2}", 2)] * (_c % 2 == 0)
        TILES += [("rg", 4), ("rback", 4), ("out0", 8)]
    else:
        TILES += [("in1", 29), ("stok", 2), ("slast", 1), ("cmean", 1), ("sxt", 8), ("cvar", 1), ("sbt", 2),
                  ("scb", 2), ("sst", 6), ("sbc0", 2)]
        for _h in range(8):
            TILES += [(f"sbc{_h + 1}", 2)] * (_h < 7) + [(f"sy{_h}", 1)] + [("srms0", 1)] * (_h == 5)
        TILES += [("srms1", 1), ("out1", 8)]
    TILES += [(f"k{_l}", 8), (f"lnt{_l}_0", 8), (f"v{_l}", 4), (f"q{_l}", 8), (f"s{_l}", 8),
              (f"pt{_l}_0", 4), (f"pv{_l}_0", 4), (f"pt{_l}_1", 4), (f"pv{_l}_1", 4), (f"wo{_l}", 8),
              (f"lnt{_l}_1", 8)]
    for _q in range(QUARTERS):
        TILES += [(f"up{_l}_{_q}", 8), (f"down{_l}_{_q}", 8)]
    if _l == 0:
        TILES += [("lnt0_2", 8)]
TILE0 = {}
TILE_OWNER = []
for _name, _count in TILES:
    TILE0[_name] = len(TILE_OWNER)
    TILE_OWNER += [(_name, _i + 1) for _i in range(_count)]
FAMILY, BEFORE = {}, {}
_seen = {}
for _name, _count in TILES:
    _kind = _name.rstrip("0123456789_")
    FAMILY[_name] = _kind
    BEFORE[_name] = _seen.get(_kind, 0)
    _seen[_kind] = BEFORE[_name] + _count

GROUP = {"rdec": "rlora", "ra": "rlora", "rg": "rlora", "rgt": "rt", "rtw": "rt", "rat": "rt", "rrho": "rt",
         "cmean": "c", "cvar": "c"}
for _name in "rss rbon rprod rtok rw lru ryt rz rback stok slast sxt sbt scb sst sbc sy srms".split():
    GROUP[_name] = _name
MADE = {_kind: [] for _kind in GROUP.values()}
_n = 0
for _name, _i in TILE_OWNER:
    if FAMILY[_name] in GROUP:
        _n += 1
        MADE[GROUP[FAMILY[_name]]].append(_n)


def build(nc, x_tok, x_feat, mem_feat, weights, vectors, lora, lru_w, ln_rows, out):
    with ExitStack() as ctx:
        base = (nc.sbuf_base + 31) // 32 * 32
        place = {"at": base}

        def sb(name, shape, dt=F32, at=None):
            size = 4
            for n in shape[1:]:
                size *= n
            if at is None:
                at = place["at"]
                place["at"] = at + (size + 31) // 32 * 32
            return nc.alloc_sbuf_tensor_at(name, shape, dt, offset=at)

        w_raw = sb("w_raw", [P, W_SLOTS, CHUNK])
        w_hi = sb("w_hi", [P, W_SLOTS, CHUNK], F32R)
        w_lo = sb("w_lo", [P, W_SLOTS, CHUNK], F32R)
        h_at = place["at"]
        h = sb("h", [P, NT, D])
        act_at = place["at"]
        act_hi = sb("act_hi", [P, 12, T], F32R)
        act_lo = sb("act_lo", [P, 12, T], F32R)
        aux_at = place["at"]
        aux_hi = sb("aux_hi", [P, 8, T], F32R)
        aux_lo = sb("aux_lo", [P, 8, T], F32R)
        k_hi = sb("k_hi", [P, 8, MEM], F32R)
        k_lo = sb("k_lo", [P, 8, MEM], F32R)
        v_hi = sb("v_hi", [P, 2, D], F32R)
        v_lo = sb("v_lo", [P, 2, D], F32R)
        stage = sb("stage", [P, 8, T])
        mix_end = place["at"]
        gb_at = place["at"]
        gb = sb("gb", [P, 2, D])
        vec = sb("vec", [P, N_VEC])
        ident = sb("ident", [P, P])
        ones = sb("ones", [P, P])
        bdones = sb("bdones", [P, P])
        lastrow = sb("lastrow", [P, P])
        eye2 = sb("eye2", [P, RC])
        m_strict = sb("m_strict", [P, RC])
        m_incl = sb("m_incl", [P, RC])
        m_tri = sb("m_tri", [P, SC])
        m_lev = sb("m_lev", [P, 7, RC])
        m_scan = sb("m_scan", [P, T])
        small = sb("small", [P, 256])
        lnst = sb("lnst", [P, NT, 12])
        lnmv = sb("lnmv", [P, NT, 2])
        lnsd = sb("lnsd", [P, NT])
        omu = sb("omu", [P, 14])
        dend = sb("dend", [P, 2, 2, NRC])
        lora_at = place["at"]
        lora_sb = sb("lora_sb", [P, 2, T])
        lru_at = place["at"]
        lru_sb = sb("lru_sb", [P, 8, P])

        p0 = sb("p0", [P, 22, PW], at=aux_at)
        after_p0 = (aux_at + 22 * PW * 4 + 31) // 32 * 32

        def pair(name, region, i):
            return sb(name, [P, 2, T], at=region + i * 4096)

        ALPHA_ = [pair("alpha0", after_p0, 0), pair("alpha1", after_p0, 1)]
        NBH = [pair("nbh0", after_p0, 2), pair("nbh1", after_p0, 5)]
        KH = [pair("kh0", after_p0, 3), pair("kh1", after_p0, 6)]
        BON = [pair("bonus0", after_p0, 4), pair("bonus1", after_p0, 7)]
        NBT = [pair("nbt0", h_at, 0), pair("nbt1", h_at, 1)]
        M_ = [pair("m0", act_at, 0), pair("m1", act_at, 4)]
        XT_ = [pair("xt0", h_at, 2), pair("xt1", h_at, 3)]
        PAK = [pair("pak0", act_at, 1), pair("pak1", act_at, 5)]
        PRB = [pair("prb0", act_at, 6), pair("prb1", act_at, 10)]
        PRK = [pair("prk0", act_at, 7), pair("prk1", act_at, 11)]
        s_a, s_dec, s_cum, s_fwd, s_inv = XT_[1], M_[1], PAK[1], PRB[1], PRK[1]
        hall = sb("hall", [P, 4, T], at=act_at + 2 * 4096)
        oall = sb("oall", [P, 4, T], at=after_p0)
        zsq = KH[0]
        lc = sb("lc", [P, 4, T], at=gb_at)
        li = sb("li", [P, 4, T], at=act_at + 8 * 4096)
        lt = sb("lt", [P, T], at=after_p0 + 8 * 4096)
        assert after_p0 + 8 * 4096 + 2048 <= mix_end
        YT0 = [14, 15, 16, 17, 0, 1, 2, 3]

        def yt_(b, v):
            return hall[:, 2 * b:2 * b + 2] if v % 2 else KH[b][:]

        def rows_(c):
            return slice(RC * (c % 2), RC * (c % 2) + RC)

        def split_cols(j, c):
            at = j * 256 + (c // 2) * RC
            return slice(at, at + RC)

        def every_other(ap, s):
            return ap.rearrange("p j (m u) -> p j m u", u=P)[:, :, :, s * RC:s * RC + RC]

        def cols_(c, q):
            at = (c // 2) * P + q * RC
            return slice(at, at + RC)

        p1 = sb("p1", [P, 29, PW], at=aux_at)
        after_p1 = (aux_at + 29 * PW * 4 + 31) // 32 * 32
        cu = sb("cu", [P, 4, CP + T], at=after_p1)
        cacc = sb("cacc", [P, 4, T], at=after_p1 + 4 * (CP + T) * 4)
        sconv = sb("sconv", [P, 2, T], at=after_p1 + 4 * (CP + T) * 4 + 8192)
        pconv = sb("pconv", [P, 2, T], at=lru_at)
        gtmp = sb("gtmp", [P, 4, T], at=gb_at)
        sdt = sb("sdt", [16, 2, T], at=lora_at)
        c_std = sb("c_std", [P, T], at=lru_at)[:]
        DT, XS, BS, CS, ZS = 8, 9, 17, 19, 21
        YT1 = [0, 1, 2, 3] + [ZS + i for i in range(8)]
        xdt = sb("xdt", [P, NSC, D], at=act_at)
        xdtd = sb("xdtd", [P, NSC, D], at=act_at + 16384)
        prev = sb("prev", [P, NSC - 1, D], at=act_at + 36864)
        bt = sb("bt", [P, NSC, 256], at=after_p1)
        cbt = sb("cbt", [P, NSC, 2, SC], at=after_p1 + 4096)
        cs = sb("cs", [P, 4, T], at=after_p1 + 8192)
        mts = [sb("mt01", [P, 2, T], at=after_p1 + 16384), sb("mt23", [P, 2, T], at=act_at + 32768)]
        stm = sb("stm", [P, 4, NSC, 16])

        def mt(n):
            return mts[n % 4 // 2][:, n % 2]

        assert place["at"] <= nc.sbuf_usable_end and after_p1 + 20992 <= mix_end

        ps = [ctx.enter_context(nc.psum_tensor(f"bank{i}", [P, 512], F32)) for i in range(8)]

        sems = {}

        def S(name):
            if name not in sems:
                sems[name] = ctx.enter_context(nc.semaphore(name))
            return sems[name]

        def V(name, i):
            c = VEC[name] + i
            return vec[:, c:c + 1]

        def bank(stg, i):
            return ps[(TILE0[stg] + i) % 8]

        def of(stg, suffix, n):
            return S(FAMILY[stg] + suffix), BEFORE[stg] + n

        def made(kind, n):
            return S("mixer_mm"), MADE[kind][n - 1]

        def out_sem(stg, n):
            return of(stg, "_out", n)

        landed = [S(f"w_landed{i}") for i in range(W_SLOTS)]
        block = ctx.enter_context(nc.Block())

        def bc(ap, n):
            return ap.unsqueeze(2).to_broadcast([ap.shape[0], ap.shape[1], n])

        def mid(ap, n):
            return ap.unsqueeze(1).to_broadcast([ap.shape[0], n, ap.shape[1]])

        @block.sync
        def _(sp):
            sp.dma_start(stage[:], x_feat).then_inc(S("x_in"), 16)
            sp.dma_start(w_raw[:, 0], weights[0]).then_inc(landed[0], 16)
            sp.dma_start(vec[:], vectors).then_inc(S("const_in"), 16)
            sp.dma_start(w_raw[:, 1], weights[1]).then_inc(landed[1], 16)
            sp.dma_start(lora_sb[:], lora).then_inc(S("const_in"), 16)
            sp.dma_start(lru_sb[:], lru_w).then_inc(S("const_in"), 16)
            ln_at = {FIRST["out0"] + 3: 0, FIRST["wo0"] + 3: 1, FIRST["down0_3"] + 1: 2,
                     FIRST["out1"] + 3: 3, FIRST["wo1"] + 3: 4, FIRST["down1_3"] + 1: 5}
            for c in range(2, N_CHUNKS):
                if c >= W_SLOTS:
                    sp.wait_ge(S("w_split"), c - W_SLOTS + 1)
                sp.dma_start(w_raw[:, c % W_SLOTS], weights[c]).then_inc(landed[c % W_SLOTS], 16)
                if c == FIRST["out0"] + 2:
                    sp.wait_ge(S("rst_mm"), 2 * NRC - 2)
                    sp.dma_start(h[:], x_tok).then_inc(S("h_in"), 16)
                if c in ln_at:
                    n = ln_at[c]
                    if n == 0:
                        sp.wait_ge(S("mix_done"), 1)
                    if n:
                        sp.wait_ge(S("ln_used"), n)
                    if n == 3:
                        sp.wait_ge(S("s_bc"), 4)
                        sp.wait_ge(S("s_conv"), 8)
                    sp.dma_start(gb[:], ln_rows[n:n + 1].to_broadcast([P, 2, D])).then_inc(S("gb_in"), 16)
                for l in range(2):
                    if c == FIRST[f"k{l}"]:
                        sp.wait_ge(S("mix_done"), l + 1)
                        sp.dma_start(stage[:].rearrange("p a t -> p (a t)")[:, 0:8 * MEM], mem_feat)\
                            .then_inc(S("mem_in"), 16)
            for t in range(NT):
                sp.wait_ge(S("out_rows"), t + 1)
                sp.dma_start(out[:, t], h[:, t]).then_inc(S("stored"), 16)
            sp.wait_ge(S("stored"), 16 * NT)

        @block.gpsimd
        def _(pool):
            def fill(t, value):
                pool.memset(t, value).then_inc(S("pool_step"), 1)
                fill.n += 1
                pool.wait_ge(S("pool_step"), fill.n)
            fill.n = 0

            def sel(t, op, base, pattern, mult, fillv, inner=None):
                pool.affine_select(out=t, in_=t, compare_op=op, fill=fillv, base=base, pattern=pattern,
                                   channel_multiplier=mult).then_inc(S("pool_step"), 1)
                fill.n += 1
                pool.wait_ge(S("pool_step"), fill.n)

            fill(ident[:], 0.0)
            sel(ident[:], ALU.not_equal, 0, [[-1, P]], 1, 1.0)
            fill(ones[:], 1.0)
            fill(bdones[:], 0.0)
            fill(bdones[0:64, 0:64], 1.0)
            fill(bdones[64:128, 64:128], 1.0)
            fill(lastrow[:], 0.0)
            sel(lastrow[:], ALU.not_equal, -(P - 1), [[0, P]], 1, 1.0)
            fill(m_tri[:], 1.0)
            sel(m_tri[:], ALU.is_ge, 0, [[1, SC]], -1, 0.0)
            fill(eye2[:], 0.0)
            sel(eye2[:], ALU.not_equal, 0, [[-1, RC]], 1, 1.0)
            sel(eye2[:], ALU.not_equal, -RC, [[-1, RC]], 1, 1.0)
            fill(m_strict[:], 1.0)
            fill(m_incl[:], 1.0)
            for q in range(2):
                rows = slice(RC * q, RC * q + RC)
                sel(m_strict[rows], ALU.is_gt, 0, [[1, RC]], -1, 0.0)
                sel(m_incl[rows], ALU.is_ge, 0, [[1, RC]], -1, 0.0)
            fill(m_lev[:], 1.0)
            for v in range(6):
                n = 1 << v
                for q in range(2):
                    rows = slice(RC * q, RC * q + RC)
                    view = m_lev[rows, v].rearrange("p (b u) -> p b u", u=2 * n)
                    sel(view, ALU.is_ge, 0, [[-2 * n, RC // (2 * n)], [0, 2 * n]], 1, 0.0)
                    sel(view, ALU.is_ge, n - 1, [[2 * n, RC // (2 * n)], [0, 2 * n]], -1, 0.0)
                    sel(view, ALU.is_ge, -n, [[0, RC // (2 * n)], [1, 2 * n]], 0, 0.0)
            for q in range(2):
                rows = slice(RC * q, RC * q + RC)
                view = m_lev[rows, 6].rearrange("p (b u) -> p b u", u=2)
                sel(view, ALU.is_equal, -1, [[-2, RC // 2], [0, 2]], 1, 0.0)
                sel(view, ALU.is_ge, 0, [[0, RC // 2], [-1, 2]], 0, 0.0)
            fill(m_scan[:], 1.0)
            fill(m_scan[:].rearrange("p (c t) -> p c t", t=RC)[:, :, 0:1], 0.0)
            pool.memset(small[:], 0.0).then_inc(S("masks"), 1)

            def affine(n):
                pool.wait_ge(S("gb_in"), 16 * (n + 1))
                l, which = divmod(n, 3)
                pool.wait_ge(*of(f"lnt{l}_{which}", "_mm", 8))
                for t in range(NT):
                    pool.tensor_tensor(h[:, t], h[:, t], gb[:, 0], ALU.mult).then_inc(S("pool_step"), 1)
                    fill.n += 1
                    pool.wait_ge(S("pool_step"), fill.n)
                    pool.tensor_tensor(h[:, t], h[:, t], gb[:, 1], ALU.add).then_inc(S("h_ready"), 1)
                pool.wait_ge(S("h_ready"), NT * (n + 1))
                pool.memset(small[:, 253:254], 0.0).then_inc(S("ln_used"), 1)
                pool.wait_ge(S("ln_used"), n + 1)

            def differences(b):
                pool.wait_ge(S("r_cum"), b + 1)
                pool.tensor_tensor(s_dec[:], s_cum[:], s_dec[:], ALU.subtract).then_inc(S("r_diff"), 1)
                cum = s_cum[:].rearrange("p j (c t) -> p (j c) t", t=RC)
                pool.tensor_tensor(KH[b][:].rearrange("p j (c t) -> p (j c) t", t=RC),
                                   bc(dend[:, b].rearrange("p j c -> p (j c)"), RC), cum, ALU.subtract)\
                    .then_inc(S("r_diff"), 1)

            def r_times_k(b):
                pool.wait_ge(S("r_k"), b + 1)
                pool.tensor_tensor(BON[b][:], p0[:, 2 * b:2 * b + 2, PAD:PW], p0[:, 4 + 2 * b:6 + 2 * b, PAD:PW],
                                   ALU.mult).then_inc(S("r_rk"), 1)

            def clear(ap, n):
                pool.memset(ap, 0.0).then_inc(S("yt_zero"), 1)

            differences(0)
            r_times_k(0)
            differences(1)
            r_times_k(1)
            g_ = p0[:, 18:22, PAD:PW]

            def gelu(ins):
                gelu.n += 1
                ins.then_inc(S("l_gelu"), 1)
                pool.wait_ge(S("l_gelu"), gelu.n)
            gelu.n = 0
            pool.wait_ge(S("l_gact"), 1)
            gelu(pool.tensor_scalar(li[:], li[:], 0.044715, 1.0, ALU.mult, ALU.add))
            gelu(pool.tensor_tensor(li[:], li[:], g_, ALU.mult))
            clear(yt_(0, 1), 0)
            clear(yt_(1, 1), 0)
            pool.wait_ge(*made("rprod", 10))
            clear(yt_(0, 2), 0)
            pool.wait_ge(S("l_gact"), 2)
            gelu(pool.tensor_scalar(li[:], li[:], 1.0, 0.5, ALU.add, ALU.mult))
            gelu(pool.tensor_tensor(g_, g_, li[:], ALU.mult))
            pool.wait_ge(*made("rprod", 20))
            clear(yt_(1, 2), 0)
            for j in range(4):
                pool.wait_ge(S("lru_out"), 2 * j + 2)
                pool.tensor_tensor(lc[:, j], lc[:, j], li[:, j], ALU.mult).then_inc(S("l_gx"), 1)
                if j in (1, 2):
                    for b in range(2):
                        pool.wait_ge(*made("rz", 4 * j - 2 + 2 * b))
                        clear(yt_(b, j + 2), 0)
            for b in range(2):
                pool.wait_ge(*made("ryt", 9 + b))
                pool.tensor_tensor(M_[b][:].rearrange("p j (c t) -> p (j c) t", t=RC),
                                   bc(dend[:, b].rearrange("p j c -> p (j c)"), RC), mid(eye2[:], 2 * NRC),
                                   ALU.mult).then_inc(S("r_diag"), 1)

            pool.wait_ge(S("mix_done"), 1)
            fill(m_scan[:], 1.0)
            pool.memset(m_scan[:].rearrange("p (c t) -> p c t", t=SC)[:, :, 0:1], 0.0).then_inc(S("masks"), 1)
            for n in range(3):
                affine(n)
            for n in range(1, CONF_TAPS):
                pool.wait_ge(S("c_prod"), n + 1)
                pool.tensor_tensor(cacc[:, 3], cacc[:, 3], gtmp[:, n % 2], ALU.add).then_inc(S("c_conv3"), 1)
                pool.wait_ge(S("c_conv3"), n)

            def gated(m):
                pool.wait_ge(S("s_sigbc"), m + 1)
                pool.tensor_tensor(p1[:, BS + m, PAD:PW], pconv[:, m % 2], gtmp[:, 3], ALU.mult).then_inc(S("s_bc"), 1)
                pool.wait_ge(S("s_bc"), m + 1)

            for m in range(4):
                for k in range(1, 4):
                    pool.wait_ge(S("s_prod"), 4 * m + k + 1)
                    pool.tensor_tensor(pconv[:, m % 2], pconv[:, m % 2], gtmp[:, (3 * m + k) % 2], ALU.add)\
                        .then_inc(S("s_padd"), 1)
                    pool.wait_ge(S("s_padd"), 3 * m + k)
                gated(m)
            for hp in range(8):
                for n in (2 * hp, 2 * hp + 1):
                    pool.wait_ge(S("sbc_out"), n + 1)
                    pool.tensor_tensor(cs[:, n % 4], cs[:, n % 4], p1[:, CS + hp // 4, PAD:PW], ALU.mult)\
                        .then_inc(S("s_cs"), 1)
                pool.wait_ge(S("s_zsig"), hp + 1)
                z_ = p1[:, ZS + hp, PAD:PW]
                pool.tensor_tensor(z_, z_, p1[:, 4 + hp % 4, PAD:PW], ALU.mult).then_inc(S("s_z"), 1)
            for n in range(3, 5):
                affine(n)

        @block.tensor
        def _(pe):
            def take(stg, i):
                n = TILE0[stg] + i
                if n >= 8:
                    owner, k = TILE_OWNER[n - 8]
                    pe.wait_ge(*out_sem(owner, k))
                return ps[n % 8]

            def mm3(o, whi, wlo, xhi, xlo, first, last):
                pe.matmul(o, whi, xlo, start=first, stop=False)
                pe.matmul(o, wlo, xhi, start=False, stop=False)
                return pe.matmul(o, whi, xhi, start=False, stop=last)

            def feature_major(stg, count, xhi, xlo, n, ready=None):
                for i in range(count):
                    c = FIRST[stg] + i
                    s = c % W_SLOTS
                    o = take(stg, i)
                    pe.wait_ge(S("w_split"), c + 1)
                    for k in range(KD):
                        if ready and i == 0:
                            pe.wait_ge(*of(ready, "_out", k + 1))
                        cols = slice(k * P, k * P + P)
                        last = mm3(o[:, 0:n], w_hi[:, s, cols], w_lo[:, s, cols], xhi[:, k, 0:n], xlo[:, k, 0:n],
                                   k == 0, k == KD - 1)
                    last.then_inc(S("chunk_done"), 1)

            def token_major(stg, tiles, kts, xhi, xlo, ready=None):
                for half in range(2):
                    o = [take(stg, half * tiles + t) for t in range(tiles)]
                    for i in range(kts // 2):
                        c = FIRST[stg] + half * (kts // 2) + i
                        s = c % W_SLOTS
                        pe.wait_ge(S("w_split"), c + 1)
                        for kk in range(2):
                            k = 2 * i + kk
                            if ready and half == 0:
                                pe.wait_ge(*ready(k))
                            cols = slice(kk * HALF, kk * HALF + HALF)
                            for t in range(tiles):
                                tok = slice(t * P, t * P + P)
                                last = mm3(o[t][:, 0:HALF], xhi[:, k, tok], xlo[:, k, tok], w_hi[:, s, cols],
                                           w_lo[:, s, cols], k == 0, k == kts - 1)
                        last.then_inc(S("chunk_done"), 1)

            def each(fn):
                for c in range(NRC):
                    for q in range(2):
                        last = fn(c, q, rows_(c), slice(RD * q, RD * q + RD), slice(c * RC, c * RC + RC), cols_(c, q))
                return last

            def low_rank(b):
                if b:
                    pe.wait_ge(S("r_ops"), 1)
                else:
                    pe.wait_ge(S("r_lora"), 2)
                    pe.wait_ge(S("const_in"), 48)
                for name, rows in (("rdec", slice(0, 64)), ("ra", slice(64, 128))):
                    for j in range(2):
                        o = take(f"{name}{b}", j)
                        col = slice((2 * b + j) * P, (2 * b + j) * P + P)
                        pe.matmul(o[:], lora_sb[rows, 0, col], p0[rows, 12, PAD:PW], start=True, stop=True)\
                            .then_inc(S("mixer_mm"), 1)

            def norms(b):
                pe.wait_ge(S("r_kksq"), b + 1)
                for j in range(2):
                    o = take(f"rss{b}", j)
                    pe.matmul(o[:], bdones[:], s_fwd[:, j], start=True, stop=True).then_inc(S("mixer_mm"), 1)

            def bonus(b):
                pe.wait_ge(S("r_rkr"), 2 * b + 2)
                for j in range(2):
                    o = take(f"rbon{b}", j)
                    pe.matmul(o[:], bdones[:], BON[b][:, j], start=True, stop=True).then_inc(S("mixer_mm"), 1)

            def operands(b):
                r_, k_, v_ = (p0[:, 4 * m + 2 * b:4 * m + 2 * b + 2, PAD:PW] for m in range(3))
                return ALPHA_[b], NBH[b], KH[b], r_, NBT[b], k_, v_

            def within_chunks(b):
                alpha, nbh, kh, rho, nbt, kt, v_ = operands(b)
                pe.wait_ge(S("r_ops"), b + 1)
                for n, (lhs, rhs) in enumerate([(alpha, nbh), (nbh, alpha), (kh, alpha), (nbh, rho), (kh, rho)]):
                    for q in range(2):
                        o = take(f"rprod{b}", 2 * n + q)
                        feat = slice(RD * q, RD * q + RD)
                        for j in range(2):
                            for c in range(NRC):
                                cf = slice(c * RC, c * RC + RC)
                                last = pe.matmul(o[rows_(c), split_cols(j, c)], lhs[feat, j, cf], rhs[feat, j, cf],
                                                 start=True, stop=True)
                        last.then_inc(S("mixer_mm"), 1)
                for n, src in enumerate([alpha, nbt, kt, v_]):
                    for j in range(2):
                        o = take(f"rtok{b}", 2 * n + j)
                        for m in range(NT):
                            last = pe.transpose(o[:, m * P:m * P + P], src[:, j, m * P:m * P + P], ident[:])
                        last.then_inc(S("mixer_mm"), 1)
                pe.wait_ge(*out_sem(f"rtok{b}", 8))
                for j in range(2):
                    o = take(f"rw{b}", j)
                    each(lambda c, q, tok, feat, cf, ct: pe.matmul(o[tok, ct], PAK[b][tok, j, ct], v_[tok, j, ct],
                                                                   start=True, stop=True)).then_inc(S("mixer_mm"), 1)

            def halves(ap, n, upper):
                return ap.rearrange("p (b u) -> p b u", u=2 * n)[:, :, 0:n] if upper else \
                    ap.rearrange("p (b u) -> p b u", u=2 * n)[:, :, n:2 * n]

            def compact(o, j, c, q, n):
                at = j * 256 + ((c // 2) * 2 + q) * 32
                return o[rows_(c), at:at + 32].rearrange("p (b n) -> p b n", n=n)

            def level_y(b, v):
                n = 1 << v
                o = take(f"ryt{b}_{v}", 0)
                pe.wait_ge(*(out_sem(f"rz{b}_{v - 1}", 2) if v > 1 else (S("r_x0"), 2 * b + 2)))
                for j in range(2):
                    last = each(lambda c, q, tok, feat, cf, ct: pe.matmul(
                        compact(o, j, c, q, n), M_[b][tok, j, ct], halves(XT_[b][tok, j, ct], n, False),
                        start=True, stop=True))
                last.then_inc(S("mixer_mm"), 1)

            def level_z(b, v):
                n = 1 << v
                x_, y_ = NBH[b], yt_(b, v)
                pe.wait_ge(*out_sem(f"ryt{b}_{v}", 1))
                if v < 5:
                    o = take(f"rz{b}_{v}", 0)
                    for j in range(2):
                        last = each(lambda c, q, tok, feat, cf, ct: pe.matmul(
                            compact(o, j, c, q, n), y_[tok, j, ct], halves(x_[tok, j, ct], n, True),
                            start=True, stop=True))
                    last.then_inc(S("mixer_mm"), 1)
                o = take(f"rz{b}_{v}", 1 if v < 5 else 0)
                for j in range(2):
                    last = each(lambda c, q, tok, feat, cf, ct: pe.matmul(
                        compact(o, j, c, q, n), x_[tok, j, ct], halves(y_[tok, j, ct], n, False),
                        start=True, stop=True))
                last.then_inc(S("mixer_mm"), 1)

            def transitions(b, part):
                if part:
                    pe.wait_ge(*out_sem(f"rgt{b}", 2))
                    for name, right in (("rat", NBT[b]), ("rrho", PRB[b])):
                        for s in range(2):
                            o = take(f"{name}{b}", s)
                            tok = slice(RC * s, RC * s + RC)
                            for j in range(2):
                                for c in range(s, NRC, 2):
                                    for q in range(2):
                                        ct = cols_(c, q)
                                        last = pe.matmul(o[RD * q:RD * q + RD, split_cols(j, c)], KH[b][tok, j, ct],
                                                         right[tok, j, ct], start=True, stop=True)
                            last.then_inc(S("mixer_mm"), 1)
                    return
                for j in range(2):
                    o = take(f"rgt{b}", j)
                    if part == 0:
                        each(lambda c, q, tok, feat, cf, ct: pe.matmul(
                            o[tok, ct], XT_[b][tok, j, ct], ALPHA_[b][tok, j, ct], start=True, stop=True))\
                            .then_inc(S("mixer_mm"), 1)
                for j in range(2):
                    o = take(f"rtw{b}", j)
                    if part == 0:
                        pe.wait_ge(*out_sem(f"rw{b}", j + 1))
                        each(lambda c, q, tok, feat, cf, ct: pe.matmul(
                            o[tok, ct], XT_[b][tok, j, ct], PAK[b][tok, j, ct], start=True, stop=True))\
                            .then_inc(S("mixer_mm"), 1)

            def scan():
                both = [(jj, q, slice(RD * q, RD * q + RD)) for jj in range(4) for q in range(2)]
                for b in range(2):
                    pe.wait_ge(*out_sem(f"rtw{b}", 2))
                    pe.wait_ge(*out_sem(f"rat{b}", 2))
                    pe.wait_ge(*out_sem(f"rrho{b}", 2))
                banks = {}

                def from_tokens(c):
                    tok = rows_(c)
                    if c < NRC - 1:
                        banks["h", c] = take(f"rst{c}", 0)
                    if c % 2 == 0:
                        for q in range(2):
                            banks["o", c // 2, q] = take(f"ro{c // 2}", q)
                    for jj, q, feat in both:
                        b, j = divmod(jj, 2)
                        kt, v_ = operands(b)[5:7]
                        ct, oc = cols_(c, q), slice(jj * RD, jj * RD + RD)
                        if c < NRC - 1:
                            o = banks["h", c]
                            pe.matmul(o[feat, oc], kt[tok, j, ct], v_[tok, j, ct], start=(jj == 0), stop=False)
                            pe.matmul(o[feat, oc], NBT[b][tok, j, ct], NBH[b][tok, j, ct], start=False,
                                      stop=(c == 0 and jj == 3))
                        o = banks["o", c // 2, q]
                        pe.matmul(o[tok, oc], PRB[b][tok, j, ct], NBH[b][tok, j, ct], start=(jj == 0), stop=False)
                        last = pe.matmul(o[tok, oc], PRK[b][tok, j, ct], v_[tok, j, ct], start=False,
                                         stop=(c == 0 and jj == 3))
                    last.then_inc(S("rst_mm"), 1)

                def from_state(c):
                    tok, cf = rows_(c), slice(c * RC, c * RC + RC)
                    pe.wait_ge(S("rst_mm"), 2 * c)
                    pe.wait_ge(*out_sem(f"rst{c - 1}", 1))
                    if c < NRC - 1:
                        for jj, q, feat in both:
                            b, j = divmod(jj, 2)
                            last = pe.matmul(banks["h", c][feat, jj * RD:jj * RD + RD], M_[b][feat, j, cf],
                                             hall[feat, jj, cf], start=False, stop=(jj == 3))
                        last.then_inc(S("rst_mm"), 1)
                    for jj, q, feat in both:
                        b, j = divmod(jj, 2)
                        last = pe.matmul(banks["o", c // 2, q][tok, jj * RD:jj * RD + RD],
                                         operands(b)[3][feat, j, cf], hall[feat, jj, cf], start=False, stop=(jj == 3))
                    if c % 2:
                        last.then_inc(S("ro_mm"), 1)

                from_tokens(0)
                for c in range(1, NRC):
                    from_tokens(c)
                    from_state(c)

            def even_output():
                for j in range(4):
                    o = take("rg", j)
                    pe.matmul(o[:], lora_sb[:, 1, j * P:j * P + P], p0[:, 13, PAD:PW], start=True, stop=True)\
                        .then_inc(S("mixer_mm"), 1)
                pe.wait_ge(S("r_gn"), 4)
                for jj in range(4):
                    o = take("rback", jj)
                    for m in range(NT):
                        last = pe.transpose(o[:, m * P:m * P + P], oall[:, m, jj * P:jj * P + P], ident[:])
                    last.then_inc(S("mixer_mm"), 1)

            def lru():
                pe.wait_ge(S("l_conv"), 4)
                for j in range(4):
                    for m in range(2):
                        o = take("lru", 2 * j + m)
                        pe.matmul(o[:], lru_sb[:, 4 * m + j], lc[:, j], start=True, stop=True)\
                            .then_inc(S("mixer_mm"), 1)

            def even_mixer():
                def project(n):
                    feature_major(IN0[n][0], IN0[n][1], act_hi, act_lo, T)

                project(0)
                project(1)
                low_rank(0)
                project(2)
                norms(0)
                project(3)
                bonus(0)
                project(4)
                low_rank(1)
                project(5)
                project(6)
                norms(1)
                within_chunks(0)
                bonus(1)
                within_chunks(1)
                lru()
                for v in range(1, 6):
                    for b in range(2):
                        level_y(b, v)
                    for b in range(2):
                        level_z(b, v)
                for b in range(2):
                    pe.wait_ge(*out_sem(f"rz{b}_5", 1))
                    transitions(b, 0)
                for b in range(2):
                    transitions(b, 1)
                scan()
                even_output()

            def decay_rows(hp):
                for q in range(2):
                    hd = 2 * hp + q
                    o = take(f"sbc{hp}", q)
                    pe.matmul(o[:], ident[0:16, hd:hd + 1].to_broadcast([16, P]), sdt[:, 1, :], start=True, stop=True)\
                        .then_inc(S("mixer_mm"), 1)

            def sum_squares(g):
                o = take(f"srms{g}", 0)
                for j in range(4):
                    pe.wait_ge(S("s_ysq"), 4 * g + j + 1)
                    last = pe.matmul(o[:], ones[:], p1[:, XS + 4 * g + j, PAD:PW], start=(j == 0), stop=(j == 3))
                last.then_inc(S("mixer_mm"), 1)

            def odd_mixer():
                pe.wait_ge(S("s_acum"), 1)
                for m in range(2):
                    o = take("stok", m)
                    for c in range(NSC):
                        last = pe.transpose(o[:, c * 16:c * 16 + 16], sdt[:, m, c * SC:c * SC + SC], ident[0:16, 0:16])
                    last.then_inc(S("mixer_mm"), 1)
                o = take("slast", 0)
                pe.wait_ge(*out_sem("stok", 2))
                pe.matmul(o[:, 0:64], lastrow[:], stm[:, 1].rearrange("p c h -> p (c h)"), start=True, stop=True)\
                    .then_inc(S("mixer_mm"), 1)
                pe.wait_ge(S("c_conv"), 4)
                pe.wait_ge(S("c_conv3"), CONF_TAPS - 1)
                o = take("cmean", 0)
                for j in range(4):
                    last = pe.matmul(o[:], ones[:], cacc[:, j], start=(j == 0), stop=(j == 3))
                last.then_inc(S("mixer_mm"), 1)
                pe.wait_ge(S("s_conv"), 8)
                for c in range(NSC):
                    for q in range(2):
                        o = take("sxt", 2 * c + q)
                        for j in range(4):
                            last = pe.transpose(o[:, j * P:j * P + P],
                                                p1[:, XS + 4 * q + j, PAD + c * SC:PAD + c * SC + SC], ident[:])
                        last.then_inc(S("mixer_mm"), 1)
                o = take("cvar", 0)
                for j in range(4):
                    pe.wait_ge(S("c_sq"), j + 1)
                    last = pe.matmul(o[:], ones[:], p1[:, 4 + j, PAD:PW], start=(j == 0), stop=(j == 3))
                last.then_inc(S("mixer_mm"), 1)
                pe.wait_ge(S("s_bc"), 4)
                for q in range(2):
                    o = take("sbt", q)
                    for c in range(2):
                        for g in range(2):
                            n = 2 * c + g
                            last = pe.transpose(o[:, n * P:n * P + P],
                                                p1[:, BS + g, PAD + (2 * q + c) * SC:PAD + (2 * q + c + 1) * SC], ident[:])
                    last.then_inc(S("mixer_mm"), 1)
                for g in range(2):
                    o = take("scb", g)
                    for c in range(NSC):
                        cols = slice(PAD + c * SC, PAD + c * SC + SC)
                        last = pe.matmul(o[:, c * SC:c * SC + SC], p1[:, BS + g, cols], p1[:, CS + g, cols],
                                         start=True, stop=True)
                    last.then_inc(S("mixer_mm"), 1)
                pe.wait_ge(*out_sem("sbt", 2))
                pe.wait_ge(*out_sem("sxt", 8))
                for c in range(NSC - 1):
                    for g in range(2):
                        o = take("sst", 2 * c + g)
                        pe.matmul(o[:], bt[:, c, g * P:g * P + P], xdtd[:, c, g * 512:g * 512 + 512],
                                  start=True, stop=True).then_inc(S("mixer_mm"), 1)
                decay_rows(0)
                pe.wait_ge(*out_sem("sst", 6))
                for hp in range(8):
                    if hp < 7:
                        decay_rows(hp + 1)
                    o = take(f"sy{hp}", 0)
                    for q in range(2):
                        hd = 2 * hp + q
                        pe.wait_ge(S("s_mt"), hd + 1)
                        pe.wait_ge(S("s_cs"), hd + 1)
                        for c in range(NSC):
                            rows = slice(64 * q, 64 * q + 64)
                            cols = slice(c * SC, c * SC + SC)
                            last = pe.matmul(o[rows, cols], xdt[:, c, hd * 64:hd * 64 + 64], mt(hd)[:, cols],
                                             start=True, stop=(c == 0))
                            if c:
                                last = pe.matmul(o[rows, cols], prev[:, c - 1, hd * 64:hd * 64 + 64],
                                                 cs[:, hd % 4, cols], start=False, stop=True)
                    last.then_inc(S("mixer_mm"), 1)
                    if hp == 5:
                        sum_squares(0)
                sum_squares(1)

            def to_features(l, which):
                n = 3 * l + which
                pe.wait_ge(S("ln_rows"), NT * (n + 1))
                for k in range(KD):
                    o = take(f"lnt{l}_{which}", k)
                    for t in range(NT):
                        last = pe.transpose(o[:, t * P:t * P + P], h[:, t, k * P:k * P + P], ident[:])
                    last.then_inc(S("lnt_mm"), 1)

            def attention(l):
                pe.wait_ge(S("mem_split"), l + 1)
                memv = [a[:].rearrange("p a t -> p (a t)")[:, 0:8 * MEM].rearrange("p (a t) -> p a t", a=8)
                        for a in (aux_hi, aux_lo)]
                feature_major(f"k{l}", 8, memv[0], memv[1], MEM)
                to_features(l, 0)
                token_major(f"v{l}", 2, KD, memv[0], memv[1])
                feature_major(f"q{l}", 8, act_hi, act_lo, T, ready=f"lnt{l}_0")
                pe.wait_ge(*out_sem(f"q{l}", 8))
                pe.wait_ge(*out_sem(f"k{l}", 8))
                for hp in range(2):
                    for t in range(NT):
                        o = take(f"s{l}", 4 * hp + t)
                        tok = slice(t * P, t * P + P)
                        for q in range(2):
                            hd = 2 * hp + q
                            for k in range(2):
                                last = mm3(o[:, q * MEM:q * MEM + MEM], aux_hi[:, 2 * hd + k, tok],
                                           aux_lo[:, 2 * hd + k, tok], k_hi[:, 2 * hd + k], k_lo[:, 2 * hd + k],
                                           k == 0, k == 1)
                        last.then_inc(S("s_mm"), 1)
                pe.wait_ge(*out_sem(f"v{l}", 4))
                for hp in range(2):
                    for t in range(NT):
                        pe.wait_ge(S("p_ready"), 8 * l + 4 * hp + t + 1)
                        o = take(f"pt{l}_{hp}", t)
                        for q in range(2):
                            for m in range(2):
                                n = 2 * q + m
                                last = pe.transpose(o[:, n * P:n * P + P],
                                                    stage[:, 4 * hp + t, q * MEM + m * P:q * MEM + m * P + P], ident[:])
                        last.then_inc(S("pt_mm"), 1)
                    pe.wait_ge(*out_sem(f"pt{l}_{hp}", 4))
                    for q in range(2):
                        for dt in range(2):
                            o = take(f"pv{l}_{hp}", 2 * q + dt)
                            col = slice((2 * hp + q) * 256 + dt * P, (2 * hp + q) * 256 + dt * P + P)
                            for m in range(2):
                                last = mm3(o[:], v_hi[:, m, col], v_lo[:, m, col], act_hi[:, 8 + 2 * q + m],
                                           act_lo[:, 8 + 2 * q + m], m == 0, m == 1)
                            last.then_inc(S("pv_mm"), 1)
                pe.wait_ge(*out_sem(f"pv{l}_1", 4))
                token_major(f"wo{l}", NT, KD, act_hi, act_lo)

            def mlp(l):
                for q in range(QUARTERS):
                    feature_major(f"up{l}_{q}", 8, act_hi, act_lo, T, ready=f"lnt{l}_1" if q == 0 else None)
                    token_major(f"down{l}_{q}", NT, KD, aux_hi, aux_lo, 
                                ready=lambda k, q=q: of(f"up{l}_{q}", "_lo", k + 1))

            pe.wait_ge(S("masks"), 1)
            for l in range(2):
                if l == 0:
                    pe.wait_ge(S("x_split"), 1)
                if l == 0:
                    even_mixer()
                else:
                    feature_major("in1", 29, act_hi, act_lo, T, ready="lnt0_2")
                    pe.wait_ge(S("masks"), 2)
                    odd_mixer()
                token_major(f"out{l}", NT, 8 if l == 0 else 12, act_hi, act_lo,
                            ready=lambda k, l=l: (S("mix_lo"), 8 * l + k + 1))
                attention(l)
                to_features(l, 1)
                mlp(l)
                if l == 0:
                    to_features(0, 2)

        @block.scalar
        def _(act):
            n_split = [0]
            n_step = [0]

            def step(ins):
                n_step[0] += 1
                ins.then_inc(S("act_step"), 1)
                act.wait_ge(S("act_step"), n_step[0])

            counts = {"in_out": 14}

            def done(ins, name):
                counts[name] = counts.get(name, 0) + 1
                ins.then_inc(S(name), 1)
                act.wait_ge(S(name), counts[name])

            def split(upto):
                while n_split[0] < min(upto, N_CHUNKS):
                    c = n_split[0]
                    s = c % W_SLOTS
                    act.wait_ge(landed[s], 16 * (c // W_SLOTS + 1))
                    if c >= W_SLOTS:
                        act.wait_ge(S("chunk_done"), c - W_SLOTS + 1)
                    act.activation(w_hi[:, s], w_raw[:, s], ACT.Copy).then_inc(S("w_hi_done"), 1)
                    n_split[0] += 1

            def chunk(stg, i):
                c = FIRST[stg] + i
                split(c + W_SLOTS)
                act.wait_ge(S("chunk_done"), c + 1)

            def copy_hi(stg, i, dst, n=T):
                done(act.activation(dst, bank(stg, i)[:, 0:n], ACT.Copy), FAMILY[stg] + "_hi")

            act.wait_ge(S("x_in"), 16)
            done(act.activation(act_hi[:, 0:8], stage[:], ACT.Copy), "x_hi")
            act.wait_ge(S("const_in"), 48)
            step(act.activation(omu[:], vec[:, VEC["mu"]:VEC["mu"] + 14], ACT.Identity, bias=1.0, scale=-1.0))
            act.wait_ge(S("masks"), 1)
            step(act.activation(small[:, 80:84], vec[:, VEC["lam"]:VEC["lam"] + 4], ACT.Exp, scale=-1.0))
            step(act.activation(small[:, 80:84], small[:, 80:84], ACT.Ln, bias=1.0))
            step(act.activation(small[:, 80:84], small[:, 80:84], ACT.Copy, scale=-8.0))

            def gates(b):
                if b:
                    act.wait_ge(S("r_ops"), 1)
                for j in range(2):
                    act.wait_ge(*made("rlora", 4 * b + j + 1))
                    done(act.activation(s_dec[:, j], bank(f"rdec{b}", j)[:], ACT.Sigmoid, bias=V("w0", 2 * b + j)),
                         "rdec_out")
                for j in range(2):
                    act.wait_ge(*made("rlora", 4 * b + 2 + j + 1))
                    done(act.activation(s_a[:, j], bank(f"ra{b}", j)[:], ACT.Sigmoid, bias=V("a0", 2 * b + j)),
                         "ra_out")

            def squares(b):
                act.wait_ge(S("r_kk"), b + 1)
                done(act.activation(s_fwd[:], NBT[b][:], ACT.Square), "r_kksq")

            def norms(b):
                for j in range(2):
                    act.wait_ge(*made("rss", 2 * b + j + 1))
                    done(act.activation(NBH[b][:, j], bank(f"rss{b}", j)[:], ACT.Sqrt), "rss_out")

            def exponentials(b):
                act.wait_ge(S("r_diff"), 2 * b + 1)
                done(act.activation(ALPHA_[b][:], s_dec[:], ACT.Exp, scale=NEG_EXP_HALF), "r_e")
                done(act.activation(s_inv[:], s_cum[:], ACT.Exp, scale=-NEG_EXP_HALF), "r_e")
                done(act.activation(s_fwd[:], s_cum[:], ACT.Exp, scale=NEG_EXP_HALF), "r_e")
                act.wait_ge(S("r_diff"), 2 * b + 2)
                done(act.activation(s_dec[:], KH[b][:], ACT.Exp, scale=NEG_EXP_HALF), "r_e")

            def bonus(b):
                act.wait_ge(S("r_rk"), b + 1)
                for j in range(2):
                    done(act.activation(BON[b][:, j], BON[b][:, j], ACT.Copy, scale=V("rk", 2 * b + j)), "r_rkr")

            for i in range(22):
                stg, n = PLACE0[i]
                tile = ORDER0[i]
                chunk(stg, n)
                if i < 14:
                    done(act.activation(p0[:, tile, PAD:PW], bank(stg, n)[:], ACT.Identity, bias=0.0,
                                        scale=omu[:, tile:tile + 1]), "r_in")
                else:
                    act.wait_ge(S("in_out"), 14)
                    done(act.activation(p0[:, tile, PAD:PW], bank(stg, n)[:], ACT.Copy), "in_out")
                if i == 1:
                    act.wait_ge(S("in_out"), 2)
                    done(act.activation(p0[0:64, 12, PAD:PW], p0[0:64, 12, PAD:PW], ACT.Tanh), "r_lora")
                    done(act.activation(p0[:, 13, PAD:PW], p0[:, 13, PAD:PW], ACT.Sigmoid), "r_lora")
                if i == 5:
                    gates(0)
                if i == 6:
                    squares(0)
                if i == 9:
                    norms(0)
                    exponentials(0)
                if i == 10:
                    bonus(0)
                if i == 13:
                    gates(1)
                if i == 14:
                    squares(1)
                if i == 21:
                    done(act.activation(li[:], p0[:, 18:22, PAD:PW], ACT.Square), "l_gact")
            split(FIRST["out0"] + W_SLOTS)
            norms(1)
            exponentials(1)
            bonus(1)

            def tokens(b):
                k_, v_ = (p0[:, 4 * m + 2 * b:4 * m + 2 * b + 2, PAD:PW] for m in (1, 2))
                act.wait_ge(S("rbon_out"), 2 * b + 2)
                for n in range(8):
                    act.wait_ge(*made("rtok", 8 * b + n + 1))
                    dst = (ALPHA_[b], NBT[b], k_, v_)[n // 2]
                    done(act.activation(dst[:, n % 2], bank(f"rtok{b}", n)[:], ACT.Copy), "rtok_out")
                for j in range(2):
                    act.wait_ge(*made("rw", 2 * b + j + 1))
                    done(act.activation(PAK[b][:, j], bank(f"rw{b}", j)[:], ACT.Copy), "rw_out")

            tokens(0)
            act.wait_ge(S("l_gelu"), 2)
            done(act.activation(li[:], li[:], ACT.Tanh, scale=0.7978845608028654), "l_gact")
            tokens(1)
            act.wait_ge(S("l_gelu"), 4)
            for j in range(4):
                lam = small[:, 80 + j:81 + j]
                a_ = p0[:, 14 + j, PAD:PW]
                act.wait_ge(*made("lru", 2 * j + 2))
                done(act.activation(a_, bank("lru", 2 * j)[:], ACT.Sigmoid, bias=V("lba", j)), "lru_out")
                done(act.activation(li[:, j], bank("lru", 2 * j + 1)[:], ACT.Sigmoid, bias=V("lbx", j)), "lru_out")
            for j in range(4):
                lam = small[:, 80 + j:81 + j]
                a_ = p0[:, 14 + j, PAD:PW]
                if j:
                    act.wait_ge(S("l_var"), j)
                done(act.activation(lt[:], a_, ACT.Tanh, scale=lam), "l_act")
                done(act.activation(a_, a_, ACT.Exp, scale=lam), "l_act")
                act.wait_ge(S("l_var"), j + 1)
                done(act.activation(li[:, j], li[:, j], ACT.Sqrt, scale=-1.0), "l_std")
            for b in range(2):
                for j in range(2):
                    act.wait_ge(*made("rt", 4 * b + j + 1))
                    done(act.activation(KH[b][:, j], bank(f"rgt{b}", j)[:], ACT.Copy), "rgt_out")
                for j in range(2):
                    act.wait_ge(*made("rt", 4 * b + 2 + j + 1))
                    done(act.activation(NBH[b][:, j], bank(f"rtw{b}", j)[:], ACT.Copy), "rtw_out")
            for c in range(NRC - 1):
                act.wait_ge(S("rst_mm"), 2 * c + 1)
                done(act.activation(hall[:, :, (c + 1) * RC:(c + 2) * RC],
                                    bank(f"rst{c}", 0)[:, 0:256].rearrange("p (j v) -> p j v", j=4), ACT.Copy), "rst_out")
                if c % 2 and c > 1:
                    m = c // 2 - 1
                    act.wait_ge(S("ro_out"), 2 * m + 2)
                    done(act.activation(zsq[:, m % 2], oall[:, m], ACT.Square), "r_osq")
                    act.wait_ge(S("r_gvar"), m + 1)
                    done(act.activation(small[:, 48 + 8 * m:56 + 8 * m], small[:, 48 + 8 * m:56 + 8 * m], ACT.Sqrt), "r_gstd")
            for m in range(2, 4):
                act.wait_ge(S("ro_out"), 2 * m + 2)
                done(act.activation(zsq[:, m % 2], oall[:, m], ACT.Square), "r_osq")
                act.wait_ge(S("r_gvar"), m + 1)
                done(act.activation(small[:, 48 + 8 * m:56 + 8 * m], small[:, 48 + 8 * m:56 + 8 * m], ACT.Sqrt), "r_gstd")
            act.wait_ge(S("l_mix"), 4)
            for i in range(4):
                done(act.activation(act_hi[:, i], p0[:, YT0[i], PAD:PW], ACT.Copy), "mix_hi")
            for jj in range(4):
                act.wait_ge(*made("rback", jj + 1))
                done(act.activation(p0[:, jj, PAD:PW], bank("rback", jj)[:], ACT.Identity, bias=V("gnb", jj),
                                    scale=V("gng", jj)), "rback_out")
            for jj in range(4):
                act.wait_ge(S("rg_out"), jj + 1)
                done(act.activation(act_hi[:, 4 + jj], p0[:, jj, PAD:PW], ACT.Copy), "mix_hi")

            def ln_std(n):
                act.wait_ge(S("ln_var"), n + 1)
                done(act.activation(lnsd[:], lnsd[:], ACT.Sqrt), "ln_std")

            def feature_hi(l, which, k):
                stg = f"lnt{l}_{which}"
                c = 8 * (3 * l + which) + k
                act.wait_ge(*of(stg, "_mm", k + 1))
                done(act.activation(act_hi[:, k], bank(stg, k)[:], ACT.Identity, bias=V("lnb", c), scale=V("lng", c)),
                     "lnt_hi")

            def attention(l):
                act.wait_ge(S("mem_in"), 16 * (l + 1))
                memv = aux_hi[:].rearrange("p a t -> p (a t)")[:, 0:8 * MEM]
                done(act.activation(memv, stage[:].rearrange("p a t -> p (a t)")[:, 0:8 * MEM], ACT.Copy), "mem_hi")
                ln_std(3 * l)
                for i in range(8):
                    chunk(f"k{l}", i)
                    copy_hi(f"k{l}", i, k_hi[:, i], MEM)
                for half in range(2):
                    for i in range(4):
                        for k in range(4 * half + i + (half + i > 0), min(4 * half + i + 2, KD)):
                            feature_hi(l, 0, k)
                        chunk(f"v{l}", 4 * half + i)
                    for m in range(2):
                        copy_hi(f"v{l}", 2 * half + m, v_hi[:, m, half * HALF:half * HALF + HALF])
                for i in range(8):
                    chunk(f"q{l}", i)
                    copy_hi(f"q{l}", i, aux_hi[:, i])
                split(FIRST[f"wo{l}"] + W_SLOTS)
                for n in range(8):
                    act.wait_ge(S("p_max"), 8 * l + n + 1)
                    for q in range(2):
                        ins = act.activation(stage[:, n, q * MEM:q * MEM + MEM], bank(f"s{l}", n)[:, q * MEM:q * MEM + MEM],
                                             ACT.Exp, bias=small[:, 128 + 2 * n + q:129 + 2 * n + q], scale=1.0 / 16,
                                             accum_out=small[:, 144 + 2 * n + q:145 + 2 * n + q])
                        if q == 0:
                            step(ins)
                        else:
                            done(ins, "s_out")
                for hp in range(2):
                    for t in range(NT):
                        act.wait_ge(*of(f"pt{l}_{hp}", "_mm", t + 1))
                        if hp and t == 0:
                            act.wait_ge(*of(f"pv{l}_0", "_mm", 4))
                        done(act.activation(act_hi[:, 8:12, t * P:t * P + P],
                                       bank(f"pt{l}_{hp}", t)[:].rearrange("p (a t) -> p a t", a=4), ACT.Copy), "pt_hi")
                    for n in range(4):
                        act.wait_ge(*of(f"pv{l}_{hp}", "_mm", n + 1))
                        done(act.activation(act_hi[:, 4 * hp + n], bank(f"pv{l}_{hp}", n)[:], ACT.Copy), "pv_hi")
                for i in range(8):
                    chunk(f"wo{l}", i)
                ln_std(3 * l + 1)
                for k in range(KD):
                    feature_hi(l, 1, k)

            def mlp(l):
                for q in range(QUARTERS):
                    for i in range(8):
                        chunk(f"up{l}_{q}", i)
                        n = 8 * q + i
                        done(act.activation(stage[:, n % 2], bank(f"up{l}_{q}", i)[:], ACT.Relu), "up_out")
                        act.wait_ge(*of(f"up{l}_{q}", "_sq", i + 1))
                        done(act.activation(aux_hi[:, i], stage[:, 2 + n % 2], ACT.Copy), "up_hi")
                    for i in range(8):
                        chunk(f"down{l}_{q}", i)
                ln_std(3 * l + 2)

            for i in range(8):
                chunk("out0", i)
            attention(0)
            mlp(0)
            for k in range(KD):
                feature_hi(0, 2, k)
            def conf_product(n):
                src = cu[:, 3, CP - (CONF_TAPS - 1) + n:CP - (CONF_TAPS - 1) + n + T]
                if n == 0:
                    act.wait_ge(S("c_u"), 4)
                    done(act.activation(cacc[:, 3], src, ACT.Identity, bias=V("ccb", 3), scale=V("ccw", 3)), "c_prod")
                else:
                    if n >= 3:
                        act.wait_ge(S("c_conv3"), n - 2)
                    done(act.activation(gtmp[:, n % 2], src, ACT.Copy, scale=V("ccw", 4 * n + 3)), "c_prod")

            def ssd_products(m):
                i = 8 + m
                x_ = p1[:, XS + i]
                for k in range(4):
                    n = 4 * m + k
                    if k == 0:
                        if m >= 2:
                            act.wait_ge(S("s_bc"), m - 1)
                        done(act.activation(pconv[:, m % 2], x_[:, 1:1 + T], ACT.Identity, bias=V("scb", i),
                                            scale=V("scw", i)), "s_prod")
                    else:
                        if 3 * m + k >= 3:
                            act.wait_ge(S("s_padd"), 3 * m + k - 2)
                        act.wait_ge(S("c_conv3"), CONF_TAPS - 1)
                        done(act.activation(gtmp[:, (3 * m + k) % 2], x_[:, 1 + k:1 + k + T], ACT.Copy,
                                            scale=V("scw", 12 * k + i)), "s_prod")

            def ssd_gate(m):
                act.wait_ge(S("s_cv"), m + 1)
                if m:
                    act.wait_ge(S("s_conv"), m)
                done(act.activation(gtmp[:, 2], sconv[:, m % 2], ACT.Sigmoid), "s_sig")

            def ssd_gate_bc(m):
                act.wait_ge(S("s_padd"), 3 * m + 3)
                if m:
                    act.wait_ge(S("s_bc"), m)
                done(act.activation(gtmp[:, 3], pconv[:, m % 2], ACT.Sigmoid), "s_sigbc")

            act.wait_ge(S("ln_used"), 3)
            act.wait_ge(S("c_zero"), 1)
            for i in range(29):
                chunk("in1", i)
                fn = ACT.Sigmoid if 4 <= i < 8 else ACT.Copy
                done(act.activation(p1[:, i, PAD:PW], bank("in1", i)[:], fn), "in_out")
                if i >= 8:
                    for n in range(3 * (i - 8), min(3 * (i - 7), CONF_TAPS)):
                        conf_product(n)
                if i >= 13 and i % 2 and (i - 13) // 2 < 8:
                    ssd_gate((i - 13) // 2)
                if i == 19:
                    raw = p1[0:16, DT, PAD:PW]
                    step(act.activation(raw, raw, ACT.Identity, bias=vec[0:16, VEC["dtb"]:VEC["dtb"] + 1]))
                    step(act.activation(sdt[:, 0], raw, ACT.Abs))
                    step(act.activation(sdt[:, 0], sdt[:, 0], ACT.Exp, scale=-1.0))
                    step(act.activation(small[0:16, 200:201], vec[0:16, VEC["alog"]:VEC["alog"] + 1], ACT.Exp))
                    done(act.activation(sdt[:, 0], sdt[:, 0], ACT.Ln, bias=1.0), "s_sp")
                if i in (21, 23, 25, 27):
                    ssd_products((i - 21) // 2)
                if i in (22, 24, 26, 28):
                    ssd_gate_bc((i - 22) // 2)
            split(FIRST["out1"] + W_SLOTS)
            act.wait_ge(*made("slast", 1))
            done(act.activation(stm[:, 3], bank("slast", 0)[:, 0:64].rearrange("p (c h) -> p c h", c=NSC), ACT.Copy),
                 "slast_out")
            act.wait_ge(S("s_dte"), 1)
            step(act.activation(stm[:, 2], stm[:, 2], ACT.Exp))
            done(act.activation(stm[:, 3], stm[:, 3], ACT.Exp), "s_dtee")
            for j in range(4):
                act.wait_ge(S("c_cent"), j + 1)
                done(act.activation(p1[:, 4 + j, PAD:PW], cacc[:, j], ACT.Square), "c_sq")
            for q in range(2):
                act.wait_ge(*made("sbt", q + 1))
                done(act.activation(bt[:, 2 * q:2 * q + 2].rearrange("p c n -> p (c n)"), bank("sbt", q)[:], ACT.Copy),
                     "sbt_out")
            act.wait_ge(S("cvar_out"), 1)
            done(act.activation(c_std, c_std, ACT.Sqrt), "c_stdd")
            for j in range(4):
                act.wait_ge(S("c_norm"), j + 1)
                done(act.activation(p1[:, 4 + j, PAD:PW], cacc[:, j], ACT.Sigmoid), "c_sig")
            act.wait_ge(S("mix_f1"), 4)

            def z_gate(hp):
                done(act.activation(p1[:, 4 + hp % 4, PAD:PW], p1[:, ZS + hp, PAD:PW], ACT.Sigmoid), "s_zsig")

            for hp in range(4):
                z_gate(hp)

            def decays(hp):
                for n in (2 * hp, 2 * hp + 1):
                    act.wait_ge(S("s_diff"), n + 1)
                    if hp >= 2:
                        act.wait_ge(*made("sy", hp - 1))
                    done(act.activation(cs[:, n % 4], bank(f"sbc{hp}", n % 2)[:], ACT.Exp), "sbc_out")
                    done(act.activation(mt(n), mt(n), ACT.Exp), "s_exp")

            decays(0)
            for hp in range(8):
                if hp < 7:
                    decays(hp + 1)
                if hp == 3:
                    for n in range(4, 8):
                        act.wait_ge(S("s_z"), n - 3)
                        z_gate(n)
                act.wait_ge(S("s_y"), hp + 1)
                done(act.activation(p1[:, XS + hp, PAD:PW], p1[:, ZS + hp, PAD:PW], ACT.Square), "s_ysq")
            for g in range(2):
                act.wait_ge(S("srms_out"), g + 1)
                done(act.activation(p1[:, BS + g, PAD:PW], p1[:, BS + g, PAD:PW], ACT.Sqrt), "s_rstd")
                if g == 0:
                    act.wait_ge(*made("sy", 8))
                    for i in range(4):
                        done(act.activation(act_hi[:, i], p1[:, YT1[i], PAD:PW], ACT.Copy), "mix_hi")
            for i in range(4, 12):
                act.wait_ge(S("mix_f1"), i + 1)
                done(act.activation(act_hi[:, i], p1[:, YT1[i], PAD:PW], ACT.Copy), "mix_hi")
            for i in range(12):
                chunk("out1", i)
            attention(1)
            mlp(1)

        @block.vector
        def _(dve):
            n_split = [0]
            n_step = [0]

            def step(ins, lag=0):
                n_step[0] += 1
                ins.then_inc(S("dve_step"), 1)
                if n_step[0] > lag:
                    dve.wait_ge(S("dve_step"), n_step[0] - lag)

            counts = {}

            def done(ins, name):
                counts[name] = counts.get(name, 0) + 1
                ins.then_inc(S(name), 1)
                dve.wait_ge(S(name), counts[name])

            def f(ap):
                return ap.bitcast(F32)

            def split(upto):
                while n_split[0] < min(upto, N_CHUNKS):
                    c = n_split[0]
                    s = c % W_SLOTS
                    dve.wait_ge(S("w_hi_done"), c + 1)
                    dve.tensor_tensor(w_lo[:, s], w_raw[:, s], f(w_hi[:, s]), ALU.subtract).then_inc(S("w_split"), 1)
                    n_split[0] += 1

            def chunk(stg, i):
                c = FIRST[stg] + i
                split(c + W_SLOTS)
                dve.wait_ge(S("chunk_done"), c + 1)

            def tt(o, a, b_, op):
                return dve.tensor_tensor(o, a, b_, op)

            def stt(o, a, s, b_, op0, op1):
                return dve.scalar_tensor_tensor(out=o, in0=a, scalar=s, in1=b_, op0=op0, op1=op1)

            MUL, ADD, SUB = ALU.mult, ALU.add, ALU.subtract

            dve.wait_ge(S("x_hi"), 1)
            dve.wait_ge(S("x_in"), 16)
            tt(act_lo[:, 0:8], stage[:], f(act_hi[:, 0:8]), SUB).then_inc(S("x_split"), 1)
            dve.wait_ge(S("x_split"), 1)
            step(dve.memset(p0[:, :, 0:PAD], 0.0))
            dve.wait_ge(S("const_in"), 48)
            dve.wait_ge(S("masks"), 1)
            step(dve.tensor_scalar(small[:, 84:88], vec[:, VEC["ka"]:VEC["ka"] + 4], -1.0, 1.0, MUL, ADD))

            def scaled_keys(b):
                for j in range(2):
                    ins = dve.tensor_scalar(NBT[b][:, j], p0[:, 4 + 2 * b + j, PAD:PW], V("kk", 2 * b + j), None, MUL)
                    if j:
                        done(ins, "r_kk")
                    else:
                        step(ins, 1)

            def running_decay(b):
                dve.wait_ge(S("rdec_out"), 2 * b + 2)
                for j in range(2):
                    step(dve.tensor_tensor_scan(s_cum[:, j], m_scan[:], s_dec[:, j], 0.0, MUL, ADD))
                cum = s_cum[:].rearrange("p j (c t) -> p j c t", t=RC)
                done(dve.tensor_copy(dend[:, b], cum[:, :, :, RC - 1]), "r_cum")

            def keys(b):
                k_ = p0[:, 4 + 2 * b:6 + 2 * b, PAD:PW]
                dve.wait_ge(S("ra_out"), 2 * b + 2)
                for j in range(2):
                    step(dve.tensor_scalar(BON[b][:, j], s_a[:, j], V("ka", 2 * b + j),
                                           small[:, 84 + 2 * b + j:85 + 2 * b + j], MUL, ADD))
                done(tt(k_, k_, BON[b][:], MUL), "r_k")

            def normalised(b, part):
                dve.wait_ge(S("rss_out"), 2 * b + part + 1)
                step(dve.tensor_scalar(NBH[b][:, part], NBH[b][:, part], 1e-12, None, ALU.max))
                step(dve.reciprocal(NBH[b][:, part], NBH[b][:, part]))
                step(tt(NBT[b][:, part], NBT[b][:, part], NBH[b][:, part], MUL))

            def scale_operands(b, part):
                r_, k_ = p0[:, 2 * b:2 * b + 2, PAD:PW], p0[:, 4 + 2 * b:6 + 2 * b, PAD:PW]
                if part == 0:
                    dve.wait_ge(S("r_e"), 4 * b + 4)
                    step(tt(ALPHA_[b][:], ALPHA_[b][:], NBT[b][:], MUL))
                    step(stt(NBT[b][:], NBT[b][:], -1.0, s_a[:], MUL, MUL))
                    step(tt(KH[b][:], k_, s_inv[:], MUL))
                    step(tt(NBH[b][:], NBT[b][:], s_inv[:], MUL))
                else:
                    dve.wait_ge(S("r_rk"), b + 1)
                    step(tt(r_, r_, s_fwd[:], MUL))
                    fwd = s_fwd[:].rearrange("p j (c t) -> p j c t", t=RC)
                    step(dve.tensor_copy(dend[:, b], fwd[:, :, :, RC - 1]))
                    step(tt(NBT[b][:], NBT[b][:], s_dec[:], MUL))
                    done(tt(k_, k_, s_dec[:], MUL), "r_ops")

            def bonus(b):
                for j in range(2):
                    dve.wait_ge(*made("rbon", 2 * b + j + 1))
                    done(tt(BON[b][:, j], bank(f"rbon{b}", j)[:], p0[:, 8 + 2 * b + j, PAD:PW], MUL), "rbon_out")

            for i in range(22):
                stg, n = PLACE0[i]
                tile = ORDER0[i]
                split(i + W_SLOTS)
                if i < 14:
                    dve.wait_ge(S("r_in"), i + 1)
                    cur = p0[:, tile, PAD + 1:PW]
                    done(stt(cur, bank(stg, n)[:, 0:T - 1], V("mu", tile), cur, MUL, ADD), "in_out")
                if i == 5:
                    scaled_keys(0)
                if i == 6:
                    running_decay(0)
                    keys(0)
                if i == 10:
                    normalised(0, 0)
                    normalised(0, 1)
                if i == 11:
                    scaled_keys(1)
                    scale_operands(0, 0)
                if i == 12:
                    scale_operands(0, 1)
                if i == 13:
                    bonus(0)
                if i == 14:
                    running_decay(1)
                    keys(1)
            split(FIRST["out0"] + W_SLOTS)
            normalised(1, 0)
            normalised(1, 1)
            scale_operands(1, 0)
            scale_operands(1, 1)

            def three(ap):
                return ap.rearrange("p (c t) -> p c t", t=RC)

            def convolution(n):
                j, k = divmod(n, 4)
                x_ = p0[:, 14 + j]
                if k == 0:
                    step(dve.tensor_scalar(lc[:, j], x_[:, 1:1 + T], V("lcw", j), V("lcb", j), MUL, ADD))
                else:
                    ins = stt(lc[:, j], x_[:, 1 + k:1 + k + T], V("lcw", 4 * k + j), lc[:, j], MUL, ADD)
                    if k < 3:
                        step(ins)
                    else:
                        done(ins, "l_conv")

            def masked_products(b):
                for n, (dst, mask) in enumerate([(M_[b], None), (XT_[b], m_lev[:, 0]), (PAK[b], m_strict[:]),
                                                 (PRB[b], m_incl[:]), (PRK[b], m_incl[:])]):
                    for j in range(2):
                        dve.wait_ge(*made("rprod", 10 * b + 2 * n + j + 1))
                        blk = dst[:].rearrange("p j (m u) -> p (j m) u", u=P)[:, :, j * RC:j * RC + RC]
                        src = three(bank(f"rprod{b}", 2 * n + j)[:])
                        if mask is None:
                            done(dve.tensor_copy(blk, src), "rprod_out")
                        else:
                            done(tt(blk, src, mid(mask, NRC), MUL), "rprod_out")
                        if 8 * b + n * 2 + j - 2 * b < 16 and n < 4:
                            convolution(8 * b + 2 * n + j)
                for j in range(2):
                    done(tt(three(XT_[b][:, j]), three(XT_[b][:, j]), mid(eye2[:], NRC), ADD), "r_x0")
                    step(tt(three(NBH[b][:, j]), three(M_[b][:, j]), mid(m_lev[:, 6], NRC), MUL))
                    step(tt(three(NBH[b][:, j]), three(NBH[b][:, j]), mid(eye2[:], NRC), ADD))

            masked_products(0)
            bonus(1)
            masked_products(1)

            def blocks(ap, n, upper):
                at = 0 if upper else n
                return ap.rearrange("p j (b u) -> p (j b) u", u=2 * n)[:, :, at:at + n]

            def level_y(b, v):
                n = 1 << v
                dve.wait_ge(S("yt_zero"), (0, 4 if b else 3, 4 if b else 3, 5 + b, 7 + b, 7 + b)[v])
                dve.wait_ge(*made("ryt", 2 * (v - 1) + b + 1))
                dst = yt_(b, v).rearrange("p j (g b u) -> p (j g) b u", b=32 // n, u=2 * n)[:, :, :, n:2 * n]
                mask = m_lev[:, v].rearrange("p (b u) -> p b u", u=2 * n)[:, :, n:2 * n]
                done(tt(dst, bank(f"ryt{b}_{v}", 0)[:].rearrange("p (g b n) -> p g b n", b=32 // n, n=n),
                        mask.unsqueeze(1).to_broadcast([P, 16, 32 // n, n]), MUL), "ryt_out")

            def level_z(b, v):
                n = 1 << v
                before = 4 * (v - 1) + (2 if v < 5 else 1) * b
                for m, (x_, upper) in enumerate([(NBH[b], True), (XT_[b], False)][0 if v < 5 else 1:]):
                    dve.wait_ge(*made("rz", before + (2 if v < 5 else 1)))
                    view = blocks(x_[:], n, upper)
                    done(tt(view, view, bank(f"rz{b}_{v}", m)[:].rearrange("p (b n) -> p b n", n=n), ADD), "rz_out")

            def lru_variance(j):
                dve.wait_ge(S("l_gx"), j + 1)
                dve.wait_ge(S("l_act"), 2 * j + 2)
                a_ = p0[:, 14 + j, PAD:PW]
                step(tt(li[:, j], a_, a_, MUL))
                done(stt(li[:, j], li[:, j], 1.0, lt[:], ADD, MUL), "l_var")

            def lru_scan(j):
                dve.wait_ge(S("l_std"), j + 1)
                a_ = p0[:, 14 + j, PAD:PW]
                step(tt(lc[:, j], lc[:, j], li[:, j], MUL))
                step(dve.tensor_tensor_scan(li[:, j], a_, lc[:, j], 0.0, MUL, ADD))
                if j == 0:
                    dve.wait_ge(S("l_gelu"), 4)
                done(tt(a_, li[:, j], p0[:, 18 + j, PAD:PW], MUL), "l_mix")

            for v in range(1, 6):
                for b in range(2):
                    level_y(b, v)
                if v >= 2:
                    lru_variance(v - 2)
                for b in range(2):
                    level_z(b, v)
                    if b == 0 and v >= 3:
                        lru_scan(v - 3)
            lru_scan(3)
            for b in range(2):
                for j in range(2):
                    dve.wait_ge(*made("rt", 8 + 4 * b + j + 1))
                    if j == 0:
                        dve.wait_ge(S("r_diag"), b + 1)
                    view = every_other(M_[b][:], j)
                    done(tt(view, view, bank(f"rat{b}", j)[:].rearrange("p (j m v) -> p j m v", j=2, v=RC), ADD), "rat_out")
                for j in range(2):
                    view = every_other(p0[:, 2 * b:2 * b + 2, PAD:PW], j)
                    dve.wait_ge(*made("rt", 8 + 4 * b + 2 + j + 1))
                    done(tt(view, view, bank(f"rrho{b}", j)[:].rearrange("p (j m v) -> p j m v", j=2, v=RC), ADD),
                         "rrho_out")

            def heads(ap):
                return ap.rearrange("p (h v) -> p h v", v=RD)

            for m in range(NT):
                mean, var = small[:, 16 + 8 * m:24 + 8 * m], small[:, 48 + 8 * m:56 + 8 * m]
                dve.wait_ge(S("ro_mm"), m + 1)
                for q in range(2):
                    step(dve.tensor_reduce(mean[:, 4 * q:4 * q + 4], heads(bank(f"ro{m}", q)[:, 0:256]), AX_X, ADD))
                step(dve.tensor_scalar(mean, mean, 1.0 / RD, None, MUL))
                for q in range(2):
                    done(tt(oall[:, m].rearrange("p (j q v) -> p q j v", q=2, v=RD)[:, q], heads(bank(f"ro{m}", q)[:, 0:256]),
                            bc(mean[:, 4 * q:4 * q + 4], RD), SUB), "ro_out")
                dve.wait_ge(S("r_osq"), m + 1)
                step(dve.tensor_reduce(var, heads(zsq[:, m % 2]), AX_X, ADD))
                done(dve.tensor_scalar(var, var, 1.0 / RD, GN_EPS, MUL, ADD), "r_gvar")
                dve.wait_ge(S("r_gstd"), m + 1)
                step(dve.reciprocal(var, var))
                done(tt(heads(oall[:, m]), heads(oall[:, m]), bc(var, RD), MUL), "r_gn")
            for i in range(4):
                dve.wait_ge(S("mix_hi"), i + 1)
                done(tt(act_lo[:, i], p0[:, YT0[i], PAD:PW], f(act_hi[:, i]), SUB), "mix_lo")
            for jj in range(4):
                y_ = p0[:, jj, PAD:PW]
                dve.wait_ge(S("rback_out"), jj + 1)
                step(tt(y_, y_, BON[jj // 2][:, jj % 2], ADD))
                if jj == 0:
                    dve.wait_ge(*made("rlora", 12))
                done(tt(y_, y_, bank("rg", jj)[:], MUL), "rg_out")
                if jj:
                    dve.wait_ge(S("mix_hi"), 4 + jj)
                    done(tt(act_lo[:, 3 + jj], p0[:, jj - 1, PAD:PW], f(act_hi[:, 3 + jj]), SUB), "mix_lo")
            dve.wait_ge(S("mix_hi"), 8)
            done(tt(act_lo[:, 7], p0[:, 3, PAD:PW], f(act_hi[:, 7]), SUB), "mix_lo")
            done(dve.tensor_copy(small[:, 255:256], small[:, 254:255]), "mix_done")

            def residual(stg, half, first, final):
                cols = slice(half * HALF, half * HALF + HALF)
                for t in range(NT):
                    if first:
                        ins = stt(h[:, t, cols], h[:, t, cols], ALPHA, bank(stg, half * NT + t)[:], MUL, ADD)
                    else:
                        ins = tt(h[:, t, cols], h[:, t, cols], bank(stg, half * NT + t)[:], ADD)
                    done(ins, FAMILY[stg] + "_out")
                    if final:
                        step(dve.bn_stats(lnst[:, t, 6 * half:6 * half + 6], h[:, t, cols]))

            def layer_norm(n):
                for t in range(NT):
                    step(dve.bn_aggr(lnmv[:, t], lnst[:, t]))
                done(dve.tensor_scalar(lnsd[:], lnmv[:, :, 1], LN_EPS, None, ADD), "ln_var")
                dve.wait_ge(S("ln_std"), n + 1)
                step(dve.reciprocal(lnsd[:], lnsd[:]))
                if n == 5:
                    dve.wait_ge(S("gb_in"), 16 * 6)
                for t in range(NT):
                    done(dve.tensor_scalar(h[:, t], h[:, t], lnmv[:, t, 0:1], lnsd[:, t:t + 1], SUB, MUL), "ln_rows")
                    if n == 5:
                        step(tt(h[:, t], h[:, t], gb[:, 0], MUL))
                        done(tt(h[:, t], h[:, t], gb[:, 1], ADD), "out_rows")

            def feature_lo(l, which, k):
                stg = f"lnt{l}_{which}"
                c = 8 * (3 * l + which) + k
                dve.wait_ge(*of(stg, "_hi", k + 1))
                tmp = stage[:, 6 + k % 2]
                step(dve.tensor_scalar(tmp, bank(stg, k)[:], V("lng", c), V("lnb", c), MUL, ADD))
                done(tt(act_lo[:, k], tmp, f(act_hi[:, k]), SUB), "lnt_out")

            def attention(l):
                dve.wait_ge(S("mem_hi"), l + 1)
                n8 = 8 * MEM
                done(tt(aux_lo[:].rearrange("p a t -> p (a t)")[:, 0:n8], stage[:].rearrange("p a t -> p (a t)")[:, 0:n8],
                        f(aux_hi[:].rearrange("p a t -> p (a t)")[:, 0:n8]), SUB), "mem_split")
                layer_norm(3 * l)
                for i in range(8):
                    chunk(f"k{l}", i)
                    dve.wait_ge(*of(f"k{l}", "_hi", i + 1))
                    done(tt(k_lo[:, i], bank(f"k{l}", i)[:, 0:MEM], f(k_hi[:, i]), SUB), "k_out")
                for half in range(2):
                    for i in range(4):
                        for k in range(4 * half + i + (half + i > 0), min(4 * half + i + 2, KD)):
                            feature_lo(l, 0, k)
                        chunk(f"v{l}", 4 * half + i)
                    for m in range(2):
                        cols = slice(half * HALF, half * HALF + HALF)
                        dve.wait_ge(*of(f"v{l}", "_hi", 2 * half + m + 1))
                        done(tt(v_lo[:, m, cols], bank(f"v{l}", 2 * half + m)[:], f(v_hi[:, m, cols]), SUB), "v_out")
                for i in range(8):
                    chunk(f"q{l}", i)
                    dve.wait_ge(*of(f"q{l}", "_hi", i + 1))
                    done(tt(aux_lo[:, i], bank(f"q{l}", i)[:], f(aux_hi[:, i]), SUB), "q_out")
                split(FIRST[f"wo{l}"] + W_SLOTS)

                def row_max(n):
                    dve.wait_ge(*of(f"s{l}", "_mm", n + 1))
                    step(dve.tensor_reduce(small[:, 160 + 2 * n:162 + 2 * n],
                                           bank(f"s{l}", n)[:].rearrange("p (q m) -> p q m", q=2), AX_X, ALU.max))
                    done(dve.tensor_scalar(small[:, 128 + 2 * n:130 + 2 * n], small[:, 160 + 2 * n:162 + 2 * n],
                                           -1.0 / 16, None, MUL), "p_max")

                def probs(n):
                    dve.wait_ge(*of(f"s{l}", "_out", n + 1))
                    step(dve.reciprocal(small[:, 176 + 2 * n:178 + 2 * n], small[:, 144 + 2 * n:146 + 2 * n]))
                    for q in range(2):
                        pr = stage[:, n, q * MEM:q * MEM + MEM]
                        ins = dve.tensor_scalar(pr, pr, small[:, 176 + 2 * n + q:177 + 2 * n + q], None, MUL)
                        if q:
                            done(ins, "p_ready")
                        else:
                            step(ins)

                for n in range(9):
                    if n < 8:
                        row_max(n)
                    if n:
                        probs(n - 1)
                for hp in range(2):
                    for t in range(NT):
                        dve.wait_ge(*of(f"pt{l}_{hp}", "_hi", t + 1))
                        dst = slice(t * P, t * P + P)
                        ins = tt(act_lo[:, 8:12, dst], bank(f"pt{l}_{hp}", t)[:].rearrange("p (a t) -> p a t", a=4),
                                 f(act_hi[:, 8:12, dst]), SUB)
                        done(ins, "pt_out")
                    for n in range(4):
                        dve.wait_ge(*of(f"pv{l}_{hp}", "_hi", n + 1))
                        i = 4 * hp + n
                        done(tt(act_lo[:, i], bank(f"pv{l}_{hp}", n)[:], f(act_hi[:, i]), SUB), "pv_out")
                dve.wait_ge(S("h_ready"), NT * (3 * l + 1))
                for half in range(2):
                    for i in range(4):
                        chunk(f"wo{l}", 4 * half + i)
                    residual(f"wo{l}", half, True, True)
                layer_norm(3 * l + 1)
                for k in range(KD):
                    feature_lo(l, 1, k)

            def mlp(l):
                for q in range(QUARTERS):
                    for i in range(8):
                        chunk(f"up{l}_{q}", i)
                        n = 8 * q + i
                        dve.wait_ge(*of(f"up{l}_{q}", "_out", i + 1))
                        done(tt(stage[:, 2 + n % 2], stage[:, n % 2], stage[:, n % 2], MUL), "up_sq")
                        dve.wait_ge(*of(f"up{l}_{q}", "_hi", i + 1))
                        done(tt(aux_lo[:, i], stage[:, 2 + n % 2], f(aux_hi[:, i]), SUB), "up_lo")
                    for half in range(2):
                        for i in range(4):
                            chunk(f"down{l}_{q}", 4 * half + i)
                        if q == 0 and half == 0:
                            dve.wait_ge(S("h_ready"), NT * (3 * l + 2))
                        residual(f"down{l}_{q}", half, q == 0, q == QUARTERS - 1)
                layer_norm(3 * l + 2)

            dve.wait_ge(S("h_in"), 16)
            for half in range(2):
                for i in range(4):
                    chunk("out0", 4 * half + i)
                residual("out0", half, True, True)
            attention(0)
            mlp(0)
            for k in range(KD):
                feature_lo(0, 2, k)
            def conf_taps(first, last):
                for n in range(first, last):
                    k, j = divmod(n, 3)
                    src = cu[:, j, CP - (CONF_TAPS - 1) + k:CP - (CONF_TAPS - 1) + k + T]
                    w_ = V("ccw", 4 * k + j)
                    if k == 0:
                        step(dve.tensor_scalar(cacc[:, j], src, w_, V("ccb", j), MUL, ADD), 2)
                    else:
                        step(stt(cacc[:, j], src, w_, cacc[:, j], MUL, ADD), 2)

            def ssd_gated(m):
                dve.wait_ge(S("s_sig"), m + 1)
                done(tt(p1[:, XS + m, PAD:PW], sconv[:, m % 2], gtmp[:, 2], MUL), "s_conv")

            def ssd_conv(m):
                x_, d_ = p1[:, XS + m], sconv[:, m % 2]
                dve.wait_ge(*out_sem("in1", XS + m + 1))
                step(dve.tensor_scalar(d_, x_[:, 1:1 + T], V("scw", m), V("scb", m), MUL, ADD))
                for k in range(1, 4):
                    ins = stt(d_, x_[:, 1 + k:1 + k + T], V("scw", 12 * k + m), d_, MUL, ADD)
                    if k < 3:
                        step(ins)
                    else:
                        done(ins, "s_cv")

            step(dve.memset(p1[:, :, 0:PAD], 0.0))
            done(dve.memset(cu[:, :, 0:CP], 0.0), "c_zero")
            N_TAPS = 3 * CONF_TAPS
            for i in range(29):
                split(FIRST["in1"] + i + W_SLOTS)
                if i == 8:
                    for j in (3, 0, 1, 2):
                        dve.wait_ge(*out_sem("in1", 8))
                        done(tt(cu[:, j, CP:CP + T], p1[:, j, PAD:PW], p1[:, 4 + j, PAD:PW], MUL), "c_u")
                if i >= 8:
                    conf_taps(min(4 * (i - 8), N_TAPS), min(4 * (i - 7), N_TAPS))
                if i >= 12 and i % 2 == 0 and i <= 26:
                    m = (i - 12) // 2
                    ssd_conv(m)
                    if m:
                        ssd_gated(m - 1)
                if i == 20:
                    dve.wait_ge(S("s_sp"), 1)
                    dve.wait_ge(S("masks"), 2)
                    raw = p1[0:16, DT, PAD:PW]
                    step(stt(sdt[:, 0], raw, 0.0, sdt[:, 0], ALU.max, ADD))
                    step(dve.tensor_scalar(raw, sdt[:, 0], small[0:16, 200:201], -1.0, MUL, MUL))
                    done(dve.tensor_tensor_scan(sdt[:, 1], m_scan[0:16], raw, 0.0, MUL, ADD), "s_acum")
            split(FIRST["out1"] + W_SLOTS)
            ssd_gated(7)
            conf_taps(4 * 21, N_TAPS)
            for j in range(3):
                done(dve.tensor_copy(small[:, 255:256], small[:, 254:255]), "c_conv")
            done(dve.tensor_copy(small[:, 255:256], small[:, 254:255]), "c_conv")
            for m in range(2):
                dve.wait_ge(*made("stok", m + 1))
                done(dve.tensor_copy(stm[:, m].rearrange("p c h -> p (c h)"), bank("stok", m)[:, 0:64]), "stok_out")
            cmean = p1[:, 0, PAD:PW]
            dve.wait_ge(*made("c", 1))
            done(dve.tensor_scalar(cmean, bank("cmean", 0)[:], 1.0 / 512, None, MUL), "cmean_out")
            dve.wait_ge(S("c_conv3"), CONF_TAPS - 1)
            for j in range(4):
                done(tt(cacc[:, j], cacc[:, j], cmean, SUB), "c_cent")
            dve.wait_ge(S("slast_out"), 1)
            done(tt(stm[:, 2], stm[:, 3], stm[:, 1], SUB), "s_dte")
            dve.wait_ge(S("s_dtee"), 1)
            for c in range(NSC):
                for q in range(2):
                    dve.wait_ge(*made("sxt", 2 * c + q + 1))
                    dst = xdt[:, c, q * 512:q * 512 + 512].rearrange("p (h v) -> p h v", v=64)
                    step(tt(dst, bank("sxt", 2 * c + q)[:].rearrange("p (h v) -> p h v", v=64),
                            bc(stm[:, 0, c, 8 * q:8 * q + 8], 64), MUL))
                    done(tt(xdtd[:, c, q * 512:q * 512 + 512].rearrange("p (h v) -> p h v", v=64), dst,
                            bc(stm[:, 2, c, 8 * q:8 * q + 8], 64), MUL), "sxt_out")
            dve.wait_ge(*made("c", 2))
            done(dve.tensor_scalar(c_std, bank("cvar", 0)[:], 1.0 / 512, LN_EPS, MUL, ADD), "cvar_out")
            for g in range(2):
                dve.wait_ge(*made("scb", g + 1))
                done(tt(cbt[:, :, g], bank("scb", g)[:].rearrange("p (c t) -> p c t", c=NSC), mid(m_tri[:], NSC), MUL),
                     "scb_out")
            dve.wait_ge(S("c_stdd"), 1)
            step(dve.reciprocal(c_std, c_std))
            for j in range(4):
                step(tt(cacc[:, j], cacc[:, j], c_std, MUL))
                done(dve.tensor_scalar(cacc[:, j], cacc[:, j], V("clg", j), V("clb", j), MUL, ADD), "c_norm")
            for c in range(NSC - 1):
                for g in range(2):
                    dve.wait_ge(*made("sst", 2 * c + g + 1))
                    nxt = prev[:, c, g * 512:g * 512 + 512].rearrange("p (h v) -> p h v", v=64)
                    src = bank("sst", 2 * c + g)[:].rearrange("p (h v) -> p h v", v=64)
                    if c == 0:
                        done(dve.tensor_copy(nxt, src), "sst_out")
                    else:
                        cur = prev[:, c - 1, g * 512:g * 512 + 512].rearrange("p (h v) -> p h v", v=64)
                        step(tt(nxt, cur, bc(stm[:, 3, c, 8 * g:8 * g + 8], 64), MUL))
                        done(tt(nxt, nxt, src, ADD), "sst_out")
            for j in range(4):
                dve.wait_ge(S("c_sig"), j + 1)
                done(tt(p1[:, YT1[j], PAD:PW], cacc[:, j], p1[:, 4 + j, PAD:PW], MUL), "mix_f1")

            def differences(hp):
                for n in (2 * hp, 2 * hp + 1):
                    dve.wait_ge(*made("sbc", n + 1))
                    if hp >= 2:
                        dve.wait_ge(*made("sy", hp - 1))
                    for c in range(NSC):
                        cols = slice(c * SC, c * SC + SC)
                        ins = dve.tensor_scalar(mt(n)[:, cols], bank(f"sbc{hp}", n % 2)[:, cols],
                                                stm[:, 1, c, n:n + 1], 0.0, SUB, ALU.min)
                        if c < NSC - 1:
                            step(ins, 3)
                        else:
                            done(ins, "s_diff")

            def scores(hp):
                for n in (2 * hp, 2 * hp + 1):
                    dve.wait_ge(S("s_exp"), n + 1)
                    m3 = mt(n).rearrange("p (c t) -> p c t", c=NSC)
                    done(tt(m3, m3, cbt[:, :, hp // 4], MUL), "s_mt")

            def rms(g):
                r_ = p1[:, BS + g, PAD:PW]
                dve.wait_ge(S("s_rstd"), g + 1)
                step(dve.reciprocal(r_, r_))
                for j in range(4):
                    z_ = p1[:, ZS + 4 * g + j, PAD:PW]
                    done(stt(z_, z_, V("sng", 4 * g + j), r_, MUL, MUL), "mix_f1")

            def mean_square(g):
                dve.wait_ge(*made("srms", g + 1))
                done(dve.tensor_scalar(p1[:, BS + g, PAD:PW], bank(f"srms{g}", 0)[:], 1.0 / 512, LN_EPS, MUL, ADD),
                     "srms_out")

            differences(0)
            scores(0)
            for hp in range(8):
                if hp < 7:
                    differences(hp + 1)
                    scores(hp + 1)
                dve.wait_ge(*made("sy", hp + 1))
                xs, z_ = p1[:, XS + hp, PAD:PW], p1[:, ZS + hp, PAD:PW]
                done(stt(xs, xs, V("dsk", hp), bank(f"sy{hp}", 0)[:], MUL, ADD), "sy_out")
                dve.wait_ge(S("s_z"), hp + 1)
                done(tt(z_, xs, z_, MUL), "s_y")
                if hp == 6:
                    mean_square(0)
            mean_square(1)
            rms(0)
            for i in range(4):
                dve.wait_ge(S("mix_hi"), 8 + i + 1)
                done(tt(act_lo[:, i], p1[:, YT1[i], PAD:PW], f(act_hi[:, i]), SUB), "mix_lo")
            rms(1)
            for i in range(4, 12):
                dve.wait_ge(S("mix_hi"), 8 + i + 1)
                done(tt(act_lo[:, i], p1[:, YT1[i], PAD:PW], f(act_hi[:, i]), SUB), "mix_lo")
            done(dve.tensor_copy(small[:, 255:256], small[:, 254:255]), "mix_done")
            for half in range(2):
                for i in range(6):
                    chunk("out1", 6 * half + i)
                if half == 0:
                    dve.wait_ge(S("h_ready"), NT * 3)
                residual("out1", half, True, True)
            attention(1)
            mlp(1)


_OUT = (1, T, D)


def kernel(**inputs):
    import numpy as _np
    import concourse.bacc as _bacc
    from concourse import mybir as _mybir
    from concourse.bass_utils import run_bass_kernel_spmd as _run

    a = {k: _np.asarray(v) for k, v in inputs.items()}

    def by_feature(w):
        k, m = w.shape
        return w.reshape(k // P, P, m // P, P).transpose(2, 1, 0, 3).reshape(m // P, P, CHUNK)

    def by_token(w):
        k, _ = w.shape
        return w.reshape(k // 256, 2, P, 2, HALF).transpose(3, 0, 2, 1, 4).reshape(k // P, P, CHUNK)

    def padded(w, rows, cols):
        z = _np.zeros((rows, cols), w.dtype)
        z[:w.shape[0], :w.shape[1]] = w
        return z

    stream = []
    for l in range(2):
        if l == 0:
            w_in, w_out = a["ev_w_in"][0], a["ev_w_out"][0]
            stream += [by_feature(w_in)[_np.array(ORDER0)],
                       by_token(_np.concatenate([w_out[HALF:], w_out[:HALF]]))]
        else:
            w_in = a["od_w_in"][0]
            stream += [by_feature(w_in[:, 0:D]), by_feature(padded(w_in[:, 3584:], D, P)),
                       by_feature(w_in[:, 2 * D:3584]), by_feature(w_in[:, D:2 * D]), by_token(a["od_w_out"][0])]
        stream += [by_feature(a["xa_wk"][l]), by_token(a["xa_wv"][l]), by_feature(a["xa_wq"][l]),
                   by_token(a["xa_wo"][l])]
        for q in range(QUARTERS):
            cut = slice(q * D, q * D + D)
            stream += [by_feature(a["ffn_w1"][l][:, cut]), by_token(a["ffn_w2"][l][cut])]

    def tiles(v):
        v = v.reshape(-1, v.shape[-1])
        return v.reshape(v.shape[0] * v.shape[1] // P, P).T

    vecs = {"mu": a["ev_mu"], "w0": a["ev_w0"], "a0": a["ev_a0"], "kk": a["ev_k_k"], "ka": a["ev_k_a"],
            "rk": a["ev_r_k"].reshape(1, -1), "gng": a["ev_gn_g"], "gnb": a["ev_gn_b"],
            "lcw": a["ev_lru_conv_w"][0], "lcb": a["ev_lru_conv_b"], "lba": a["ev_lru_ba"], "lbx": a["ev_lru_bx"],
            "lam": a["ev_lru_lam"], "ccw": a["od_cf_conv_w"][0], "ccb": a["od_cf_conv_b"],
            "clg": a["od_cf_ln_g"], "clb": a["od_cf_ln_b"], "scw": a["od_ssm_conv_w"][0],
            "lng": _np.concatenate([a[f"ln_{w}_g"][l] for l in range(2) for w in ("mix", "mem", "ffn")])[None],
            "lnb": _np.concatenate([a[f"ln_{w}_b"][l] for l in range(2) for w in ("mix", "mem", "ffn")])[None],
            "scb": a["od_ssm_conv_b"], "sng": a["od_ssm_norm_g"], "dsk": _np.repeat(a["od_d_skip"], 64, axis=1)}
    table = [tiles(vecs[n]) for n, _ in VEC_TILES[:-2]]
    table += [padded(a["od_dt_bias"].T, P, 1), padded(a["od_a_log"].T, P, 1)]
    lora = _np.stack([_np.concatenate([a["ev_w2"][0], a["ev_a2"][0]]), a["ev_g2"][0]], axis=1)
    lru = _np.zeros((P, 8, P), _np.float32)
    for m, name in enumerate(["ev_lru_wa", "ev_lru_wx"]):
        for n in range(8):
            rows = slice(64 * (n % 2), 64 * (n % 2) + 64)
            lru[rows, 4 * m + n // 2, rows] = a[name][0, n]
    rows = [_np.stack([a[f"ln_{w}_g"][l], a[f"ln_{w}_b"][l]]) for l in range(2) for w in ("mix", "mem", "ffn")]
    x, mem = a["x"][0], a["mem"][0]
    arrays = {
        "x_tok": x.reshape(NT, P, D).transpose(1, 0, 2),
        "x_feat": x.T.reshape(KD, P, T).transpose(1, 0, 2),
        "mem_feat": mem.T.reshape(KD, P, MEM).transpose(1, 0, 2).reshape(P, KD * MEM),
        "weights": _np.concatenate(stream),
        "vectors": _np.concatenate(table, axis=1),
        "lora": lora,
        "lru_w": lru,
        "ln_rows": _np.stack(rows),
    }
    arrays = {k: _np.ascontiguousarray(v) for k, v in arrays.items()}
    nc = _bacc.Bacc("TRN2", target_bir_lowering=False, num_devices=1)
    args = [nc.dram_tensor(k, v.shape, _mybir.dt.float32, kind="ExternalInput").ap() for k, v in arrays.items()]
    out = nc.dram_tensor("out", _OUT, _mybir.dt.float32, kind="ExternalOutput").ap()
    build(nc, *args, out.rearrange("a (t p) d -> p (a t) d", p=P))
    r = _run(nc, [arrays], core_ids=[0])
    return r.results[0]["out"]
```

```python
from contextlib import ExitStack

import concourse.bass as bass
from concourse import mybir

F32 = mybir.dt.float32
F32R = mybir.dt.float32r
ALU = mybir.AluOpType
ACT = mybir.ActivationFunctionType
AX_X = mybir.AxisListType.X

P = 128
T = 512
D = 1024
KD = D // P
NT = T // P
MEM = 256
HALF = 512
CHUNK = 1024
W_SLOTS = 3
PAD = 4
PW = PAD + T
ALPHA = 4.0 ** 0.25
LN_EPS = 1e-5
GN_EPS = 64e-5
HEADS_XA = 4
D_FF = 4096
QUARTERS = 4
RC = 64
NRC = T // RC
RD = 64
SC = 128
NSC = T // SC
CONF_TAPS = 31
POOL_TAPS = 15
CONF_SUMS = CONF_TAPS - 1 + POOL_TAPS - 1
CP = 32
NEG_EXP_HALF = -0.6065306597126334

ORDER0 = [12, 13, 0, 1, 4, 5, 8, 9, 2, 3, 6, 7, 10, 11, 14, 15, 16, 17, 18, 19, 20, 21]
IN0 = [("in0_0", 2), ("in0_1", 4), ("in0_2", 4), ("in0_3", 2), ("in0_4", 2), ("in0_5", 2), ("in0_6", 2), ("in0_7", 4)]
PLACE0 = [(_name, _i) for _name, _count in IN0 for _i in range(_count)]

STREAM = []
for _l in range(2):
    STREAM += IN0 if _l == 0 else [("in1", 29)]
    STREAM += [(f"out{_l}", 8 if _l == 0 else 12),
               (f"k{_l}", 8), (f"v{_l}", 8), (f"q{_l}", 8), (f"wo{_l}", 8)]
    for _q in range(QUARTERS):
        STREAM += [(f"up{_l}_{_q}", 8), (f"down{_l}_{_q}", 8)]
FIRST = {}
_n = 0
for _name, _count in STREAM:
    FIRST[_name] = _n
    _n += _count
N_CHUNKS = _n

VEC_TILES = [("mu", 14), ("w0", 4), ("a0", 4), ("kk", 4), ("ka", 4), ("rk", 4), ("gng", 4), ("gnb", 4),
             ("lcw", 16), ("lcb", 4), ("lba", 4), ("lbx", 4), ("lam", 4),
             ("ccw", CONF_TAPS * 4), ("ccb", 4), ("clg", 4), ("clb", 4),
             ("scw", 48), ("scb", 12), ("sng", 8), ("dsk", 8), ("lng", 48), ("lnb", 48), ("dtb", 1), ("alog", 1)]
VEC = {}
_n = 0
for _name, _count in VEC_TILES:
    VEC[_name] = _n
    _n += _count
N_VEC = _n

TILES = []
for _l in range(2):
    if _l == 0:
        TILES += [IN0[0], IN0[1], ("rdec0", 2), ("ra0", 2), IN0[2], ("rss0", 2), IN0[3], ("rbon0", 2), IN0[4],
                  IN0[5], ("rdec1", 2), ("ra1", 2), IN0[6], ("rss1", 2), IN0[7], ("rprod0", 10), ("rtok0", 8), ("rw0", 2),
                  ("rbon1", 2), ("rprod1", 10), ("rtok1", 8), ("rw1", 2), ("lru", 8)]
        for _v in range(1, 6):
            TILES += [(f"ryt0_{_v}", 1), (f"ryt1_{_v}", 1)]
            TILES += [(f"rz0_{_v}", 2 if _v < 5 else 1), (f"rz1_{_v}", 2 if _v < 5 else 1)]
        TILES += [("rgt0", 2), ("rtw0", 2), ("rgt1", 2), ("rtw1", 2), ("rat0", 2), ("rrho0", 2), ("rat1", 2),
                  ("rrho1", 2)]
        for _c in range(NRC):
            TILES += [(f"rst{_c}", 1)] * (_c < NRC - 1) + [(f"ro{_c // 2}", 2)] * (_c % 2 == 0)
        TILES += [("rg", 4), ("out0", 4), ("rback", 4), ("out0", 4)]
    else:
        TILES += [("in1", 25), ("stok", 2), ("in1", 2), ("slast", 1), ("in1", 2), ("cmean", 1), ("sxt", 8), ("cvar", 1), ("sbt", 2),
                  ("scb", 2), ("sst", 6), ("sbc0", 2)]
        for _h in range(8):
            TILES += [(f"sbc{_h + 1}", 2)] * (_h < 7) + [(f"sy{_h}", 1)] + [("srms0", 1)] * (_h == 5)
        TILES += [("srms1", 1), ("out1", 8)]
    TILES += [(f"k{_l}", 8), (f"lnt{_l}_0", 8), (f"v{_l}", 4), (f"q{_l}", 8), (f"s{_l}", 8),
              (f"pt{_l}_0", 4), (f"pt{_l}_1", 4), (f"pv{_l}_0", 4), (f"pv{_l}_1", 4), (f"wo{_l}", 8),
              (f"lnt{_l}_1", 8)]
    for _q in range(QUARTERS):
        TILES += [(f"up{_l}_{_q}", 8), (f"down{_l}_{_q}", 8)]
    if _l == 0:
        TILES += [("lnt0_2", 8)]
TILE_AT = {}
TILE_OWNER = []
_made = {}
for _name, _count in TILES:
    for _i in range(_made.get(_name, 0), _made.get(_name, 0) + _count):
        TILE_AT[_name, _i] = len(TILE_OWNER)
        TILE_OWNER.append((_name, _i + 1))
    _made[_name] = _made.get(_name, 0) + _count
FAMILY, BEFORE = {}, {}
_seen = {}
for _name, _count in TILES:
    _kind = _name.rstrip("0123456789_")
    FAMILY[_name] = _kind
    BEFORE.setdefault(_name, _seen.get(_kind, 0))
    _seen[_kind] = _seen.get(_kind, 0) + _count

GROUP = {"rdec": "rlora", "ra": "rlora", "rg": "rlora", "rgt": "rt", "rtw": "rt", "rat": "rt", "rrho": "rt",
         "cmean": "c", "cvar": "c"}
for _name in "rss rbon rprod rtok rw lru ryt rz rback stok slast sxt sbt scb sst sbc sy srms".split():
    GROUP[_name] = _name
MADE = {_kind: [] for _kind in GROUP.values()}
_n = 0
for _name, _i in TILE_OWNER:
    if FAMILY[_name] in GROUP:
        _n += 1
        MADE[GROUP[FAMILY[_name]]].append(_n)


def build(nc, x_tok, x_feat, mem_feat, weights, vectors, lora, lru_w, ln_rows, out):
    with ExitStack() as ctx:
        base = (nc.sbuf_base + 31) // 32 * 32
        place = {"at": base}

        def sb(name, shape, dt=F32, at=None):
            size = 4
            for n in shape[1:]:
                size *= n
            if at is None:
                at = place["at"]
                place["at"] = at + (size + 31) // 32 * 32
            return nc.alloc_sbuf_tensor_at(name, shape, dt, offset=at)

        w_raw = sb("w_raw", [P, W_SLOTS, CHUNK])
        w_hi = sb("w_hi", [P, W_SLOTS, CHUNK], F32R)
        w_lo = sb("w_lo", [P, W_SLOTS, CHUNK], F32R)
        h_at = place["at"]
        h = sb("h", [P, NT, D])
        act_at = place["at"]
        act_hi = sb("act_hi", [P, 12, T], F32R)
        act_lo = sb("act_lo", [P, 12, T], F32R)
        aux_at = place["at"]
        aux_hi = sb("aux_hi", [P, 8, T], F32R)
        aux_lo = sb("aux_lo", [P, 8, T], F32R)
        k_hi = sb("k_hi", [P, 8, MEM], F32R)
        k_lo = sb("k_lo", [P, 8, MEM], F32R)
        v_hi = sb("v_hi", [P, 2, D], F32R)
        v_lo = sb("v_lo", [P, 2, D], F32R)
        stage = sb("stage", [P, 8, T])
        mix_end = place["at"]
        gb_at = place["at"]
        gb = sb("gb", [P, 2, D])
        vec = sb("vec", [P, N_VEC])
        ident = sb("ident", [P, P])
        ones = sb("ones", [P, P])
        bdones = sb("bdones", [P, P])
        lastrow = sb("lastrow", [P, P])
        eye2 = sb("eye2", [P, RC])
        m_strict = sb("m_strict", [P, RC])
        m_incl = sb("m_incl", [P, RC])
        m_tri = sb("m_tri", [P, SC])
        m_lev = sb("m_lev", [P, 7, RC])
        m_scan = sb("m_scan", [P, T])
        small = sb("small", [P, 256])
        lnst = sb("lnst", [P, NT, 12])
        lnmv = sb("lnmv", [P, NT, 2])
        lnsd = sb("lnsd", [P, NT])
        eps = sb("eps", [P, 1])
        omu = sb("omu", [P, 14])
        dend = sb("dend", [P, 2, 2, NRC])
        lora_at = place["at"]
        lora_sb = sb("lora_sb", [P, 2, T])
        lru_at = place["at"]
        lru_sb = sb("lru_sb", [P, 8, P])

        p0 = sb("p0", [P, 22, PW], at=aux_at)
        after_p0 = (aux_at + 22 * PW * 4 + 31) // 32 * 32

        def pair(name, region, i):
            return sb(name, [P, 2, T], at=region + i * 4096)

        ALPH = [pair("alpha0", after_p0, 0), pair("alpha1", after_p0, 1)]
        NBH = [pair("nbh0", after_p0, 2), pair("nbh1", after_p0, 5)]
        KH = [pair("kh0", after_p0, 3), pair("kh1", after_p0, 6)]
        BON = [pair("bonus0", after_p0, 4), pair("bonus1", after_p0, 7)]
        NBT = [pair("nbt0", h_at, 0), pair("nbt1", h_at, 1)]
        M_ = [pair("m0", act_at, 0), pair("m1", act_at, 4)]
        XT_ = [pair("xt0", h_at, 2), pair("xt1", h_at, 3)]
        PAK = [pair("pak0", act_at, 1), pair("pak1", act_at, 5)]
        PRB = [pair("prb0", act_at, 6), pair("prb1", act_at, 10)]
        PRK = [pair("prk0", act_at, 7), pair("prk1", act_at, 11)]
        s_a, s_dec, s_cum, s_fwd, s_inv = XT_[1], M_[1], PAK[1], PRB[1], PRK[1]
        hall = sb("hall", [P, 4, T], at=act_at + 2 * 4096)
        oall = sb("oall", [P, 4, T], at=after_p0)
        zsq = KH[0]
        lc = sb("lc", [P, 4, T], at=gb_at)
        li = sb("li", [P, 4, T], at=act_at + 8 * 4096)
        lt = sb("lt", [P, T], at=after_p0 + 8 * 4096)
        assert after_p0 + 8 * 4096 + 2048 <= mix_end
        YT0 = [14, 15, 16, 17, 0, 1, 2, 3]

        def yt_(b, v):
            return hall[:, 2 * b:2 * b + 2] if v % 2 else KH[b][:]

        def rows_(c):
            return slice(RC * (c % 2), RC * (c % 2) + RC)

        def split_cols(j, c):
            at = j * 256 + (c // 2) * RC
            return slice(at, at + RC)

        def every_other(ap, s):
            return ap.rearrange("p j (m u) -> p j m u", u=P)[:, :, :, s * RC:s * RC + RC]

        def cols_(c, q):
            at = (c // 2) * P + q * RC
            return slice(at, at + RC)

        p1 = sb("p1", [P, 29, PW], at=aux_at)
        after_p1 = (aux_at + 29 * PW * 4 + 31) // 32 * 32
        cu = sb("cu", [P, 4, CP + T], at=after_p1)
        cacc = sb("cacc", [P, 4, T], at=after_p1 + 4 * (CP + T) * 4)
        cacc2 = sb("cacc2", [P, T], at=act_at + 8 * T * 4)
        sconv = sb("sconv", [P, 2, T], at=after_p1 + 4 * (CP + T) * 4 + 8192)
        pconv = sb("pconv", [P, 2, T], at=lru_at)
        gtmp = sb("gtmp", [P, 4, T], at=gb_at)
        sdt = sb("sdt", [16, 2, T], at=lora_at)
        c_std = sb("c_std", [P, T], at=lru_at)[:]
        DT, XS, BS, CS, ZS = 8, 9, 17, 19, 21
        YT1 = [0, 1, 2, 3] + [ZS + i for i in range(8)]
        xdt = sb("xdt", [P, NSC, D], at=act_at)
        xdtd = sb("xdtd", [P, NSC, D], at=act_at + 16384)
        prev = sb("prev", [P, NSC - 1, D], at=act_at + 36864)
        bt = sb("bt", [P, NSC, 256], at=after_p1)
        cbt = sb("cbt", [P, NSC, 2, SC], at=after_p1 + 4096)
        cs = sb("cs", [P, 4, T], at=act_at + 16384)
        mts = [sb("mt01", [P, 2, T], at=act_at + 24576), sb("mt23", [P, 2, T], at=act_at + 32768)]
        stm = sb("stm", [P, 4, NSC, 16])

        def mt(n):
            return mts[n % 4 // 2][:, n % 2]

        assert place["at"] <= nc.sbuf_usable_end and after_p1 + 20992 <= mix_end

        ps = [ctx.enter_context(nc.psum_tensor(f"bank{i}", [P, 512], F32)) for i in range(8)]

        sems = {}

        def S(name):
            if name not in sems:
                sems[name] = ctx.enter_context(nc.semaphore(name))
            return sems[name]

        def V(name, i):
            c = VEC[name] + i
            return vec[:, c:c + 1]

        def bank(stg, i):
            return ps[TILE_AT[stg, i] % 8]

        def of(stg, suffix, n):
            return S(FAMILY[stg] + suffix), BEFORE[stg] + n

        def made(kind, n):
            return S("mixer_mm"), MADE[kind][n - 1]

        def out_sem(stg, n):
            return of(stg, "_out", n)

        landed = [S(f"w_landed{i}") for i in range(W_SLOTS)]
        block = ctx.enter_context(nc.Block())

        def bc(ap, n):
            return ap.unsqueeze(2).to_broadcast([ap.shape[0], ap.shape[1], n])

        def mid(ap, n):
            return ap.unsqueeze(1).to_broadcast([ap.shape[0], n, ap.shape[1]])

        @block.sync
        def _(sp):
            sp.dma_start(stage[:, 0:2], x_feat[:, 0:2]).then_inc(S("x_in0"), 16)
            sp.dma_start(w_raw[:, 0], weights[0]).then_inc(landed[0], 16)
            for i in range(1, 4):
                sp.dma_start(stage[:, 2 * i:2 * i + 2], x_feat[:, 2 * i:2 * i + 2]).then_inc(S(f"x_in{i}"), 16)
            sp.dma_start(w_raw[:, 1], weights[1]).then_inc(landed[1], 16)
            sp.dma_start(vec[:], vectors).then_inc(S("vec_in"), 16)
            sp.dma_start(lora_sb[:], lora).then_inc(S("const_in"), 16)
            sp.dma_start(lru_sb[:], lru_w).then_inc(S("const_in"), 16)
            ln_at = {FIRST["out0"] + 6: 0, FIRST["wo0"] + 3: 1, FIRST["down0_3"] + 1: 2,
                     FIRST["out1"] + 3: 3, FIRST["wo1"] + 3: 4, FIRST["down1_3"] + 1: 5}
            for c in range(2, N_CHUNKS):
                if c >= W_SLOTS:
                    sp.wait_ge(S("w_split"), c - W_SLOTS + 1)
                sp.dma_start(w_raw[:, c % W_SLOTS], weights[c]).then_inc(landed[c % W_SLOTS], 16)
                if c == FIRST["out0"] + 2:
                    sp.wait_ge(S("rst_mm"), 2 * NRC - 2)
                    sp.dma_start(h[:], x_tok).then_inc(S("h_in"), 16)
                if c in ln_at:
                    n = ln_at[c]
                    if n == 0:
                        sp.wait_ge(S("mix_done"), 1)
                    if n:
                        sp.wait_ge(S("ln_used"), n)
                    if n == 3:
                        sp.wait_ge(S("s_bc"), 4)
                        sp.wait_ge(S("s_conv"), 8)
                    sp.dma_start(gb[:], ln_rows[n:n + 1].to_broadcast([P, 2, D])).then_inc(S("gb_in"), 16)
                for l in range(2):
                    if c == FIRST[f"out{l}"] + 6:
                        sp.wait_ge(S("mix_done"), l + 1)
                        sp.dma_start(stage[:].rearrange("p a t -> p (a t)")[:, 0:8 * MEM], mem_feat)\
                            .then_inc(S("mem_in"), 16)
            for t in range(NT):
                sp.wait_ge(S("out_rows"), t + 1)
                sp.dma_start(out[:, t], h[:, t]).then_inc(S("stored"), 16)
            sp.wait_ge(S("stored"), 16 * NT)

        @block.gpsimd
        def _(pool):
            def fill(t, value):
                pool.memset(t, value).then_inc(S("pool_step"), 1)
                fill.n += 1
                pool.wait_ge(S("pool_step"), fill.n)
            fill.n = 0

            def sel(t, op, base, pattern, mult, fillv, inner=None):
                pool.affine_select(out=t, in_=t, compare_op=op, fill=fillv, base=base, pattern=pattern,
                                   channel_multiplier=mult).then_inc(S("pool_step"), 1)
                fill.n += 1
                pool.wait_ge(S("pool_step"), fill.n)

            fill(ident[:], 0.0)
            sel(ident[:], ALU.not_equal, 0, [[-1, P]], 1, 1.0)
            fill(ones[:], 1.0)
            fill(bdones[:], 0.0)
            fill(bdones[0:64, 0:64], 1.0)
            fill(bdones[64:128, 64:128], 1.0)
            fill(lastrow[:], 0.0)
            sel(lastrow[:], ALU.not_equal, -(P - 1), [[0, P]], 1, 1.0)
            fill(m_tri[:], 1.0)
            sel(m_tri[:], ALU.is_ge, 0, [[1, SC]], -1, 0.0)
            fill(eye2[:], 0.0)
            sel(eye2[:], ALU.not_equal, 0, [[-1, RC]], 1, 1.0)
            sel(eye2[:], ALU.not_equal, -RC, [[-1, RC]], 1, 1.0)
            fill(m_strict[:], 1.0)
            fill(m_incl[:], 1.0)
            for q in range(2):
                rows = slice(RC * q, RC * q + RC)
                sel(m_strict[rows], ALU.is_gt, 0, [[1, RC]], -1, 0.0)
                sel(m_incl[rows], ALU.is_ge, 0, [[1, RC]], -1, 0.0)
            fill(m_lev[:], 1.0)
            for v in range(6):
                n = 1 << v
                for q in range(2):
                    rows = slice(RC * q, RC * q + RC)
                    view = m_lev[rows, v].rearrange("p (b u) -> p b u", u=2 * n)
                    sel(view, ALU.is_ge, 0, [[-2 * n, RC // (2 * n)], [0, 2 * n]], 1, 0.0)
                    sel(view, ALU.is_ge, n - 1, [[2 * n, RC // (2 * n)], [0, 2 * n]], -1, 0.0)
                    sel(view, ALU.is_ge, -n, [[0, RC // (2 * n)], [1, 2 * n]], 0, 0.0)
            for q in range(2):
                rows = slice(RC * q, RC * q + RC)
                view = m_lev[rows, 6].rearrange("p (b u) -> p b u", u=2)
                sel(view, ALU.is_equal, -1, [[-2, RC // 2], [0, 2]], 1, 0.0)
                sel(view, ALU.is_ge, 0, [[0, RC // 2], [-1, 2]], 0, 0.0)
            fill(m_scan[:], 1.0)
            fill(m_scan[:].rearrange("p (c t) -> p c t", t=RC)[:, :, 0:1], 0.0)
            fill(eps[:], LN_EPS)
            pool.memset(small[:], 0.0).then_inc(S("masks"), 1)

            def affine(n):
                pool.wait_ge(S("gb_in"), 16 * (n + 1))
                l, which = divmod(n, 3)
                pool.wait_ge(*of(f"lnt{l}_{which}", "_mm", 8))
                for t in range(NT):
                    pool.tensor_tensor(h[:, t], h[:, t], gb[:, 0], ALU.mult).then_inc(S("pool_step"), 1)
                    fill.n += 1
                    pool.wait_ge(S("pool_step"), fill.n)
                    pool.tensor_tensor(h[:, t], h[:, t], gb[:, 1], ALU.add).then_inc(S("h_ready"), 1)
                pool.wait_ge(S("h_ready"), NT * (n + 1))
                pool.memset(small[:, 253:254], 0.0).then_inc(S("ln_used"), 1)
                pool.wait_ge(S("ln_used"), n + 1)

            def differences(b):
                pool.wait_ge(S("r_cum"), b + 1)
                pool.tensor_tensor(s_dec[:], s_cum[:], s_dec[:], ALU.subtract).then_inc(S("r_diff"), 1)
                cum = s_cum[:].rearrange("p j (c t) -> p (j c) t", t=RC)
                pool.tensor_tensor(KH[b][:].rearrange("p j (c t) -> p (j c) t", t=RC),
                                   bc(dend[:, b].rearrange("p j c -> p (j c)"), RC), cum, ALU.subtract)\
                    .then_inc(S("r_diff"), 1)

            def r_times_k(b):
                pool.wait_ge(S("r_k"), b + 1)
                pool.tensor_tensor(BON[b][:], p0[:, 2 * b:2 * b + 2, PAD:PW], p0[:, 4 + 2 * b:6 + 2 * b, PAD:PW],
                                   ALU.mult).then_inc(S("r_rk"), 1)

            def clear(ap):
                pool.memset(ap, 0.0).then_inc(S("yt_zero"), 1)

            differences(0)
            r_times_k(0)
            differences(1)
            r_times_k(1)
            g_ = p0[:, 18:22, PAD:PW]

            def gelu(ins):
                gelu.n += 1
                ins.then_inc(S("l_gelu"), 1)
                pool.wait_ge(S("l_gelu"), gelu.n)
            gelu.n = 0
            pool.wait_ge(S("l_gact"), 1)
            gelu(pool.tensor_scalar(li[:], li[:], 0.044715, 1.0, ALU.mult, ALU.add))
            gelu(pool.tensor_tensor(li[:], li[:], g_, ALU.mult))
            clear(yt_(0, 1))
            clear(yt_(1, 1))
            pool.wait_ge(*made("rprod", 10))
            clear(yt_(0, 2))
            pool.wait_ge(S("l_gact"), 2)
            gelu(pool.tensor_scalar(li[:], li[:], 1.0, 0.5, ALU.add, ALU.mult))
            gelu(pool.tensor_tensor(g_, g_, li[:], ALU.mult))
            pool.wait_ge(*made("rprod", 20))
            clear(yt_(1, 2))
            for j in range(4):
                pool.wait_ge(S("lru_out"), 2 * j + 2)
                pool.tensor_tensor(lc[:, j], lc[:, j], li[:, j], ALU.mult).then_inc(S("l_gx"), 1)
                if j in (1, 2):
                    for b in range(2):
                        pool.wait_ge(*made("rz", 4 * j - 2 + 2 * b))
                        clear(yt_(b, j + 2))
            for b in range(2):
                pool.wait_ge(*made("ryt", 9 + b))
                pool.tensor_tensor(M_[b][:].rearrange("p j (c t) -> p (j c) t", t=RC),
                                   bc(dend[:, b].rearrange("p j c -> p (j c)"), RC), mid(eye2[:], 2 * NRC),
                                   ALU.mult).then_inc(S("r_diag"), 1)

            pool.wait_ge(S("mix_done"), 1)
            fill(m_scan[:], 1.0)
            pool.memset(m_scan[:].rearrange("p (c t) -> p c t", t=SC)[:, :, 0:1], 0.0).then_inc(S("masks"), 1)
            for n in range(3):
                affine(n)
            for n in range(1, CONF_SUMS + 1):
                last = n < CONF_TAPS
                acc = cacc[:, 3] if last else cacc2[:]
                pool.wait_ge(S("c_prod"), n + 1 if last else n + 2)
                pool.tensor_tensor(acc, acc, gtmp[:, n % 2], ALU.add).then_inc(S("c_conv3"), 1)
                pool.wait_ge(S("c_conv3"), n)

            def gated(m):
                pool.wait_ge(S("s_sigbc"), m + 1)
                pool.tensor_tensor(p1[:, BS + m, PAD:PW], pconv[:, m % 2], gtmp[:, 3], ALU.mult).then_inc(S("s_bc"), 1)
                pool.wait_ge(S("s_bc"), m + 1)

            for m in range(4):
                for k in range(1, 4):
                    pool.wait_ge(S("s_prod"), 4 * m + k + 1)
                    pool.tensor_tensor(pconv[:, m % 2], pconv[:, m % 2], gtmp[:, (3 * m + k) % 2], ALU.add)\
                        .then_inc(S("s_padd"), 1)
                    pool.wait_ge(S("s_padd"), 3 * m + k)
                gated(m)
            for n in range(8):
                c, q = divmod(n, 2)
                pool.wait_ge(S("sxt_out"), n + 1)
                cols = slice(q * 512, q * 512 + 512)
                pool.tensor_tensor(xdtd[:, c, cols].rearrange("p (h v) -> p h v", v=64),
                                   xdt[:, c, cols].rearrange("p (h v) -> p h v", v=64),
                                   bc(stm[:, 2, c, 8 * q:8 * q + 8], 64), ALU.mult).then_inc(S("s_xdtd"), 1)
            for hp in range(8):
                for n in (2 * hp, 2 * hp + 1):
                    pool.wait_ge(S("sbc_out"), n + 1)
                    pool.tensor_tensor(cs[:, n % 4], cs[:, n % 4], p1[:, CS + hp // 4, PAD:PW], ALU.mult)\
                        .then_inc(S("s_cs"), 1)
                pool.wait_ge(S("s_zsig"), hp + 1)
                z_ = p1[:, ZS + hp, PAD:PW]
                pool.tensor_tensor(z_, z_, p1[:, 4 + hp % 4, PAD:PW], ALU.mult).then_inc(S("s_z"), 1)
            for n in range(3, 5):
                affine(n)

        @block.tensor
        def _(pe):
            def take(stg, i):
                n = TILE_AT[stg, i]
                if n >= 8:
                    owner, k = TILE_OWNER[n - 8]
                    pe.wait_ge(*out_sem(owner, k))
                return ps[n % 8]

            def mm3(o, whi, wlo, xhi, xlo, first, last):
                pe.matmul(o, whi, xlo, start=first, stop=False)
                pe.matmul(o, wlo, xhi, start=False, stop=False)
                return pe.matmul(o, whi, xhi, start=False, stop=last)

            def feature_major(stg, count, xhi, xlo, n, ready=None, between=None):
                for i in range(count):
                    if between and i in between:
                        between[i]()
                    c = FIRST[stg] + i
                    s = c % W_SLOTS
                    o = take(stg, i)
                    pe.wait_ge(S("w_split"), c + 1)
                    for k in range(KD):
                        if ready and i == 0:
                            pe.wait_ge(*ready(k))
                        cols = slice(k * P, k * P + P)
                        last = mm3(o[:, 0:n], w_hi[:, s, cols], w_lo[:, s, cols], xhi[:, k, 0:n], xlo[:, k, 0:n],
                                   k == 0, k == KD - 1)
                    last.then_inc(S("chunk_done"), 1)

            def token_major(stg, tiles, kts, xhi, xlo, ready=None, between=None):
                for half in range(2):
                    o = [take(stg, half * tiles + t) for t in range(tiles)]
                    for i in range(kts // 2):
                        if between and (half, i) == (0, between[0]):
                            between[1]()
                        c = FIRST[stg] + half * (kts // 2) + i
                        s = c % W_SLOTS
                        pe.wait_ge(S("w_split"), c + 1)
                        end = i == kts // 2 - 1
                        if ready and half == 0:
                            pe.wait_ge(*ready(2 * i))
                        order = [(kk, t) for t in range(tiles) for kk in range(2)] if end else \
                            [(kk, t) for kk in range(2) for t in range(tiles)]
                        for n, (kk, t) in enumerate(order):
                            k = 2 * i + kk
                            if ready and half == 0 and k % 2 and (n == 1 or not end and t == 0):
                                pe.wait_ge(*ready(k))
                            cols = slice(kk * HALF, kk * HALF + HALF)
                            tok = slice(t * P, t * P + P)
                            last = mm3(o[t][:, 0:HALF], xhi[:, k, tok], xlo[:, k, tok], w_hi[:, s, cols],
                                       w_lo[:, s, cols], k == 0, k == kts - 1)
                            if end and kk and t < tiles - 1:
                                last.then_inc(S("tokens_mm"), 1)
                        last.then_inc(S("chunk_done"), 1)

            def each(fn):
                for m in range(NT):
                    for q in range(2):
                        for c in (2 * m, 2 * m + 1):
                            last = fn(c, q, rows_(c), slice(RD * q, RD * q + RD), slice(c * RC, c * RC + RC),
                                      cols_(c, q))
                return last

            def low_rank(b):
                if b:
                    pe.wait_ge(S("r_ops"), 1)
                else:
                    pe.wait_ge(S("r_lora"), 2)
                    pe.wait_ge(S("masks"), 1)
                    pe.wait_ge(S("const_in"), 32)
                for name, rows in (("rdec", slice(0, 64)), ("ra", slice(64, 128))):
                    for j in range(2):
                        o = take(f"{name}{b}", j)
                        col = slice((2 * b + j) * P, (2 * b + j) * P + P)
                        pe.matmul(o[:], lora_sb[rows, 0, col], p0[rows, 12, PAD:PW], start=True, stop=True)\
                            .then_inc(S("mixer_mm"), 1)

            def norms(b):
                pe.wait_ge(S("r_kksq"), b + 1)
                for j in range(2):
                    o = take(f"rss{b}", j)
                    pe.matmul(o[:], bdones[:], s_fwd[:, j], start=True, stop=True).then_inc(S("mixer_mm"), 1)

            def bonus(b):
                pe.wait_ge(S("r_rkr"), 2 * b + 2)
                for j in range(2):
                    o = take(f"rbon{b}", j)
                    pe.matmul(o[:], bdones[:], BON[b][:, j], start=True, stop=True).then_inc(S("mixer_mm"), 1)

            def operands(b):
                r_, k_, v_ = (p0[:, 4 * m + 2 * b:4 * m + 2 * b + 2, PAD:PW] for m in range(3))
                return ALPH[b], NBH[b], KH[b], r_, NBT[b], k_, v_

            def within_chunks(b):
                alpha, nbh, kh, rho, nbt, kt, v_ = operands(b)
                pe.wait_ge(S("r_ops"), b + 1)
                for n, (lhs, rhs) in enumerate([(alpha, nbh), (nbh, alpha), (kh, alpha), (nbh, rho), (kh, rho)]):
                    for q in range(2):
                        o = take(f"rprod{b}", 2 * n + q)
                        feat = slice(RD * q, RD * q + RD)
                        for j in range(2):
                            for c in range(NRC):
                                cf = slice(c * RC, c * RC + RC)
                                last = pe.matmul(o[rows_(c), split_cols(j, c)], lhs[feat, j, cf], rhs[feat, j, cf],
                                                 start=True, stop=True)
                        last.then_inc(S("mixer_mm"), 1)
                for n, src in enumerate([alpha, nbt, kt, v_]):
                    for j in range(2):
                        o = take(f"rtok{b}", 2 * n + j)
                        for m in range(NT):
                            last = pe.transpose(o[:, m * P:m * P + P], src[:, j, m * P:m * P + P], ident[:])
                        last.then_inc(S("mixer_mm"), 1)
                pe.wait_ge(*out_sem(f"rtok{b}", 8))
                for j in range(2):
                    o = take(f"rw{b}", j)
                    each(lambda c, q, tok, feat, cf, ct: pe.matmul(o[tok, ct], PAK[b][tok, j, ct], v_[tok, j, ct],
                                                                   start=True, stop=True)).then_inc(S("mixer_mm"), 1)

            def halves(ap, n, upper):
                return ap.rearrange("p (b u) -> p b u", u=2 * n)[:, :, 0:n] if upper else \
                    ap.rearrange("p (b u) -> p b u", u=2 * n)[:, :, n:2 * n]

            def compact(o, j, c, q, n):
                at = j * 256 + ((c // 2) * 2 + q) * 32
                return o[rows_(c), at:at + 32].rearrange("p (b n) -> p b n", n=n)

            def level_y(b, v):
                n = 1 << v
                o = take(f"ryt{b}_{v}", 0)
                pe.wait_ge(*(out_sem(f"rz{b}_{v - 1}", 2) if v > 1 else (S("r_x0"), 2 * b + 2)))
                for j in range(2):
                    last = each(lambda c, q, tok, feat, cf, ct: pe.matmul(
                        compact(o, j, c, q, n), M_[b][tok, j, ct], halves(XT_[b][tok, j, ct], n, False),
                        start=True, stop=True))
                last.then_inc(S("mixer_mm"), 1)

            def level_z(b, v):
                n = 1 << v
                x_, y_ = NBH[b], yt_(b, v)
                pe.wait_ge(*out_sem(f"ryt{b}_{v}", 1))
                if v < 5:
                    o = take(f"rz{b}_{v}", 0)
                    for j in range(2):
                        last = each(lambda c, q, tok, feat, cf, ct: pe.matmul(
                            compact(o, j, c, q, n), y_[tok, j, ct], halves(x_[tok, j, ct], n, True),
                            start=True, stop=True))
                    last.then_inc(S("mixer_mm"), 1)
                o = take(f"rz{b}_{v}", 1 if v < 5 else 0)
                for j in range(2):
                    last = each(lambda c, q, tok, feat, cf, ct: pe.matmul(
                        compact(o, j, c, q, n), x_[tok, j, ct], halves(y_[tok, j, ct], n, False),
                        start=True, stop=True))
                last.then_inc(S("mixer_mm"), 1)

            def transitions(b, part):
                if part:
                    pe.wait_ge(*out_sem(f"rgt{b}", 2))
                    for name, right in (("rat", NBT[b]), ("rrho", PRB[b])):
                        for s in range(2):
                            o = take(f"{name}{b}", s)
                            tok = slice(RC * s, RC * s + RC)
                            for j in range(2):
                                for c in range(s, NRC, 2):
                                    for q in range(2):
                                        ct = cols_(c, q)
                                        last = pe.matmul(o[RD * q:RD * q + RD, split_cols(j, c)], KH[b][tok, j, ct],
                                                         right[tok, j, ct], start=True, stop=True)
                            last.then_inc(S("mixer_mm"), 1)
                    return
                for j in range(2):
                    o = take(f"rgt{b}", j)
                    each(lambda c, q, tok, feat, cf, ct: pe.matmul(
                        o[tok, ct], XT_[b][tok, j, ct], ALPH[b][tok, j, ct], start=True, stop=True))\
                        .then_inc(S("mixer_mm"), 1)
                for j in range(2):
                    o = take(f"rtw{b}", j)
                    pe.wait_ge(*out_sem(f"rw{b}", j + 1))
                    each(lambda c, q, tok, feat, cf, ct: pe.matmul(
                        o[tok, ct], XT_[b][tok, j, ct], PAK[b][tok, j, ct], start=True, stop=True))\
                        .then_inc(S("mixer_mm"), 1)

            def scan():
                both = [(jj, q, slice(RD * q, RD * q + RD)) for jj in range(4) for q in range(2)]
                for b in range(2):
                    pe.wait_ge(*out_sem(f"rtw{b}", 2))
                    pe.wait_ge(*out_sem(f"rat{b}", 2))
                    pe.wait_ge(*out_sem(f"rrho{b}", 2))
                banks = {}

                def from_tokens(c):
                    tok = rows_(c)
                    if c < NRC - 1:
                        banks["h", c] = take(f"rst{c}", 0)
                    if c % 2 == 0:
                        for q in range(2):
                            banks["o", c // 2, q] = take(f"ro{c // 2}", q)
                    for jj, q, feat in both:
                        b, j = divmod(jj, 2)
                        kt, v_ = operands(b)[5:7]
                        ct, oc = cols_(c, q), slice(jj * RD, jj * RD + RD)
                        if c < NRC - 1:
                            o = banks["h", c]
                            pe.matmul(o[feat, oc], kt[tok, j, ct], v_[tok, j, ct], start=(jj == 0), stop=False)
                            pe.matmul(o[feat, oc], NBT[b][tok, j, ct], NBH[b][tok, j, ct], start=False,
                                      stop=(c == 0 and jj == 3))
                        o = banks["o", c // 2, q]
                        pe.matmul(o[tok, oc], PRB[b][tok, j, ct], NBH[b][tok, j, ct], start=(jj == 0), stop=False)
                        last = pe.matmul(o[tok, oc], PRK[b][tok, j, ct], v_[tok, j, ct], start=False,
                                         stop=(c == 0 and jj == 3))
                    last.then_inc(S("rst_mm"), 1)

                def from_state(c):
                    tok, cf = rows_(c), slice(c * RC, c * RC + RC)
                    pe.wait_ge(S("rst_mm"), 2 * c)
                    pe.wait_ge(*out_sem(f"rst{c - 1}", 1))
                    if c < NRC - 1:
                        for jj, q, feat in both:
                            b, j = divmod(jj, 2)
                            last = pe.matmul(banks["h", c][feat, jj * RD:jj * RD + RD], M_[b][feat, j, cf],
                                             hall[feat, jj, cf], start=False, stop=(jj == 3))
                        last.then_inc(S("rst_mm"), 1)
                    for jj, q, feat in both:
                        b, j = divmod(jj, 2)
                        last = pe.matmul(banks["o", c // 2, q][tok, jj * RD:jj * RD + RD],
                                         operands(b)[3][feat, j, cf], hall[feat, jj, cf], start=False, stop=(jj == 3))
                    if c % 2:
                        last.then_inc(S("ro_mm"), 1)

                from_tokens(0)
                for c in range(1, NRC):
                    from_tokens(c)
                    from_state(c)

            def even_output():
                for j in range(4):
                    o = take("rg", j)
                    pe.matmul(o[:], lora_sb[:, 1, j * P:j * P + P], p0[:, 13, PAD:PW], start=True, stop=True)\
                        .then_inc(S("mixer_mm"), 1)

            def even_back():
                pe.wait_ge(S("r_gn"), 4)
                for jj in range(4):
                    o = take("rback", jj)
                    for m in range(NT):
                        last = pe.transpose(o[:, m * P:m * P + P], oall[:, m, jj * P:jj * P + P], ident[:])
                    last.then_inc(S("mixer_mm"), 1)

            def lru():
                pe.wait_ge(S("l_conv"), 4)
                for j in range(4):
                    for m in range(2):
                        o = take("lru", 2 * j + m)
                        pe.matmul(o[:], lru_sb[:, 4 * m + j], lc[:, j], start=True, stop=True)\
                            .then_inc(S("mixer_mm"), 1)

            def even_mixer():
                def project(n):
                    feature_major(IN0[n][0], IN0[n][1], act_hi, act_lo, T,
                                  ready=(lambda k: (S("x_split"), k // 2 + 1)) if n == 0 else None)

                project(0)
                project(1)
                low_rank(0)
                project(2)
                norms(0)
                project(3)
                bonus(0)
                project(4)
                project(5)
                low_rank(1)
                project(6)
                norms(1)
                project(7)
                within_chunks(0)
                bonus(1)
                within_chunks(1)
                lru()
                for v in range(1, 6):
                    for b in range(2):
                        level_y(b, v)
                    for b in range(2):
                        level_z(b, v)
                for b in range(2):
                    pe.wait_ge(*out_sem(f"rz{b}_5", 1))
                    transitions(b, 0)
                for b in range(2):
                    transitions(b, 1)
                scan()
                even_output()

            def decay_rows(hp):
                for q in range(2):
                    hd = 2 * hp + q
                    o = take(f"sbc{hp}", q)
                    pe.matmul(o[:], ident[0:16, hd:hd + 1].to_broadcast([16, P]), sdt[:, 1, :], start=True, stop=True)\
                        .then_inc(S("mixer_mm"), 1)

            def sum_squares(g):
                o = take(f"srms{g}", 0)
                for j in range(4):
                    pe.wait_ge(S("s_ysq"), 4 * g + j + 1)
                    last = pe.matmul(o[:], ones[:], p1[:, XS + 4 * g + j, PAD:PW], start=(j == 0), stop=(j == 3))
                last.then_inc(S("mixer_mm"), 1)

            def dt_tokens():
                pe.wait_ge(S("s_acum"), 1)
                for m in range(2):
                    o = take("stok", m)
                    for c in range(NSC):
                        last = pe.transpose(o[:, c * 16:c * 16 + 16], sdt[:, m, c * SC:c * SC + SC], ident[0:16, 0:16])
                    last.then_inc(S("mixer_mm"), 1)

            def dt_last():
                o = take("slast", 0)
                pe.wait_ge(*out_sem("stok", 2))
                pe.matmul(o[:, 0:64], lastrow[:], stm[:, 1].rearrange("p c h -> p (c h)"), start=True, stop=True)\
                    .then_inc(S("mixer_mm"), 1)

            def odd_mixer():
                pe.wait_ge(S("c_conv"), 1)
                pe.wait_ge(S("c_conv3"), CONF_SUMS)
                o = take("cmean", 0)
                for j in range(4):
                    last = pe.matmul(o[:], ones[:], cacc[:, j], start=(j == 0), stop=(j == 3))
                last.then_inc(S("mixer_mm"), 1)
                pe.wait_ge(S("s_conv"), 8)
                for c in range(NSC):
                    for q in range(2):
                        o = take("sxt", 2 * c + q)
                        for j in range(4):
                            last = pe.transpose(o[:, j * P:j * P + P],
                                                p1[:, XS + 4 * q + j, PAD + c * SC:PAD + c * SC + SC], ident[:])
                        last.then_inc(S("mixer_mm"), 1)
                o = take("cvar", 0)
                for j in range(4):
                    pe.wait_ge(S("c_sq"), j + 1)
                    last = pe.matmul(o[:], ones[:], p1[:, 4 + j, PAD:PW], start=(j == 0), stop=(j == 3))
                last.then_inc(S("mixer_mm"), 1)
                pe.wait_ge(S("s_bc"), 4)
                for q in range(2):
                    o = take("sbt", q)
                    for c in range(2):
                        for g in range(2):
                            n = 2 * c + g
                            last = pe.transpose(o[:, n * P:n * P + P],
                                                p1[:, BS + g, PAD + (2 * q + c) * SC:PAD + (2 * q + c + 1) * SC], ident[:])
                    last.then_inc(S("mixer_mm"), 1)
                for g in range(2):
                    o = take("scb", g)
                    for c in range(NSC):
                        cols = slice(PAD + c * SC, PAD + c * SC + SC)
                        last = pe.matmul(o[:, c * SC:c * SC + SC], p1[:, BS + g, cols], p1[:, CS + g, cols],
                                         start=True, stop=True)
                    last.then_inc(S("mixer_mm"), 1)
                pe.wait_ge(*out_sem("sbt", 2))
                pe.wait_ge(S("s_xdtd"), 8)
                for c in range(NSC - 1):
                    for g in range(2):
                        o = take("sst", 2 * c + g)
                        pe.matmul(o[:], bt[:, c, g * P:g * P + P], xdtd[:, c, g * 512:g * 512 + 512],
                                  start=True, stop=True).then_inc(S("mixer_mm"), 1)
                decay_rows(0)
                for hp in range(8):
                    if hp < 7:
                        decay_rows(hp + 1)
                    if hp == 0:
                        pe.wait_ge(*out_sem("sst", 6))
                    o = take(f"sy{hp}", 0)
                    for q in range(2):
                        hd = 2 * hp + q
                        pe.wait_ge(S("s_mt"), hd + 1)
                        pe.wait_ge(S("s_cs"), hd + 1)
                        for c in range(NSC):
                            rows = slice(64 * q, 64 * q + 64)
                            cols = slice(c * SC, c * SC + SC)
                            last = pe.matmul(o[rows, cols], xdt[:, c, hd * 64:hd * 64 + 64], mt(hd)[:, cols],
                                             start=True, stop=(c == 0))
                            if c:
                                last = pe.matmul(o[rows, cols], prev[:, c - 1, hd * 64:hd * 64 + 64],
                                                 cs[:, hd % 4, cols], start=False, stop=True)
                    last.then_inc(S("mixer_mm"), 1)
                    if hp == 5:
                        sum_squares(0)

            def to_features(l, which):
                n = 3 * l + which
                for t in range(NT):
                    if t < NT - 1:
                        pe.wait_ge(S("ln_rows"), (NT - 1) * n + t + 1)
                    else:
                        pe.wait_ge(S("ln_last"), n + 1)
                    for k in range(KD):
                        o = take(f"lnt{l}_{which}", k) if t == 0 else bank(f"lnt{l}_{which}", k)
                        last = pe.transpose(o[:, t * P:t * P + P], h[:, t, k * P:k * P + P], ident[:])
                        if t == NT - 1:
                            last.then_inc(S("lnt_mm"), 1)

            def attention(l):
                pe.wait_ge(S("mem_split"), l + 1)
                memv = [a[:].rearrange("p a t -> p (a t)")[:, 0:8 * MEM].rearrange("p (a t) -> p a t", a=8)
                        for a in (aux_hi, aux_lo)]
                feature_major(f"k{l}", 8, memv[0], memv[1], MEM)
                to_features(l, 0)
                token_major(f"v{l}", 2, KD, memv[0], memv[1])
                feature_major(f"q{l}", 8, act_hi, act_lo, T, ready=lambda k: of(f"lnt{l}_0", "_out", k + 1))
                pe.wait_ge(*out_sem(f"q{l}", 8))
                pe.wait_ge(*out_sem(f"k{l}", 8))
                for hp in range(2):
                    for t in range(NT):
                        o = take(f"s{l}", 4 * hp + t)
                        tok = slice(t * P, t * P + P)
                        for q in range(2):
                            hd = 2 * hp + q
                            for k in range(2):
                                last = mm3(o[:, q * MEM:q * MEM + MEM], aux_hi[:, 2 * hd + k, tok],
                                           aux_lo[:, 2 * hd + k, tok], k_hi[:, 2 * hd + k], k_lo[:, 2 * hd + k],
                                           k == 0, k == 1)
                        last.then_inc(S("s_mm"), 1)
                pe.wait_ge(*out_sem(f"v{l}", 4))
                for hp in range(2):
                    for t in range(NT):
                        pe.wait_ge(S("p_ready"), 8 * l + 4 * hp + t + 1)
                        o = take(f"pt{l}_{hp}", t)
                        for q in range(2):
                            for m in range(2):
                                n = 2 * q + m
                                last = pe.transpose(o[:, n * P:n * P + P],
                                                    stage[:, 4 * hp + t, q * MEM + m * P:q * MEM + m * P + P], ident[:])
                        last.then_inc(S("pt_mm"), 1)
                for hp in range(2):
                    pe.wait_ge(*out_sem(f"pt{l}_{hp}", 4))
                    for q in range(2):
                        for dt in range(2):
                            o = take(f"pv{l}_{hp}", 2 * q + dt)
                            col = slice((2 * hp + q) * 256 + dt * P, (2 * hp + q) * 256 + dt * P + P)
                            for m in range(2):
                                last = mm3(o[:], v_hi[:, m, col], v_lo[:, m, col], act_hi[:, 4 + 4 * hp + 2 * q + m],
                                           act_lo[:, 4 + 4 * hp + 2 * q + m], m == 0, m == 1)
                            last.then_inc(S("pv_mm"), 1)
                pe.wait_ge(*out_sem(f"pv{l}_1", 4))
                token_major(f"wo{l}", NT, KD, act_hi, act_lo)

            def mlp(l):
                for q in range(QUARTERS):
                    feature_major(f"up{l}_{q}", 8, act_hi, act_lo, T, 
                                  ready=(lambda k: of(f"lnt{l}_1", "_out", k + 1)) if q == 0 else None)
                    token_major(f"down{l}_{q}", NT, KD, aux_hi, aux_lo, 
                                ready=lambda k, q=q: of(f"up{l}_{q}", "_lo", k + 1))

            for l in range(2):
                if l == 0:
                    even_mixer()
                else:
                    feature_major("in1", 29, act_hi, act_lo, T, ready=lambda k: of("lnt0_2", "_out", k + 1),
                                  between={25: dt_tokens, 27: dt_last})
                    odd_mixer()
                token_major(f"out{l}", NT, 8 if l == 0 else 12, act_hi, act_lo,
                            ready=lambda k, l=l: (S("mix_lo"), 8 * l + k + 1),
                            between=(1, lambda: sum_squares(1)) if l else (2, even_back))
                attention(l)
                to_features(l, 1)
                mlp(l)
                if l == 0:
                    to_features(0, 2)

        @block.scalar
        def _(act):
            n_split = [0]
            n_step = [0]

            def step(ins):
                n_step[0] += 1
                ins.then_inc(S("act_step"), 1)
                act.wait_ge(S("act_step"), n_step[0])

            counts = {"in_out": 14}

            def done(ins, name):
                counts[name] = counts.get(name, 0) + 1
                ins.then_inc(S(name), 1)
                act.wait_ge(S(name), counts[name])

            def split(upto):
                while n_split[0] < min(upto, N_CHUNKS):
                    c = n_split[0]
                    s = c % W_SLOTS
                    act.wait_ge(landed[s], 16 * (c // W_SLOTS + 1))
                    if c >= W_SLOTS:
                        act.wait_ge(S("chunk_done"), c - W_SLOTS + 1)
                    act.activation(w_hi[:, s], w_raw[:, s], ACT.Copy).then_inc(S("w_hi_done"), 1)
                    n_split[0] += 1

            def chunk(stg, i):
                c = FIRST[stg] + i
                split(c + W_SLOTS)
                act.wait_ge(S("chunk_done"), c + 1)

            def ahead(stg, i):
                split(FIRST[stg] + i + W_SLOTS)

            def copy_hi(stg, i, dst, n=T):
                done(act.activation(dst, bank(stg, i)[:, 0:n], ACT.Copy), FAMILY[stg] + "_hi")

            for i in range(4):
                act.wait_ge(S(f"x_in{i}"), 16)
                done(act.activation(act_hi[:, 2 * i:2 * i + 2], stage[:, 2 * i:2 * i + 2], ACT.Copy), "x_hi")
                if i in (0, 3):
                    split(1 + i // 3)
            act.wait_ge(S("vec_in"), 16)
            step(act.activation(omu[:], vec[:, VEC["mu"]:VEC["mu"] + 14], ACT.Identity, bias=1.0, scale=-1.0))

            def gates(b):
                if b:
                    act.wait_ge(S("r_ops"), 1)
                for j in range(2):
                    act.wait_ge(*made("rlora", 4 * b + j + 1))
                    done(act.activation(s_dec[:, j], bank(f"rdec{b}", j)[:], ACT.Sigmoid, bias=V("w0", 2 * b + j)),
                         "rdec_out")
                for j in range(2):
                    act.wait_ge(*made("rlora", 4 * b + 2 + j + 1))
                    done(act.activation(s_a[:, j], bank(f"ra{b}", j)[:], ACT.Sigmoid, bias=V("a0", 2 * b + j)),
                         "ra_out")

            def squares(b):
                act.wait_ge(S("r_kk"), b + 1)
                done(act.activation(s_fwd[:], NBT[b][:], ACT.Square), "r_kksq")

            def norms(b):
                for j in range(2):
                    act.wait_ge(*made("rss", 2 * b + j + 1))
                    done(act.activation(NBH[b][:, j], bank(f"rss{b}", j)[:], ACT.Sqrt), "rss_out")

            def exponentials(b):
                act.wait_ge(S("r_diff"), 2 * b + 1)
                done(act.activation(ALPH[b][:], s_dec[:], ACT.Exp, scale=NEG_EXP_HALF), "r_e")
                done(act.activation(s_inv[:], s_cum[:], ACT.Exp, scale=-NEG_EXP_HALF), "r_e")
                done(act.activation(s_fwd[:], s_cum[:], ACT.Exp, scale=NEG_EXP_HALF), "r_e")
                act.wait_ge(S("r_diff"), 2 * b + 2)
                done(act.activation(s_dec[:], KH[b][:], ACT.Exp, scale=NEG_EXP_HALF), "r_e")

            def bonus(b):
                act.wait_ge(S("r_rk"), b + 1)
                for j in range(2):
                    done(act.activation(BON[b][:, j], BON[b][:, j], ACT.Copy, scale=V("rk", 2 * b + j)), "r_rkr")

            for i in range(22):
                stg, n = PLACE0[i]
                tile = ORDER0[i]
                chunk(stg, n)
                if i < 14:
                    done(act.activation(p0[:, tile, PAD:PW], bank(stg, n)[:], ACT.Identity, bias=0.0,
                                        scale=omu[:, tile:tile + 1]), "r_in")
                else:
                    act.wait_ge(S("in_out"), 14)
                    done(act.activation(p0[:, tile, PAD:PW], bank(stg, n)[:], ACT.Copy), "in_out")
                if i == 1:
                    act.wait_ge(S("in_out"), 2)
                    done(act.activation(p0[0:64, 12, PAD:PW], p0[0:64, 12, PAD:PW], ACT.Tanh), "r_lora")
                    done(act.activation(p0[:, 13, PAD:PW], p0[:, 13, PAD:PW], ACT.Sigmoid), "r_lora")
                if i == 5:
                    gates(0)
                if i == 6:
                    squares(0)
                if i == 9:
                    norms(0)
                    exponentials(0)
                if i == 10:
                    bonus(0)
                if i == 15:
                    gates(1)
                    squares(1)
                if i == 17:
                    norms(1)
                if i == 18:
                    exponentials(1)
                if i == 19:
                    bonus(1)
                if i == 21:
                    done(act.activation(li[:], p0[:, 18:22, PAD:PW], ACT.Square), "l_gact")
            split(FIRST["out0"] + W_SLOTS)

            def tokens(b):
                k_, v_ = (p0[:, 4 * m + 2 * b:4 * m + 2 * b + 2, PAD:PW] for m in (1, 2))
                act.wait_ge(S("rbon_out"), 2 * b + 2)
                for n in range(8):
                    act.wait_ge(*made("rtok", 8 * b + n + 1))
                    dst = (ALPH[b], NBT[b], k_, v_)[n // 2]
                    done(act.activation(dst[:, n % 2], bank(f"rtok{b}", n)[:], ACT.Copy), "rtok_out")
                for j in range(2):
                    act.wait_ge(*made("rw", 2 * b + j + 1))
                    done(act.activation(PAK[b][:, j], bank(f"rw{b}", j)[:], ACT.Copy), "rw_out")

            tokens(0)
            act.wait_ge(S("l_gelu"), 2)
            done(act.activation(li[:], li[:], ACT.Tanh, scale=0.7978845608028654), "l_gact")
            tokens(1)
            act.wait_ge(S("masks"), 1)
            step(act.activation(small[:, 80:84], vec[:, VEC["lam"]:VEC["lam"] + 4], ACT.Exp, scale=-1.0))
            step(act.activation(small[:, 80:84], small[:, 80:84], ACT.Ln, bias=1.0))
            step(act.activation(small[:, 80:84], small[:, 80:84], ACT.Copy, scale=-8.0))
            act.wait_ge(S("l_gelu"), 4)
            for j in range(4):
                a_ = p0[:, 14 + j, PAD:PW]
                act.wait_ge(*made("lru", 2 * j + 2))
                done(act.activation(a_, bank("lru", 2 * j)[:], ACT.Sigmoid, bias=V("lba", j)), "lru_out")
                done(act.activation(li[:, j], bank("lru", 2 * j + 1)[:], ACT.Sigmoid, bias=V("lbx", j)), "lru_out")
            for j in range(4):
                lam = small[:, 80 + j:81 + j]
                a_ = p0[:, 14 + j, PAD:PW]
                if j:
                    act.wait_ge(S("l_var"), j)
                done(act.activation(lt[:], a_, ACT.Tanh, scale=lam), "l_act")
                done(act.activation(a_, a_, ACT.Exp, scale=lam), "l_act")
                act.wait_ge(S("l_var"), j + 1)
                done(act.activation(li[:, j], li[:, j], ACT.Sqrt, scale=-1.0), "l_std")
            for b in range(2):
                for j in range(2):
                    act.wait_ge(*made("rt", 4 * b + j + 1))
                    done(act.activation(KH[b][:, j], bank(f"rgt{b}", j)[:], ACT.Copy), "rgt_out")
                for j in range(2):
                    act.wait_ge(*made("rt", 4 * b + 2 + j + 1))
                    done(act.activation(NBH[b][:, j], bank(f"rtw{b}", j)[:], ACT.Copy), "rtw_out")
            for c in range(NRC - 1):
                act.wait_ge(S("rst_mm"), 2 * c + 1)
                done(act.activation(hall[:, :, (c + 1) * RC:(c + 2) * RC],
                                    bank(f"rst{c}", 0)[:, 0:256].rearrange("p (j v) -> p j v", j=4), ACT.Copy), "rst_out")
                if c % 2 and c > 1:
                    m = c // 2 - 1
                    act.wait_ge(S("ro_out"), 2 * m + 2)
                    done(act.activation(zsq[:, m % 2], oall[:, m], ACT.Square), "r_osq")
                    act.wait_ge(S("r_gvar"), m + 1)
                    done(act.activation(small[:, 48 + 8 * m:56 + 8 * m], small[:, 48 + 8 * m:56 + 8 * m], ACT.Sqrt), "r_gstd")
            for m in range(2, 4):
                if m == 3:
                    act.wait_ge(S("ro_mm"), 4)
                    act.wait_ge(S("l_mix"), 4)
                    for i in range(2):
                        done(act.activation(act_hi[:, i], p0[:, YT0[i], PAD:PW], ACT.Copy), "mix_hi")
                act.wait_ge(S("ro_out"), 2 * m + 2)
                done(act.activation(zsq[:, m % 2], oall[:, m], ACT.Square), "r_osq")
                act.wait_ge(S("r_gvar"), m + 1)
                done(act.activation(small[:, 48 + 8 * m:56 + 8 * m], small[:, 48 + 8 * m:56 + 8 * m], ACT.Sqrt), "r_gstd")
            for i in range(2, 4):
                done(act.activation(act_hi[:, i], p0[:, YT0[i], PAD:PW], ACT.Copy), "mix_hi")
            for i in range(4):
                act.wait_ge(*made("rlora", 8 + i + 1))
                done(act.activation(lc[:, i], bank("rg", i)[:], ACT.Copy), "rg_out")
            split(FIRST["out0"] + 2 + W_SLOTS)
            for jj in range(4):
                act.wait_ge(*made("rback", jj + 1))
                done(act.activation(p0[:, jj, PAD:PW], bank("rback", jj)[:], ACT.Identity, bias=V("gnb", jj),
                                    scale=V("gng", jj)), "rback_out")
            for jj in range(4):
                act.wait_ge(S("r_mix"), jj + 1)
                done(act.activation(act_hi[:, 4 + jj], p0[:, jj, PAD:PW], ACT.Copy), "mix_hi")

            def ln_std(n):
                step(act.activation(small[:, 252:253], small[:, 251:252], ACT.Sqrt))
                for t in range(NT):
                    act.wait_ge(S("ln_var"), NT * n + t + 1)
                    done(act.activation(lnsd[:, t:t + 1], lnmv[:, t, 1:2], ACT.Sqrt, bias=eps[:, 0:1]), "ln_std")
                    if n % 3 == 0 and t == 0:
                        split(FIRST[f"k{n // 3}"] + W_SLOTS)
                    if n < 5 and t < NT - 1:
                        act.wait_ge(S("ln_shift"), (NT - 1) * n + t + 1)
                        done(act.activation(h[:, t], h[:, t], ACT.Identity, bias=lnmv[:, t, 1:2],
                                            scale=lnsd[:, t:t + 1]), "ln_rows")
                    if n % 3 == 0 and t == NT - 2:
                        split(FIRST[f"k{n // 3}"] + 1 + W_SLOTS)

            def feature_hi(l, which, k):
                stg = f"lnt{l}_{which}"
                c = 8 * (3 * l + which) + k
                act.wait_ge(*of(stg, "_mm", k + 1))
                done(act.activation(act_hi[:, k], bank(stg, k)[:], ACT.Identity, bias=V("lnb", c), scale=V("lng", c)),
                     "lnt_hi")
                if k % 2:
                    if k > 1:
                        act.wait_ge(*of(stg, "_out", k - 1))
                    done(act.activation(stage[:, 7], bank(stg, k)[:], ACT.Identity, bias=V("lnb", c), scale=V("lng", c)),
                         "lnt_sum")

            def memory(l):
                act.wait_ge(S("mem_in"), 16 * (l + 1))
                memv = aux_hi[:].rearrange("p a t -> p (a t)")[:, 0:8 * MEM]
                done(act.activation(memv, stage[:].rearrange("p a t -> p (a t)")[:, 0:8 * MEM], ACT.Copy), "mem_hi")

            def attention(l):
                ln_std(3 * l)
                split(FIRST[f"k{l}"] + W_SLOTS)
                for i in range(8):
                    chunk(f"k{l}", i)
                    copy_hi(f"k{l}", i, k_hi[:, i], MEM)
                for half in range(2):
                    for i in range(4):
                        for k in range(4 * half + i + (half + i > 0), min(4 * half + i + 2, KD)):
                            feature_hi(l, 0, k)
                        chunk(f"v{l}", 4 * half + i)
                    for m in range(2):
                        copy_hi(f"v{l}", 2 * half + m, v_hi[:, m, half * HALF:half * HALF + HALF])
                for i in range(8):
                    chunk(f"q{l}", i)
                    copy_hi(f"q{l}", i, aux_hi[:, i])
                split(FIRST[f"wo{l}"] + W_SLOTS)
                for n in range(8):
                    act.wait_ge(S("p_max"), 8 * l + n + 1)
                    for q in range(2):
                        ins = act.activation(stage[:, n, q * MEM:q * MEM + MEM], bank(f"s{l}", n)[:, q * MEM:q * MEM + MEM],
                                             ACT.Exp, bias=small[:, 128 + 2 * n + q:129 + 2 * n + q], scale=1.0 / 16,
                                             accum_out=small[:, 144 + 2 * n + q:145 + 2 * n + q])
                        if q == 0:
                            step(ins)
                        else:
                            done(ins, "s_out")
                for hp in range(2):
                    for t in range(NT):
                        act.wait_ge(*of(f"pt{l}_{hp}", "_mm", t + 1))
                        done(act.activation(act_hi[:, 4 + 4 * hp:8 + 4 * hp, t * P:t * P + P],
                                       bank(f"pt{l}_{hp}", t)[:].rearrange("p (a t) -> p a t", a=4), ACT.Copy), "pt_hi")
                for hp in range(2):
                    for n in range(4):
                        act.wait_ge(*of(f"pv{l}_{hp}", "_mm", n + 1))
                        done(act.activation(act_hi[:, 4 * hp + n], bank(f"pv{l}_{hp}", n)[:], ACT.Copy), "pv_hi")
                for i in range(8):
                    (chunk if i < 7 else ahead)(f"wo{l}", i)
                ln_std(3 * l + 1)
                for k in range(KD):
                    feature_hi(l, 1, k)

            def mlp(l):
                for q in range(QUARTERS):
                    for i in range(8):
                        chunk(f"up{l}_{q}", i)
                        n = 8 * q + i
                        done(act.activation(stage[:, n % 2], bank(f"up{l}_{q}", i)[:], ACT.Relu), "up_out")
                        act.wait_ge(*of(f"up{l}_{q}", "_sq", i + 1))
                        done(act.activation(aux_hi[:, i], stage[:, 2 + n % 2], ACT.Copy), "up_hi")
                    for i in range(8):
                        (chunk if i < 7 or q < 3 else ahead)(f"down{l}_{q}", i)
                ln_std(3 * l + 2)

            for i in range(8):
                (chunk if i < 7 else ahead)("out0", i)
                if i == 6:
                    memory(0)
            attention(0)
            mlp(0)
            for k in range(KD):
                feature_hi(0, 2, k)
            def conf_product(i):
                j, n = (3, i) if i < CONF_TAPS else (2, i - CONF_TAPS)
                src = cu[:, j, CP - (CONF_TAPS - 1) + n:CP - (CONF_TAPS - 1) + n + T]
                m = i if j == 3 else i - 1
                if n == 0:
                    act.wait_ge(S("c_u"), 4)
                    done(act.activation(cacc[:, 3] if j == 3 else cacc2[:], src, ACT.Identity, bias=V("ccb", j),
                                        scale=V("ccw", j)), "c_prod")
                else:
                    if m >= 3:
                        act.wait_ge(S("c_conv3"), m - 2)
                    done(act.activation(gtmp[:, m % 2], src, ACT.Copy, scale=V("ccw", 4 * n + j)), "c_prod")

            def ssd_products(m):
                i = 8 + m
                x_ = p1[:, XS + i]
                for k in range(4):
                    n = 4 * m + k
                    if k == 0:
                        if m >= 2:
                            act.wait_ge(S("s_bc"), m - 1)
                        done(act.activation(pconv[:, m % 2], x_[:, 1:1 + T], ACT.Identity, bias=V("scb", i),
                                            scale=V("scw", i)), "s_prod")
                    else:
                        if 3 * m + k >= 3:
                            act.wait_ge(S("s_padd"), 3 * m + k - 2)
                        act.wait_ge(S("c_conv3"), CONF_SUMS)
                        done(act.activation(gtmp[:, (3 * m + k) % 2], x_[:, 1 + k:1 + k + T], ACT.Copy,
                                            scale=V("scw", 12 * k + i)), "s_prod")

            def ssd_gate(m):
                act.wait_ge(S("s_cv"), m + 1)
                if m:
                    act.wait_ge(S("s_conv"), m)
                done(act.activation(gtmp[:, 2], sconv[:, m % 2], ACT.Sigmoid), "s_sig")

            def ssd_gate_bc(m):
                act.wait_ge(S("s_padd"), 3 * m + 3)
                if m:
                    act.wait_ge(S("s_bc"), m)
                done(act.activation(gtmp[:, 3], pconv[:, m % 2], ACT.Sigmoid), "s_sigbc")

            act.wait_ge(S("c_zero"), 1)
            for i in range(29):
                chunk("in1", i)
                fn = ACT.Sigmoid if 4 <= i < 8 else ACT.Copy
                done(act.activation(p1[:, i, PAD:PW], bank("in1", i)[:], fn), "in_out")
                if i == 8:
                    act.wait_ge(S("ln_used"), 3)
                if i >= 8:
                    for n in range(4 * (i - 8), min(4 * (i - 7), CONF_TAPS + POOL_TAPS)):
                        conf_product(n)
                if 12 <= i <= 26 and i % 2 == 0:
                    ssd_gate((i - 12) // 2)
                if i == 20:
                    raw = p1[0:16, DT, PAD:PW]
                    step(act.activation(raw, raw, ACT.Identity, bias=vec[0:16, VEC["dtb"]:VEC["dtb"] + 1]))
                    step(act.activation(sdt[:, 0], raw, ACT.Abs))
                    step(act.activation(sdt[:, 0], sdt[:, 0], ACT.Exp, scale=-1.0))
                    step(act.activation(small[0:16, 200:201], vec[0:16, VEC["alog"]:VEC["alog"] + 1], ACT.Exp))
                    done(act.activation(sdt[:, 0], sdt[:, 0], ACT.Ln, bias=1.0), "s_sp")
                if i in (21, 23, 25, 27):
                    ssd_products((i - 21) // 2)
                if i in (22, 24, 26, 28):
                    ssd_gate_bc((i - 22) // 2)
                if i == 27:
                    act.wait_ge(*made("slast", 1))
                    done(act.activation(stm[:, 3], bank("slast", 0)[:, 0:64].rearrange("p (c h) -> p c h", c=NSC),
                                        ACT.Copy), "slast_out")
                if i == 28:
                    act.wait_ge(S("s_dte"), 1)
                    step(act.activation(stm[:, 2], stm[:, 2], ACT.Exp))
                    done(act.activation(stm[:, 3], stm[:, 3], ACT.Exp), "s_dtee")
            split(FIRST["out1"] + W_SLOTS)
            for j in range(4):
                act.wait_ge(S("c_cent"), j + 1)
                done(act.activation(p1[:, 4 + j, PAD:PW], cacc[:, j], ACT.Square), "c_sq")
            for q in range(2):
                act.wait_ge(*made("sbt", q + 1))
                done(act.activation(bt[:, 2 * q:2 * q + 2].rearrange("p c n -> p (c n)"), bank("sbt", q)[:], ACT.Copy),
                     "sbt_out")
            act.wait_ge(S("cvar_out"), 1)
            done(act.activation(c_std, c_std, ACT.Sqrt), "c_stdd")
            for j in range(4):
                act.wait_ge(S("c_norm"), j + 1)
                step(act.activation(p1[:, 4 + j, PAD:PW], cacc[:, j], ACT.Sigmoid, bias=V("clb", j), scale=V("clg", j)))
                done(act.activation(cacc[:, j], cacc[:, j], ACT.Identity, bias=V("clb", j), scale=V("clg", j)), "c_sig")

            def z_gate(hp):
                done(act.activation(p1[:, 4 + hp % 4, PAD:PW], p1[:, ZS + hp, PAD:PW], ACT.Sigmoid), "s_zsig")

            def decays(hp):
                for n in (2 * hp, 2 * hp + 1):
                    act.wait_ge(S("s_diff"), n + 1)
                    if hp >= 2:
                        act.wait_ge(*made("sy", hp - 1))
                    done(act.activation(cs[:, n % 4], bank(f"sbc{hp}", n % 2)[:], ACT.Exp), "sbc_out")
                    done(act.activation(mt(n), mt(n), ACT.Exp), "s_exp")

            def mix_hi(first, last):
                for i in range(first, last):
                    act.wait_ge(S("mix_f1"), i + 1)
                    done(act.activation(act_hi[:, i], p1[:, YT1[i], PAD:PW], ACT.Copy), "mix_hi")

            def root(g):
                act.wait_ge(S("srms_out"), g + 1)
                done(act.activation(p1[:, BS + g, PAD:PW], p1[:, BS + g, PAD:PW], ACT.Sqrt), "s_rstd")

            decays(0)
            act.wait_ge(S("mix_f1"), 4)
            for hp in range(4):
                z_gate(hp)
            for hp in range(8):
                if hp < 7:
                    decays(hp + 1)
                if hp == 3:
                    for n in range(4, 8):
                        act.wait_ge(S("s_z"), n - 3)
                        z_gate(n)
                if hp == 7:
                    act.wait_ge(*made("sy", 8))
                    mix_hi(0, 2)
                act.wait_ge(S("s_y"), hp + 1)
                done(act.activation(p1[:, XS + hp, PAD:PW], p1[:, ZS + hp, PAD:PW], ACT.Square), "s_ysq")
            mix_hi(2, 4)
            root(0)
            mix_hi(4, 8)
            split(FIRST["out1"] + 1 + W_SLOTS)
            root(1)
            mix_hi(8, 12)
            for i in range(12):
                (chunk if i < 11 else ahead)("out1", i)
                if i == 7:
                    memory(1)
            attention(1)
            mlp(1)

        @block.vector
        def _(dve):
            n_split = [0]
            n_step = [0]

            def step(ins, lag=0):
                n_step[0] += 1
                ins.then_inc(S("dve_step"), 1)
                if n_step[0] > lag:
                    dve.wait_ge(S("dve_step"), n_step[0] - lag)

            counts = {}

            def done(ins, name):
                counts[name] = counts.get(name, 0) + 1
                ins.then_inc(S(name), 1)
                dve.wait_ge(S(name), counts[name])

            def f(ap):
                return ap.bitcast(F32)

            def split(upto):
                while n_split[0] < min(upto, N_CHUNKS):
                    c = n_split[0]
                    s = c % W_SLOTS
                    dve.wait_ge(S("w_hi_done"), c + 1)
                    dve.tensor_tensor(w_lo[:, s], w_raw[:, s], f(w_hi[:, s]), ALU.subtract).then_inc(S("w_split"), 1)
                    n_split[0] += 1

            def chunk(stg, i):
                c = FIRST[stg] + i
                split(c + W_SLOTS)
                dve.wait_ge(S("chunk_done"), c + 1)

            def ahead(stg, i):
                split(FIRST[stg] + i + W_SLOTS)

            def tt(o, a, b_, op):
                return dve.tensor_tensor(o, a, b_, op)

            def stt(o, a, s, b_, op0, op1):
                return dve.scalar_tensor_tensor(out=o, in0=a, scalar=s, in1=b_, op0=op0, op1=op1)

            MUL, ADD, SUB = ALU.mult, ALU.add, ALU.subtract

            for i in range(4):
                dve.wait_ge(S("x_hi"), i + 1)
                dve.wait_ge(S(f"x_in{i}"), 16)
                two = slice(2 * i, 2 * i + 2)
                done(tt(act_lo[:, two], stage[:, two], f(act_hi[:, two]), SUB), "x_split")
                if i in (0, 3):
                    split(1 + i // 3)
            step(dve.memset(p0[:, :, 0:PAD], 0.0))
            dve.wait_ge(S("vec_in"), 16)

            def scaled_keys(b):
                for j in range(2):
                    ins = dve.tensor_scalar(NBT[b][:, j], p0[:, 4 + 2 * b + j, PAD:PW], V("kk", 2 * b + j), None, MUL)
                    if j:
                        done(ins, "r_kk")
                    else:
                        step(ins, 1)

            def running_decay(b):
                dve.wait_ge(S("rdec_out"), 2 * b + 2)
                for j in range(2):
                    step(dve.tensor_tensor_scan(s_cum[:, j], m_scan[:], s_dec[:, j], 0.0, MUL, ADD))
                cum = s_cum[:].rearrange("p j (c t) -> p j c t", t=RC)
                done(dve.tensor_copy(dend[:, b], cum[:, :, :, RC - 1]), "r_cum")

            def keys(b):
                k_ = p0[:, 4 + 2 * b:6 + 2 * b, PAD:PW]
                dve.wait_ge(S("ra_out"), 2 * b + 2)
                for j in range(2):
                    step(dve.tensor_scalar(BON[b][:, j], s_a[:, j], V("ka", 2 * b + j),
                                           small[:, 84 + 2 * b + j:85 + 2 * b + j], MUL, ADD))
                done(tt(k_, k_, BON[b][:], MUL), "r_k")

            def normalised(b, part):
                dve.wait_ge(S("rss_out"), 2 * b + part + 1)
                step(dve.tensor_scalar(NBH[b][:, part], NBH[b][:, part], 1e-12, None, ALU.max))
                step(dve.reciprocal(NBH[b][:, part], NBH[b][:, part]))
                step(tt(NBT[b][:, part], NBT[b][:, part], NBH[b][:, part], MUL))

            def scale_operands(b, part):
                r_, k_ = p0[:, 2 * b:2 * b + 2, PAD:PW], p0[:, 4 + 2 * b:6 + 2 * b, PAD:PW]
                if part == 0:
                    dve.wait_ge(S("r_e"), 4 * b + 4)
                    step(tt(ALPH[b][:], ALPH[b][:], NBT[b][:], MUL))
                    step(stt(NBT[b][:], NBT[b][:], -1.0, s_a[:], MUL, MUL))
                    step(tt(KH[b][:], k_, s_inv[:], MUL))
                    step(tt(NBH[b][:], NBT[b][:], s_inv[:], MUL))
                else:
                    dve.wait_ge(S("r_rk"), b + 1)
                    step(tt(r_, r_, s_fwd[:], MUL))
                    fwd = s_fwd[:].rearrange("p j (c t) -> p j c t", t=RC)
                    step(dve.tensor_copy(dend[:, b], fwd[:, :, :, RC - 1]))
                    step(tt(NBT[b][:], NBT[b][:], s_dec[:], MUL))
                    done(tt(k_, k_, s_dec[:], MUL), "r_ops")

            def bonus(b):
                for j in range(2):
                    dve.wait_ge(*made("rbon", 2 * b + j + 1))
                    done(tt(BON[b][:, j], bank(f"rbon{b}", j)[:], p0[:, 8 + 2 * b + j, PAD:PW], MUL), "rbon_out")

            def convolution(j):
                x_ = p0[:, 14 + j]
                step(dve.tensor_scalar(lc[:, j], x_[:, 1:1 + T], V("lcw", j), V("lcb", j), MUL, ADD))
                for k in range(1, 4):
                    ins = stt(lc[:, j], x_[:, 1 + k:1 + k + T], V("lcw", 4 * k + j), lc[:, j], MUL, ADD)
                    if k < 3:
                        step(ins)
                    else:
                        done(ins, "l_conv")

            for i in range(22):
                stg, n = PLACE0[i]
                tile = ORDER0[i]
                split(i + W_SLOTS)
                if i < 14:
                    dve.wait_ge(S("r_in"), i + 1)
                    cur = p0[:, tile, PAD + 1:PW]
                    done(stt(cur, bank(stg, n)[:, 0:T - 1], V("mu", tile), cur, MUL, ADD), "in_out")
                if i == 5:
                    scaled_keys(0)
                    dve.wait_ge(S("masks"), 1)
                    step(dve.tensor_scalar(small[:, 84:88], vec[:, VEC["ka"]:VEC["ka"] + 4], -1.0, 1.0, MUL, ADD))
                if i == 6:
                    running_decay(0)
                    keys(0)
                if i == 10:
                    normalised(0, 0)
                if i == 11:
                    normalised(0, 1)
                    scaled_keys(1)
                if i == 12:
                    scale_operands(0, 0)
                if i == 13:
                    scale_operands(0, 1)
                if i == 14:
                    bonus(0)
                if i == 16:
                    running_decay(1)
                    keys(1)
                if i == 17:
                    for j in range(2):
                        dve.wait_ge(S("in_out"), 15 + j)
                        convolution(j)
                if i == 18:
                    normalised(1, 0)
                if i == 19:
                    normalised(1, 1)
                if i == 20:
                    scale_operands(1, 0)
                if i == 21:
                    scale_operands(1, 1)
            split(FIRST["out0"] + W_SLOTS)
            for j in range(2, 4):
                dve.wait_ge(S("in_out"), 15 + j)
                convolution(j)

            def three(ap):
                return ap.rearrange("p (c t) -> p c t", t=RC)

            def masked_products(b):
                for n, (dst, mask) in enumerate([(M_[b], None), (XT_[b], m_lev[:, 0]), (PAK[b], m_strict[:]),
                                                 (PRB[b], m_incl[:]), (PRK[b], m_incl[:])]):
                    for j in range(2):
                        dve.wait_ge(*made("rprod", 10 * b + 2 * n + j + 1))
                        blk = dst[:].rearrange("p j (m u) -> p (j m) u", u=P)[:, :, j * RC:j * RC + RC]
                        src = three(bank(f"rprod{b}", 2 * n + j)[:])
                        if mask is None:
                            done(dve.tensor_copy(blk, src), "rprod_out")
                        else:
                            done(tt(blk, src, mid(mask, NRC), MUL), "rprod_out")
                for j in range(2):
                    done(tt(three(XT_[b][:, j]), three(XT_[b][:, j]), mid(eye2[:], NRC), ADD), "r_x0")
                    step(tt(three(NBH[b][:, j]), three(M_[b][:, j]), mid(m_lev[:, 6], NRC), MUL))
                    step(tt(three(NBH[b][:, j]), three(NBH[b][:, j]), mid(eye2[:], NRC), ADD))

            masked_products(0)
            bonus(1)
            masked_products(1)

            def blocks(ap, n, upper):
                at = 0 if upper else n
                return ap.rearrange("p j (b u) -> p (j b) u", u=2 * n)[:, :, at:at + n]

            def level_y(b, v):
                n = 1 << v
                dve.wait_ge(S("yt_zero"), (0, 4 if b else 3, 4 if b else 3, 5 + b, 7 + b, 7 + b)[v])
                dve.wait_ge(*made("ryt", 2 * (v - 1) + b + 1))
                dst = yt_(b, v).rearrange("p j (g b u) -> p (j g) b u", b=32 // n, u=2 * n)[:, :, :, n:2 * n]
                mask = m_lev[:, v].rearrange("p (b u) -> p b u", u=2 * n)[:, :, n:2 * n]
                done(tt(dst, bank(f"ryt{b}_{v}", 0)[:].rearrange("p (g b n) -> p g b n", b=32 // n, n=n),
                        mask.unsqueeze(1).to_broadcast([P, 16, 32 // n, n]), MUL), "ryt_out")

            def level_z(b, v):
                n = 1 << v
                before = 4 * (v - 1) + (2 if v < 5 else 1) * b
                for m, (x_, upper) in enumerate([(NBH[b], True), (XT_[b], False)][0 if v < 5 else 1:]):
                    dve.wait_ge(*made("rz", before + (2 if v < 5 else 1)))
                    view = blocks(x_[:], n, upper)
                    done(tt(view, view, bank(f"rz{b}_{v}", m)[:].rearrange("p (b n) -> p b n", n=n), ADD), "rz_out")

            def lru_variance(j):
                dve.wait_ge(S("l_gx"), j + 1)
                dve.wait_ge(S("l_act"), 2 * j + 2)
                a_ = p0[:, 14 + j, PAD:PW]
                step(tt(li[:, j], a_, a_, MUL))
                done(stt(li[:, j], li[:, j], 1.0, lt[:], ADD, MUL), "l_var")

            def lru_scan(j):
                dve.wait_ge(S("l_std"), j + 1)
                a_ = p0[:, 14 + j, PAD:PW]
                step(tt(lc[:, j], lc[:, j], li[:, j], MUL))
                step(dve.tensor_tensor_scan(li[:, j], a_, lc[:, j], 0.0, MUL, ADD))
                if j == 0:
                    dve.wait_ge(S("l_gelu"), 4)
                done(tt(a_, li[:, j], p0[:, 18 + j, PAD:PW], MUL), "l_mix")

            for v in range(1, 6):
                for b in range(2):
                    level_y(b, v)
                if v >= 2:
                    lru_variance(v - 2)
                for b in range(2):
                    level_z(b, v)
                    if b == 0 and v >= 3:
                        lru_scan(v - 3)
            lru_scan(3)
            for b in range(2):
                for j in range(2):
                    dve.wait_ge(*made("rt", 8 + 4 * b + j + 1))
                    if j == 0:
                        dve.wait_ge(S("r_diag"), b + 1)
                    view = every_other(M_[b][:], j)
                    done(tt(view, view, bank(f"rat{b}", j)[:].rearrange("p (j m v) -> p j m v", j=2, v=RC), ADD), "rat_out")
                for j in range(2):
                    view = every_other(p0[:, 2 * b:2 * b + 2, PAD:PW], j)
                    dve.wait_ge(*made("rt", 8 + 4 * b + 2 + j + 1))
                    done(tt(view, view, bank(f"rrho{b}", j)[:].rearrange("p (j m v) -> p j m v", j=2, v=RC), ADD),
                         "rrho_out")

            def lru_lo(i):
                dve.wait_ge(S("mix_hi"), i + 1)
                done(tt(act_lo[:, i], p0[:, YT0[i], PAD:PW], f(act_hi[:, i]), SUB), "mix_lo")

            def heads(ap):
                return ap.rearrange("p (h v) -> p h v", v=RD)

            for m in range(NT):
                mean, var = small[:, 16 + 8 * m:24 + 8 * m], small[:, 48 + 8 * m:56 + 8 * m]
                dve.wait_ge(S("ro_mm"), m + 1)
                for q in range(2):
                    step(dve.tensor_reduce(mean[:, 4 * q:4 * q + 4], heads(bank(f"ro{m}", q)[:, 0:256]), AX_X, ADD))
                if m == 3:
                    lru_lo(0)
                step(dve.tensor_scalar(mean, mean, 1.0 / RD, None, MUL))
                for q in range(2):
                    done(tt(oall[:, m].rearrange("p (j q v) -> p q j v", q=2, v=RD)[:, q], heads(bank(f"ro{m}", q)[:, 0:256]),
                            bc(mean[:, 4 * q:4 * q + 4], RD), SUB), "ro_out")
                dve.wait_ge(S("r_osq"), m + 1)
                step(dve.tensor_reduce(var, heads(zsq[:, m % 2]), AX_X, ADD))
                done(dve.tensor_scalar(var, var, 1.0 / RD, GN_EPS, MUL, ADD), "r_gvar")
                if m == 3:
                    lru_lo(1)
                dve.wait_ge(S("r_gstd"), m + 1)
                step(dve.reciprocal(var, var))
                done(tt(heads(oall[:, m]), heads(oall[:, m]), bc(var, RD), MUL), "r_gn")
            for i in range(2, 4):
                lru_lo(i)
            split(FIRST["out0"] + 2 + W_SLOTS)
            for jj in range(4):
                y_ = p0[:, jj, PAD:PW]
                dve.wait_ge(S("rback_out"), jj + 1)
                step(tt(y_, y_, BON[jj // 2][:, jj % 2], ADD))
                if jj == 0:
                    dve.wait_ge(S("rg_out"), 4)
                done(tt(y_, y_, lc[:, jj], MUL), "r_mix")
                if jj:
                    dve.wait_ge(S("mix_hi"), 4 + jj)
                    done(tt(act_lo[:, 3 + jj], p0[:, jj - 1, PAD:PW], f(act_hi[:, 3 + jj]), SUB), "mix_lo")
            dve.wait_ge(S("mix_hi"), 8)
            done(tt(act_lo[:, 7], p0[:, 3, PAD:PW], f(act_hi[:, 7]), SUB), "mix_lo")
            done(dve.tensor_copy(small[:, 255:256], small[:, 254:255]), "mix_done")

            n_rows = [0]

            def normalise(n, t):
                dve.wait_ge(S("ln_std"), NT * n + t + 1)
                step(dve.reciprocal(lnsd[:, t:t + 1], lnsd[:, t:t + 1]))
                row, mean, scale = h[:, t], lnmv[:, t, 0:1], lnsd[:, t:t + 1]
                if n < 5 and t < NT - 1:
                    done(stt(lnmv[:, t, 1:2], mean, -1.0, scale, MUL, MUL), "ln_shift")
                elif n < 5:
                    done(dve.tensor_scalar(row, row, mean, scale, SUB, MUL), "ln_last")
                else:
                    dve.wait_ge(S("gb_in"), 16 * 6)
                    step(stt(row, row, mean, gb[:, 0], SUB, MUL))
                    done(stt(row, row, scale, gb[:, 1], MUL, ADD), "out_rows")

            def residual(stg, half, first, final=None):
                cols = slice(half * HALF, half * HALF + HALF)
                for t in range(NT):
                    if t < NT - 1:
                        n_rows[0] += 1
                        dve.wait_ge(S("tokens_mm"), n_rows[0])
                    else:
                        dve.wait_ge(S("chunk_done"), FIRST[stg] + (half + 1) * dict(STREAM)[stg] // 2)
                    if first:
                        ins = stt(h[:, t, cols], h[:, t, cols], ALPHA, bank(stg, half * NT + t)[:], MUL, ADD)
                    else:
                        ins = tt(h[:, t, cols], h[:, t, cols], bank(stg, half * NT + t)[:], ADD)
                    done(ins, FAMILY[stg] + "_out")
                    if final is not None:
                        step(dve.bn_stats(lnst[:, t, 6 * half:6 * half + 6], h[:, t, cols]))
                        if half:
                            done(dve.bn_aggr(lnmv[:, t], lnst[:, t]), "ln_var")
                            if final % 3 == 0 and t == 1:
                                split(FIRST[f"k{final // 3}"] + W_SLOTS)
                            if t:
                                normalise(final, t - 1)
                if final is not None and half:
                    if final % 3 == 0:
                        split(FIRST[f"k{final // 3}"] + 1 + W_SLOTS)
                    normalise(final, NT - 1)

            ln_n = [0]

            def feature_lo(l, which, k):
                stg = f"lnt{l}_{which}"
                c = 8 * (3 * l + which) + k
                dve.wait_ge(*of(stg, "_hi", k + 1))
                tmp = stage[:, 6 + k % 2]
                if k % 2:
                    dve.wait_ge(S("lnt_sum"), 4 * ln_n[0] + k // 2 + 1)
                    ln_n[0] += k == KD - 1
                else:
                    step(dve.tensor_scalar(tmp, bank(stg, k)[:], V("lng", c), V("lnb", c), MUL, ADD))
                done(tt(act_lo[:, k], tmp, f(act_hi[:, k]), SUB), "lnt_out")

            def memory(l):
                dve.wait_ge(S("mem_hi"), l + 1)
                n8 = 8 * MEM
                done(tt(aux_lo[:].rearrange("p a t -> p (a t)")[:, 0:n8], stage[:].rearrange("p a t -> p (a t)")[:, 0:n8],
                        f(aux_hi[:].rearrange("p a t -> p (a t)")[:, 0:n8]), SUB), "mem_split")

            def attention(l):
                split(FIRST[f"k{l}"] + W_SLOTS)
                for i in range(8):
                    chunk(f"k{l}", i)
                    dve.wait_ge(*of(f"k{l}", "_hi", i + 1))
                    done(tt(k_lo[:, i], bank(f"k{l}", i)[:, 0:MEM], f(k_hi[:, i]), SUB), "k_out")
                for half in range(2):
                    for i in range(4):
                        for k in range(4 * half + i + (half + i > 0), min(4 * half + i + 2, KD)):
                            feature_lo(l, 0, k)
                        chunk(f"v{l}", 4 * half + i)
                    n_rows[0] += 1
                    for m in range(2):
                        cols = slice(half * HALF, half * HALF + HALF)
                        dve.wait_ge(*of(f"v{l}", "_hi", 2 * half + m + 1))
                        done(tt(v_lo[:, m, cols], bank(f"v{l}", 2 * half + m)[:], f(v_hi[:, m, cols]), SUB), "v_out")
                for i in range(8):
                    chunk(f"q{l}", i)
                    dve.wait_ge(*of(f"q{l}", "_hi", i + 1))
                    done(tt(aux_lo[:, i], bank(f"q{l}", i)[:], f(aux_hi[:, i]), SUB), "q_out")
                split(FIRST[f"wo{l}"] + W_SLOTS)

                def row_max(n):
                    dve.wait_ge(*of(f"s{l}", "_mm", n + 1))
                    step(dve.tensor_reduce(small[:, 160 + 2 * n:162 + 2 * n],
                                           bank(f"s{l}", n)[:].rearrange("p (q m) -> p q m", q=2), AX_X, ALU.max))
                    done(dve.tensor_scalar(small[:, 128 + 2 * n:130 + 2 * n], small[:, 160 + 2 * n:162 + 2 * n],
                                           -1.0 / 16, None, MUL), "p_max")

                def probs(n):
                    dve.wait_ge(*of(f"s{l}", "_out", n + 1))
                    step(dve.reciprocal(small[:, 176 + 2 * n:178 + 2 * n], small[:, 144 + 2 * n:146 + 2 * n]))
                    for q in range(2):
                        pr = stage[:, n, q * MEM:q * MEM + MEM]
                        ins = dve.tensor_scalar(pr, pr, small[:, 176 + 2 * n + q:177 + 2 * n + q], None, MUL)
                        if q:
                            done(ins, "p_ready")
                        else:
                            step(ins)

                for n in range(9):
                    if n < 8:
                        row_max(n)
                    if n:
                        probs(n - 1)
                for hp in range(2):
                    for t in range(NT):
                        dve.wait_ge(*of(f"pt{l}_{hp}", "_hi", t + 1))
                        dst = slice(t * P, t * P + P)
                        at = slice(4 + 4 * hp, 8 + 4 * hp)
                        ins = tt(act_lo[:, at, dst], bank(f"pt{l}_{hp}", t)[:].rearrange("p (a t) -> p a t", a=4),
                                 f(act_hi[:, at, dst]), SUB)
                        done(ins, "pt_out")
                for hp in range(2):
                    for n in range(4):
                        dve.wait_ge(*of(f"pv{l}_{hp}", "_hi", n + 1))
                        i = 4 * hp + n
                        done(tt(act_lo[:, i], bank(f"pv{l}_{hp}", n)[:], f(act_hi[:, i]), SUB), "pv_out")
                dve.wait_ge(S("h_ready"), NT * (3 * l + 1))
                for half in range(2):
                    for i in range(4):
                        (chunk if i < 3 else ahead)(f"wo{l}", 4 * half + i)
                    residual(f"wo{l}", half, True, 3 * l + 1)
                for k in range(KD):
                    feature_lo(l, 1, k)

            def mlp(l):
                for q in range(QUARTERS):
                    for i in range(8):
                        chunk(f"up{l}_{q}", i)
                        n = 8 * q + i
                        dve.wait_ge(*of(f"up{l}_{q}", "_out", i + 1))
                        done(tt(stage[:, 2 + n % 2], stage[:, n % 2], stage[:, n % 2], MUL), "up_sq")
                        dve.wait_ge(*of(f"up{l}_{q}", "_hi", i + 1))
                        done(tt(aux_lo[:, i], stage[:, 2 + n % 2], f(aux_hi[:, i]), SUB), "up_lo")
                    for half in range(2):
                        for i in range(4):
                            (chunk if i < 3 else ahead)(f"down{l}_{q}", 4 * half + i)
                        if q == 0 and half == 0:
                            dve.wait_ge(S("h_ready"), NT * (3 * l + 2))
                        residual(f"down{l}_{q}", half, q == 0, 3 * l + 2 if q == QUARTERS - 1 else None)

            dve.wait_ge(S("h_in"), 16)
            for half in range(2):
                for i in range(4):
                    (chunk if i < 3 else ahead)("out0", 4 * half + i)
                    if half and i == 2:
                        memory(0)
                residual("out0", half, True, 0)
            attention(0)
            mlp(0)
            for k in range(KD):
                feature_lo(0, 2, k)
            def conf_taps(first, last):
                for n in range(first, last):
                    k, j = divmod(n, 2) if n < 2 * POOL_TAPS else divmod(n + POOL_TAPS, 3)
                    src = cu[:, j, CP - (CONF_TAPS - 1) + k:CP - (CONF_TAPS - 1) + k + T]
                    w_ = V("ccw", 4 * k + j)
                    if k == 0:
                        step(dve.tensor_scalar(cacc[:, j], src, w_, V("ccb", j), MUL, ADD), 1)
                    elif j == 2 and k == POOL_TAPS:
                        step(dve.tensor_scalar(cacc[:, j], src, w_, None, MUL), 1)
                    else:
                        step(stt(cacc[:, j], src, w_, cacc[:, j], MUL, ADD), 1 if n < N_TAPS - 1 else 0)

            def ssd_gated(m):
                dve.wait_ge(S("s_sig"), m + 1)
                done(tt(p1[:, XS + m, PAD:PW], sconv[:, m % 2], gtmp[:, 2], MUL), "s_conv")

            def ssd_conv(m):
                x_, d_ = p1[:, XS + m], sconv[:, m % 2]
                dve.wait_ge(*out_sem("in1", XS + m + 1))
                step(dve.tensor_scalar(d_, x_[:, 1:1 + T], V("scw", m), V("scb", m), MUL, ADD))
                for k in range(1, 4):
                    ins = stt(d_, x_[:, 1 + k:1 + k + T], V("scw", 12 * k + m), d_, MUL, ADD)
                    if k < 3:
                        step(ins)
                    else:
                        done(ins, "s_cv")

            step(dve.memset(p1[:, :, 0:PAD], 0.0))
            done(dve.memset(cu[:, :, 0:CP], 0.0), "c_zero")
            N_TAPS = 3 * CONF_TAPS - POOL_TAPS

            def taps_by(i):
                return min(7 * (i - 8) if i < 12 else 28 + 3 * (i - 12), N_TAPS)

            for i in range(29):
                split(FIRST["in1"] + i + W_SLOTS)
                if i == 8:
                    for j in (3, 0, 1, 2):
                        dve.wait_ge(*out_sem("in1", 8))
                        done(tt(cu[:, j, CP:CP + T], p1[:, j, PAD:PW], p1[:, 4 + j, PAD:PW], MUL), "c_u")
                if i >= 8:
                    conf_taps(taps_by(i), taps_by(i + 1))
                if 11 <= i <= 25 and i % 2:
                    m = (i - 11) // 2
                    ssd_conv(m)
                    if m:
                        ssd_gated(m - 1)
                if i == 25:
                    for m in range(2):
                        dve.wait_ge(*made("stok", m + 1))
                        done(dve.tensor_copy(stm[:, m].rearrange("p c h -> p (c h)"), bank("stok", m)[:, 0:64]),
                             "stok_out")
                if i == 28:
                    dve.wait_ge(S("slast_out"), 1)
                    done(tt(stm[:, 2], stm[:, 3], stm[:, 1], SUB), "s_dte")
                if i == 21:
                    dve.wait_ge(S("s_sp"), 1)
                    dve.wait_ge(S("masks"), 2)
                    raw = p1[0:16, DT, PAD:PW]
                    step(stt(sdt[:, 0], raw, 0.0, sdt[:, 0], ALU.max, ADD))
                    step(dve.tensor_scalar(raw, sdt[:, 0], small[0:16, 200:201], -1.0, MUL, MUL))
                    done(dve.tensor_tensor_scan(sdt[:, 1], m_scan[0:16], raw, 0.0, MUL, ADD), "s_acum")
            ssd_gated(7)
            conf_taps(taps_by(29), N_TAPS)
            dve.wait_ge(S("c_conv3"), CONF_SUMS)
            done(tt(cacc[:, 2], cacc[:, 2], cacc2[:], ADD), "c_conv")
            split(FIRST["out1"] + W_SLOTS)
            cmean = p1[:, 0, PAD:PW]
            dve.wait_ge(*made("c", 1))
            done(dve.tensor_scalar(cmean, bank("cmean", 0)[:], 1.0 / 512, None, MUL), "cmean_out")
            for j in range(4):
                done(tt(cacc[:, j], cacc[:, j], cmean, SUB), "c_cent")
            dve.wait_ge(S("s_dtee"), 1)
            for c in range(NSC):
                for q in range(2):
                    dve.wait_ge(*made("sxt", 2 * c + q + 1))
                    dst = xdt[:, c, q * 512:q * 512 + 512].rearrange("p (h v) -> p h v", v=64)
                    done(tt(dst, bank("sxt", 2 * c + q)[:].rearrange("p (h v) -> p h v", v=64),
                            bc(stm[:, 0, c, 8 * q:8 * q + 8], 64), MUL), "sxt_out")
            dve.wait_ge(*made("c", 2))
            done(dve.tensor_scalar(c_std, bank("cvar", 0)[:], 1.0 / 512, LN_EPS, MUL, ADD), "cvar_out")
            for g in range(2):
                dve.wait_ge(*made("scb", g + 1))
                done(tt(cbt[:, :, g], bank("scb", g)[:].rearrange("p (c t) -> p c t", c=NSC), mid(m_tri[:], NSC), MUL),
                     "scb_out")
            dve.wait_ge(S("c_stdd"), 1)
            step(dve.reciprocal(c_std, c_std))
            for j in range(4):
                done(tt(cacc[:, j], cacc[:, j], c_std, MUL), "c_norm")
            def differences(hp):
                for n in (2 * hp, 2 * hp + 1):
                    dve.wait_ge(*made("sbc", n + 1))
                    if hp >= 2:
                        dve.wait_ge(*made("sy", hp - 1))
                    for c in range(NSC):
                        cols = slice(c * SC, c * SC + SC)
                        ins = dve.tensor_scalar(mt(n)[:, cols], bank(f"sbc{hp}", n % 2)[:, cols],
                                                stm[:, 1, c, n:n + 1], 0.0, SUB, ALU.min)
                        if c < NSC - 1:
                            step(ins, 3)
                        else:
                            done(ins, "s_diff")

            def scores(hp):
                for n in (2 * hp, 2 * hp + 1):
                    dve.wait_ge(S("s_exp"), n + 1)
                    m3 = mt(n).rearrange("p (c t) -> p c t", c=NSC)
                    done(tt(m3, m3, cbt[:, :, hp // 4], MUL), "s_mt")

            def rms(g):
                r_ = p1[:, BS + g, PAD:PW]
                dve.wait_ge(S("s_rstd"), g + 1)
                step(dve.reciprocal(r_, r_))
                for j in range(4):
                    z_ = p1[:, ZS + 4 * g + j, PAD:PW]
                    done(stt(z_, z_, V("sng", 4 * g + j), r_, MUL, MUL), "mix_f1")

            def mean_square(g):
                dve.wait_ge(*made("srms", g + 1))
                done(dve.tensor_scalar(p1[:, BS + g, PAD:PW], bank(f"srms{g}", 0)[:], 1.0 / 512, LN_EPS, MUL, ADD),
                     "srms_out")

            def mix_lo(first, last):
                for i in range(first, last):
                    dve.wait_ge(S("mix_hi"), 8 + i + 1)
                    done(tt(act_lo[:, i], p1[:, YT1[i], PAD:PW], f(act_hi[:, i]), SUB), "mix_lo")

            differences(0)
            for c in range(NSC - 1):
                for g in range(2):
                    dve.wait_ge(*made("sst", 2 * c + g + 1))
                    nxt = prev[:, c, g * 512:g * 512 + 512].rearrange("p (h v) -> p h v", v=64)
                    src = bank("sst", 2 * c + g)[:].rearrange("p (h v) -> p h v", v=64)
                    if c == 0:
                        done(dve.tensor_copy(nxt, src), "sst_out")
                    else:
                        cur = prev[:, c - 1, g * 512:g * 512 + 512].rearrange("p (h v) -> p h v", v=64)
                        step(tt(nxt, cur, bc(stm[:, 3, c, 8 * g:8 * g + 8], 64), MUL))
                        done(tt(nxt, nxt, src, ADD), "sst_out")
            for j in range(4):
                dve.wait_ge(S("c_sig"), j + 1)
                done(tt(p1[:, YT1[j], PAD:PW], cacc[:, j], p1[:, 4 + j, PAD:PW], MUL), "mix_f1")
            scores(0)
            for hp in range(8):
                if hp < 7:
                    differences(hp + 1)
                    scores(hp + 1)
                dve.wait_ge(*made("sy", hp + 1))
                xs, z_ = p1[:, XS + hp, PAD:PW], p1[:, ZS + hp, PAD:PW]
                done(stt(xs, xs, V("dsk", hp), bank(f"sy{hp}", 0)[:], MUL, ADD), "sy_out")
                dve.wait_ge(S("s_z"), hp + 1)
                done(tt(z_, xs, z_, MUL), "s_y")
                if hp == 7:
                    mix_lo(0, 2)
                if hp == 6:
                    mean_square(0)
            mix_lo(2, 4)
            rms(0)
            mix_lo(4, 8)
            split(FIRST["out1"] + 1 + W_SLOTS)
            mean_square(1)
            rms(1)
            mix_lo(8, 12)
            done(dve.tensor_copy(small[:, 255:256], small[:, 254:255]), "mix_done")
            for half in range(2):
                for i in range(6):
                    (chunk if i < 5 else ahead)("out1", 6 * half + i)
                    if half and i == 2:
                        memory(1)
                if half == 0:
                    dve.wait_ge(S("h_ready"), NT * 3)
                residual("out1", half, True, 3)
            attention(1)
            mlp(1)


_OUT = (1, T, D)


def kernel(**inputs):
    import numpy as _np
    import concourse.bacc as _bacc
    from concourse import mybir as _mybir
    from concourse.bass_utils import run_bass_kernel_spmd as _run

    a = {k: _np.asarray(v) for k, v in inputs.items()}

    def by_feature(w):
        k, m = w.shape
        return w.reshape(k // P, P, m // P, P).transpose(2, 1, 0, 3).reshape(m // P, P, CHUNK)

    def by_token(w):
        k, _ = w.shape
        return w.reshape(k // 256, 2, P, 2, HALF).transpose(3, 0, 2, 1, 4).reshape(k // P, P, CHUNK)

    def padded(w, rows, cols):
        z = _np.zeros((rows, cols), w.dtype)
        z[:w.shape[0], :w.shape[1]] = w
        return z

    stream = []
    for l in range(2):
        if l == 0:
            w_in, w_out = a["ev_w_in"][0], a["ev_w_out"][0]
            stream += [by_feature(w_in)[_np.array(ORDER0)],
                       by_token(_np.concatenate([w_out[HALF:], w_out[:HALF]]))]
        else:
            w_in = a["od_w_in"][0]
            stream += [by_feature(w_in[:, 0:D]), by_feature(padded(w_in[:, 3584:], D, P)),
                       by_feature(w_in[:, 2 * D:3584]), by_feature(w_in[:, D:2 * D]), by_token(a["od_w_out"][0])]
        stream += [by_feature(a["xa_wk"][l]), by_token(a["xa_wv"][l]), by_feature(a["xa_wq"][l]),
                   by_token(a["xa_wo"][l])]
        for q in range(QUARTERS):
            cut = slice(q * D, q * D + D)
            stream += [by_feature(a["ffn_w1"][l][:, cut]), by_token(a["ffn_w2"][l][cut])]

    def tiles(v):
        v = v.reshape(-1, v.shape[-1])
        return v.reshape(v.shape[0] * v.shape[1] // P, P).T

    vecs = {"mu": a["ev_mu"], "w0": a["ev_w0"], "a0": a["ev_a0"], "kk": a["ev_k_k"], "ka": a["ev_k_a"],
            "rk": a["ev_r_k"].reshape(1, -1), "gng": a["ev_gn_g"], "gnb": a["ev_gn_b"],
            "lcw": a["ev_lru_conv_w"][0], "lcb": a["ev_lru_conv_b"], "lba": a["ev_lru_ba"], "lbx": a["ev_lru_bx"],
            "lam": a["ev_lru_lam"], "ccw": a["od_cf_conv_w"][0], "ccb": a["od_cf_conv_b"],
            "clg": a["od_cf_ln_g"], "clb": a["od_cf_ln_b"], "scw": a["od_ssm_conv_w"][0],
            "lng": _np.concatenate([a[f"ln_{w}_g"][l] for l in range(2) for w in ("mix", "mem", "ffn")])[None],
            "lnb": _np.concatenate([a[f"ln_{w}_b"][l] for l in range(2) for w in ("mix", "mem", "ffn")])[None],
            "scb": a["od_ssm_conv_b"], "sng": a["od_ssm_norm_g"], "dsk": _np.repeat(a["od_d_skip"], 64, axis=1)}
    table = [tiles(vecs[n]) for n, _ in VEC_TILES[:-2]]
    table += [padded(a["od_dt_bias"].T, P, 1), padded(a["od_a_log"].T, P, 1)]
    lora = _np.stack([_np.concatenate([a["ev_w2"][0], a["ev_a2"][0]]), a["ev_g2"][0]], axis=1)
    lru = _np.zeros((P, 8, P), _np.float32)
    for m, name in enumerate(["ev_lru_wa", "ev_lru_wx"]):
        for n in range(8):
            rows = slice(64 * (n % 2), 64 * (n % 2) + 64)
            lru[rows, 4 * m + n // 2, rows] = a[name][0, n]
    rows = [_np.stack([a[f"ln_{w}_g"][l], a[f"ln_{w}_b"][l]]) for l in range(2) for w in ("mix", "mem", "ffn")]
    x, mem = a["x"][0], a["mem"][0]
    arrays = {
        "x_tok": x.reshape(NT, P, D).transpose(1, 0, 2),
        "x_feat": x.T.reshape(KD, P, T).transpose(1, 0, 2),
        "mem_feat": mem.T.reshape(KD, P, MEM).transpose(1, 0, 2).reshape(P, KD * MEM),
        "weights": _np.concatenate(stream),
        "vectors": _np.concatenate(table, axis=1),
        "lora": lora,
        "lru_w": lru,
        "ln_rows": _np.stack(rows),
    }
    arrays = {k: _np.ascontiguousarray(v) for k, v in arrays.items()}
    nc = _bacc.Bacc("TRN2", target_bir_lowering=False, num_devices=1)
    args = [nc.dram_tensor(k, v.shape, _mybir.dt.float32, kind="ExternalInput").ap() for k, v in arrays.items()]
    out = nc.dram_tensor("out", _OUT, _mybir.dt.float32, kind="ExternalOutput").ap()
    build(nc, *args, out.rearrange("a (t p) d -> p (a t) d", p=P))
    r = _run(nc, [arrays], core_ids=[0])
    return r.results[0]["out"]
```
